# Optimizing a Trainium2 kernel written in Bass

```python
import jax, jax.numpy as jnp
from jax import lax
import numpy as np

D_MODEL = 1024
BATCH = 1
SEQ = 2048
DEPTH = 1
DEC_BATCH = 8
DEC_SEQ = 16
PAST_LEN = 1024

CHUNK = 64
MIX = D_MODEL
HEAD_DIM = 64
N_ATT_HEADS = 8
D_ATT = N_ATT_HEADS * HEAD_DIM
POOL_WINDOWS = (2, 4, 8, 16)
POOL_GROUP = 64
D_POOL = POOL_GROUP * len(POOL_WINDOWS)
POOL_STATE = max(POOL_WINDOWS) - 1
CONV_GROUP = 64
N_CONV_GROUPS = 4
D_CONV = CONV_GROUP * N_CONV_GROUPS
CONV_W = 3
Q_BLOCK = 128
EPS = 1e-6
IN_SPLITS = (D_POOL, D_POOL, D_ATT, D_ATT, D_ATT, D_ATT, N_ATT_HEADS, D_CONV, D_CONV, D_CONV, D_CONV)
IN_COLS = 2 * D_POOL + 4 * D_ATT + N_ATT_HEADS + 4 * D_CONV

kernel_name = "hybrid_pool_fox_shortconv_stream_step"

def _split_points():
    pts, acc = [], 0
    for w in IN_SPLITS[:-1]:
        acc += w
        pts.append(acc)
    return pts

def rmsnorm(x, g):
    xf = x.astype(jnp.float32)
    y = xf * lax.rsqrt(jnp.mean(xf * xf, axis=-1, keepdims=True) + EPS)
    return (y * g.astype(jnp.float32)).astype(x.dtype)

def pool_mixer(u, prev, past):
    T = u.shape[1]
    ext = jnp.concatenate([prev.astype(u.dtype), u], axis=1)
    cs = jnp.cumsum(ext.astype(jnp.float32), axis=1)
    cs = jnp.concatenate([jnp.zeros_like(cs[:, :1]), cs], axis=1)
    pos = past + jnp.arange(T)
    means = []
    for g, w in enumerate(POOL_WINDOWS):
        c0, c1 = g * POOL_GROUP, (g + 1) * POOL_GROUP
        hi = cs[:, POOL_STATE + 1:POOL_STATE + 1 + T, c0:c1]
        lo = cs[:, POOL_STATE + 1 - w:POOL_STATE + 1 - w + T, c0:c1]
        cnt = jnp.minimum(pos + 1, w).astype(jnp.float32)[None, :, None]
        means.append((hi - lo) / cnt)
    pooled = jnp.concatenate(means, axis=-1) - u.astype(jnp.float32)
    return pooled, ext[:, -POOL_STATE:]

def conv_mixer(bg, cg, xc, prev):
    T = xc.shape[1]
    z = cg * xc
    ext = jnp.concatenate([prev.astype(z.dtype), z], axis=1)
    return ext, T

def attend(q, K, V, Fq, Fk, q_pos, k_pos):
    B, T, H, Dh = q.shape
    qb = min(Q_BLOCK, T)
    nb = T // qb
    scale = Dh ** -0.5
    qs = q.reshape(B, nb, qb, H, Dh).transpose(1, 0, 2, 3, 4)
    fqs = Fq.reshape(B, nb, qb, H).transpose(1, 0, 3, 2)
    ps = q_pos.reshape(nb, qb)
    fkT = Fk.transpose(0, 2, 1)[:, :, None, :]

    def block(args):
        qblk, fblk, pblk = args
        s = jnp.einsum('bqhd,bkhd->bhqk', qblk, K, preferred_element_type=jnp.float32) * scale
        s = s + fblk[..., None] - fkT
        mask = k_pos[None, :] <= pblk[:, None]
        s = jnp.where(mask[None, None], s, -jnp.inf)
        p = jax.nn.softmax(s, axis=-1)
        return jnp.einsum('bhqk,bkhd->bqhd', p.astype(V.dtype), V)

    o = lax.map(block, (qs, fqs, ps))
    return o.transpose(1, 0, 2, 3, 4).reshape(B, T, H, Dh)

def layer(x, prev_k, prev_v, prev_logf, prev_pool, prev_conv,
          norm_g, w_in, b_f, q_norm_g, k_norm_g, pool_w, pool_scale, conv_w, w_out):
    B, T, _ = x.shape
    past = prev_k.shape[1]
    h = rmsnorm(x, norm_g)
    proj = jnp.einsum('btd,de->bte', h, w_in)
    pu, pg, q, k, v, ag, fl, cb, cc, cx, cgate = jnp.split(proj, _split_points(), axis=-1)

    pooled, new_pool = pool_mixer(pu, prev_pool, past)
    pooled = pooled.reshape(B, T, len(POOL_WINDOWS), POOL_GROUP)
    a = jnp.einsum('btgc,gcd->btgd', pooled, pool_w.astype(jnp.float32)).reshape(B, T, D_POOL)
    a = (a * pool_scale.astype(jnp.float32)).astype(h.dtype) * jax.nn.silu(pg)

    q = rmsnorm(q.reshape(B, T, N_ATT_HEADS, HEAD_DIM), q_norm_g)
    k = rmsnorm(k.reshape(B, T, N_ATT_HEADS, HEAD_DIM), k_norm_g)
    v = v.reshape(B, T, N_ATT_HEADS, HEAD_DIM)
    logf = jax.nn.log_sigmoid(fl.astype(jnp.float32) + b_f.astype(jnp.float32))
    K = jnp.concatenate([prev_k.astype(k.dtype), k], axis=1)
    V = jnp.concatenate([prev_v.astype(v.dtype), v], axis=1)
    F = jnp.cumsum(jnp.concatenate([prev_logf.astype(jnp.float32), logf], axis=1), axis=1)
    k_pos = jnp.arange(past + T)
    q_pos = past + jnp.arange(T)
    o = attend(q, K, V, F[:, past:], F, q_pos, k_pos)
    b = o.reshape(B, T, D_ATT).astype(h.dtype) * jax.nn.silu(ag)

    ext, _ = conv_mixer(cb, cc, cx, prev_conv)
    y = sum(conv_w[j][None, None, :] * ext[:, j:j + T] for j in range(CONV_W))
    c = (cb * y) * jax.nn.silu(cgate)
    new_conv = ext[:, -(CONV_W - 1):]

    mixed = jnp.concatenate([a, b, c.astype(h.dtype)], axis=-1)
    x_out = x + jnp.einsum('bte,ed->btd', mixed, w_out).astype(x.dtype)
    return x_out, k, v, logf.astype(x.dtype), new_pool, new_conv

def setup_inputs(seed: int = 0) -> dict:
    key = jax.random.key(seed)
    ks = jax.random.split(key, 20)
    f32 = jnp.float32
    x_prompt = jax.random.normal(ks[0], (BATCH, SEQ, D_MODEL), f32)
    x_sample = jax.random.normal(ks[1], (DEC_BATCH, DEC_SEQ, D_MODEL), f32)
    cache_k = jax.random.normal(ks[2], (DEPTH, DEC_BATCH, PAST_LEN, N_ATT_HEADS, HEAD_DIM), f32)
    cache_v = jax.random.normal(ks[3], (DEPTH, DEC_BATCH, PAST_LEN, N_ATT_HEADS, HEAD_DIM), f32)
    cache_logf = jax.nn.log_sigmoid(3.0 + jax.random.normal(ks[4], (DEPTH, DEC_BATCH, PAST_LEN, N_ATT_HEADS), f32))
    state_pool = jax.random.normal(ks[5], (DEPTH, DEC_BATCH, POOL_STATE, D_POOL), f32)
    state_conv = jax.random.normal(ks[6], (DEPTH, DEC_BATCH, CONV_W - 1, D_CONV), f32)
    norm_g = 1.0 + 0.1 * jax.random.normal(ks[7], (DEPTH, D_MODEL), f32)
    w_in = jax.random.normal(ks[8], (DEPTH, D_MODEL, IN_COLS), f32) * D_MODEL ** -0.5
    b_f = 3.0 + 0.1 * jax.random.normal(ks[9], (DEPTH, N_ATT_HEADS), f32)
    q_norm_g = 1.0 + 0.1 * jax.random.normal(ks[10], (DEPTH, HEAD_DIM), f32)
    k_norm_g = 1.0 + 0.1 * jax.random.normal(ks[11], (DEPTH, HEAD_DIM), f32)
    pool_w = jax.random.normal(ks[12], (DEPTH, len(POOL_WINDOWS), POOL_GROUP, POOL_GROUP), f32) * POOL_GROUP ** -0.5
    pool_scale = 1.0 + 0.1 * jax.random.normal(ks[13], (DEPTH, D_POOL), f32)
    conv_w = jax.random.normal(ks[14], (DEPTH, CONV_W, D_CONV), f32) * CONV_W ** -0.5
    w_out = jax.random.normal(ks[15], (DEPTH, MIX, D_MODEL), f32) * (0.5 * MIX ** -0.5)
    return {"x_prompt": x_prompt, "x_sample": x_sample,
            "cache_k": cache_k, "cache_v": cache_v, "cache_logf": cache_logf,
            "state_pool": state_pool, "state_conv": state_conv,
            "norm_g": norm_g, "w_in": w_in, "b_f": b_f, "q_norm_g": q_norm_g, "k_norm_g": k_norm_g,
            "pool_w": pool_w, "pool_scale": pool_scale, "conv_w": conv_w, "w_out": w_out}

def reference(x_prompt, x_sample, cache_k, cache_v, cache_logf, state_pool, state_conv,
              norm_g, w_in, b_f, q_norm_g, k_norm_g, pool_w, pool_scale, conv_w, w_out):
    Bp = x_prompt.shape[0]
    dt = x_prompt.dtype
    xp, xs = x_prompt, x_sample
    kp, vp, fp, pp, cp = [], [], [], [], []
    ksm, vsm, fsm, psm, csm = [], [], [], [], []
    for l in range(DEPTH):
        params = (norm_g[l], w_in[l], b_f[l], q_norm_g[l], k_norm_g[l],
                  pool_w[l], pool_scale[l], conv_w[l], w_out[l])
        xp, k1, v1, f1, p1, c1 = layer(
            xp,
            jnp.zeros((Bp, 0, N_ATT_HEADS, HEAD_DIM), dt),
            jnp.zeros((Bp, 0, N_ATT_HEADS, HEAD_DIM), dt),
            jnp.zeros((Bp, 0, N_ATT_HEADS), dt),
            jnp.zeros((Bp, POOL_STATE, D_POOL), dt),
            jnp.zeros((Bp, CONV_W - 1, D_CONV), dt),
            *params)
        kp.append(k1); vp.append(v1); fp.append(f1); pp.append(p1); cp.append(c1)
        xs, k2, v2, f2, p2, c2 = layer(
            xs, cache_k[l], cache_v[l], cache_logf[l], state_pool[l], state_conv[l], *params)
        ksm.append(k2); vsm.append(v2); fsm.append(f2); psm.append(p2); csm.append(c2)
    return (xp, xs,
            jnp.stack(kp), jnp.stack(vp), jnp.stack(fp), jnp.stack(pp), jnp.stack(cp),
            jnp.stack(ksm), jnp.stack(vsm), jnp.stack(fsm), jnp.stack(psm), jnp.stack(csm))


_drawn_inputs = setup_inputs


def setup_inputs(seed=0):
    import zlib

    import numpy as np

    out = dict(_drawn_inputs(seed))
    spreads = {}
    factors = {'cache_logf': 7.407, 'q_norm_g': 8.0, 'pool_scale': 4.273}
    for name, (base, spread) in spreads.items():
        noise = np.random.default_rng([zlib.crc32(name.encode()), seed]).standard_normal(out[name].shape)
        drawn = base * np.exp(spread * noise) if base else spread * noise
        out[name] = __import__('jax').numpy.asarray(drawn.astype(out[name].dtype))
    for name, factor in factors.items():
        out[name] = (out[name] * factor).astype(out[name].dtype)
    return out
```

```python
from contextlib import ExitStack

import concourse.bass as bass
from concourse import mybir

F32 = mybir.dt.float32
F32R = mybir.dt.float32r
BF16 = mybir.dt.bfloat16
ALU = mybir.AluOpType
ACT = mybir.ActivationFunctionType
AX_X = mybir.AxisListType.X

P = 128
D = 1024
KT = D // P
SEQ = 2048
PT = SEQ // P
NB, NQ, PAST = 8, 16, 1024
H, HD = 8, 64
DA = H * HD
NT = PT + 1
DP = DC = 256
POOL_WINDOWS = (2, 4, 8, 16)
HIST = 15
CONV_W = 3
EPS = 1e-6
Q0 = 2 * DP
CA = 4 * DA + H
C0 = Q0 + CA
MASKED = -1e38


def ds(start, n):
    return bass.ds(start, n)


def wait_some(eng, sem, count):
    if not isinstance(count, int) or count > 0:
        eng.wait_ge(sem, count)


def passed(eng, sem):
    eng.sem_inc(sem, 1)


class Memory:

    def __init__(self, nc, ctx, stage):
        self.nc, self.ctx, self.stage = nc, ctx, stage

    def sbuf(self, name, shape, dt=F32):
        return self.ctx.enter_context(self.nc.sbuf_tensor(f"{self.stage}_{name}", shape, dt))

    def psum(self, name, shape, dt=F32):
        return self.ctx.enter_context(self.nc.psum_tensor(f"{self.stage}_{name}", shape, dt))

    def sem(self, name):
        return self.ctx.enter_context(self.nc.semaphore(f"{self.stage}_{name}"))


def make_constants(nc, ident, tri):
    with ExitStack() as ctx:
        made = Memory(nc, ctx, "const").sem("made")
        block = ctx.enter_context(nc.Block())

        @block.gpsimd
        def _(pool):
            pool.memset(ident[:, :], 0.0).then_inc(made, 1)
            pool.memset(tri[:, :], 1.0).then_inc(made, 1)
            pool.wait_ge(made, 2)
            pool.affine_select(out=ident[:, :], in_=ident[:, :], compare_op=ALU.not_equal, fill=1.0,
                               base=0, pattern=[[-1, P]], channel_multiplier=1).then_inc(made, 1)
            pool.affine_select(out=tri[:, :], in_=tri[:, :], compare_op=ALU.is_ge, fill=0.0,
                               base=0, pattern=[[1, P]], channel_multiplier=-1).then_inc(made, 1)
            pool.wait_ge(made, 4)


def attention_projection(nc, ident, fl_raw, x_prompt, x_sample, norm_g, w_in, q_norm_g, k_norm_g,
                         new_k, new_v, new_k_s, new_v_s, q_all, gate_all, xt_hi_all, xt_lo_all):
    half = (DA + H) // 2
    chunks = [(0, DA), (DA, DA), (2 * DA, DA), (3 * DA, half), (3 * DA + half, half)]
    NCH = len(chunks)
    QC, KC, VC, G0, G1 = range(NCH)
    g_rest = DA - half
    with ExitStack() as ctx:
        m = Memory(nc, ctx, "ap")
        w_hi = m.sbuf("w_hi", [P, KT, CA], F32R)
        w_lo = m.sbuf("w_lo", [P, KT, CA], F32R)
        w_raw = m.sbuf("w_raw", [P, 2, CA])
        g_in = m.sbuf("g_in", [P, KT])
        qk_g = m.sbuf("qk_g", [P, 2, HD])
        neg_half = m.sbuf("neg_half", [P, H])
        x = m.sbuf("x", [P, 2, D])
        xt_hi = m.sbuf("xt_hi", [P, 2, D], F32R)
        xt_lo = m.sbuf("xt_lo", [P, 2, D], F32R)
        x_ss = m.sbuf("x_ss", [P, 2])
        x_rstd = m.sbuf("x_rstd", [P, 2])
        squares = m.sbuf("squares", [P, D])
        h_ss = m.sbuf("h_ss", [P, 2, H])
        h_ms = m.sbuf("h_ms", [P, 2, H])
        h_rstd = m.sbuf("h_rstd", [P, 2, H])
        out = m.sbuf("out", [P, 2, 4, DA])
        ps = m.psum("ps", [P, NCH, 512])
        ps_t = m.psum("ps_t", [P, 2, 512])

        w_in_sem = [m.sem(f"w_loaded{i}") for i in range(2)]
        small_in = m.sem("gains_loaded")
        w_hi_done = m.sem("w_hi_done")
        w_lo_done = m.sem("w_lo_done")
        gains = m.sem("gains_scaled")
        x_in = [m.sem(f"x_loaded{i}") for i in range(2)]
        x_sq = m.sem("x_squared")
        x_rs = m.sem("x_rstd_done")
        x_norm = m.sem("x_normed")
        xt_ps = m.sem("x_transposed")
        xt_h = m.sem("xt_hi_done")
        xt_l = m.sem("xt_lo_done")
        proj = m.sem("chunk_projected")
        qk_sq = m.sem("qk_squared")
        qk_ss = m.sem("qk_summed")
        qk_rs = m.sem("qk_rstd_done")
        qk_n = m.sem("qk_scaled")
        qk_out = m.sem("qk_out_done")
        vg_out = m.sem("v_gate_out_done")
        fl_out = m.sem("logits_out")
        stored = [m.sem(f"stored{i}") for i in range(2)]
        xt_stored = [m.sem(f"xt_stored{i}") for i in range(2)]
        pool_on = m.sem("pool_passed_waits")
        block = ctx.enter_context(nc.Block())

        w_v = w_in.rearrange("(k p) c -> p k c", p=P)

        def steps(eng, step, prep):
            prep(0, 0, 0)
            with eng.Fori(0, PT // 2) as i:
                step(i * 2, i, 0, lambda: prep(i * 2 + 1, i, 1))
                step(i * 2 + 1, i, 1, lambda: prep(i * 2 + 2, i + 1, 0))
            step(PT, PT // 2, 0, lambda: None)

        @block.sync
        def _(sp):
            for k in range(KT):
                if k >= 2:
                    sp.wait_ge(w_hi_done, k - 1)
                    sp.wait_ge(w_lo_done, k - 1)
                sp.dma_start(w_raw[:, k % 2, :], w_v[:, k, Q0:Q0 + CA]).then_inc(w_in_sem[k % 2], 16)

            def store(t, i, par, rows):
                k_rows, v_rows = rows
                sp.wait_ge(qk_out, 2 * t + 1)
                sp.dma_start(q_all[ds(t * P, P), :], out[:, par, 0, :]).then_inc(stored[par], 16)
                sp.wait_ge(qk_out, 2 * t + 2)
                sp.dma_start(k_rows, out[:, par, 1, :]).then_inc(stored[par], 16)
                sp.wait_ge(vg_out, 3 * t + 1)
                sp.dma_start(v_rows, out[:, par, 2, :]).then_inc(stored[par], 16)
                sp.wait_ge(vg_out, 3 * t + 3)
                sp.dma_start(gate_all[ds(t * P, P), :], out[:, par, 3, :]).then_inc(stored[par], 16)

            def store_xt(t, par):
                sp.wait_ge(xt_l, 2 * t + 2)
                sp.dma_start(xt_hi_all[ds(t * P, P), :],
                             xt_hi[:, par, :].bitcast(F32)).then_inc(xt_stored[par], 16)
                sp.dma_start(xt_lo_all[ds(t * P, P), :],
                             xt_lo[:, par, :].bitcast(F32)).then_inc(xt_stored[par], 16)

            sp.dma_start(x[:, 0, :], x_prompt[0:P, :]).then_inc(x_in[0], 16)
            sp.dma_start(x[:, 1, :], x_prompt[P:2 * P, :]).then_inc(x_in[1], 16)
            with sp.Fori(0, PT // 2 - 1) as i:
                for par in range(2):
                    t = i * 2 + par
                    store_xt(t, par)
                    sp.wait_ge(xt_ps, 2 * t + 2)
                    sp.dma_start(x[:, par, :], x_prompt[ds((t + 2) * P, P), :]).then_inc(x_in[par], 16)
                    store(t, i, par, (new_k[ds(t * P, P), :], new_v[ds(t * P, P), :]))
            for t in range(PT - 2, NT):
                store_xt(t, t % 2)
                if t == PT - 2:
                    sp.wait_ge(xt_ps, 2 * t + 2)
                    sp.dma_start(x[:, 0, :], x_sample).then_inc(x_in[0], 16)
                rows = ((new_k[t * P:(t + 1) * P, :], new_v[t * P:(t + 1) * P, :]) if t < PT
                        else (new_k_s, new_v_s))
                store(t, t // 2, t % 2, rows)
            for par in range(2):
                tiles = PT // 2 + (1 - par)
                sp.wait_ge(stored[par], 64 * tiles)
                sp.wait_ge(xt_stored[par], 32 * tiles)

        @block.gpsimd
        def _(pool):
            pool.dma_start(g_in[:, :], norm_g.rearrange("(k p) -> p k", p=P),
                           allow_slow_non_contiguous=True).then_inc(small_in, 16)
            pool.dma_start(qk_g[:, 0, :], q_norm_g.partition_broadcast(P)).then_inc(small_in, 16)
            pool.dma_start(qk_g[:, 1, :], k_norm_g.partition_broadcast(P)).then_inc(small_in, 16)
            pool.memset(neg_half[:, :], -0.5).then_inc(gains, 1)
            pool.wait_ge(small_in, 48)
            pool.tensor_scalar(qk_g[:, 0, :], qk_g[:, 0, :], HD ** -0.5, 0.0, ALU.mult, ALU.add).then_inc(gains, 1)
            pool.wait_ge(gains, 2)

            def prep(t, i, par):
                pool.wait_ge(x_sq, t + 1)
                passed(pool, pool_on)
                pool.tensor_scalar(x_rstd[:, par:par + 1], x_ss[:, par:par + 1], 1.0 / D, EPS,
                                   ALU.mult, ALU.add).then_inc(x_rs, 1)
                pool.wait_ge(x_rs, 2 * t + 1)
                pool.tensor_tensor(x_rstd[:, par:par + 1], x_rstd[:, par:par + 1], neg_half[:, 0:1],
                                   ALU.pow).then_inc(x_rs, 1)

            def step(t, i, par, ahead):
                ahead()
                for c in (QC, KC):
                    pool.wait_ge(qk_ss, 2 * t + c + 1)
                    passed(pool, pool_on)
                    pool.tensor_scalar(h_ms[:, c, :], h_ss[:, c, :], 1.0 / HD, EPS,
                                       ALU.mult, ALU.add).then_inc(qk_rs, 1)
                    pool.wait_ge(qk_rs, 4 * t + 2 * c + 1)
                    pool.tensor_tensor(h_rstd[:, c, :], h_ms[:, c, :], neg_half[:, :], ALU.pow).then_inc(qk_rs, 1)
                for c in (QC, KC):
                    pool.wait_ge(qk_n, 2 * t + c + 1)
                    rows = out[:, par, c, :].rearrange("p (h d) -> p h d", h=H)
                    gain = qk_g[:, c, :].rearrange("p (o d) -> p o d", o=1).to_broadcast([P, H, HD])
                    pool.tensor_tensor(rows, rows, gain, ALU.mult).then_inc(qk_out, 1)

            steps(pool, step, prep)

        @block.scalar
        def _(act):
            act.wait_ge(small_in, 48)
            for k in range(KT):
                act.wait_ge(w_in_sem[k % 2], 16 * (k // 2 + 1))
                act.activation(w_hi[:, k, :], w_raw[:, k % 2, :], ACT.Copy,
                               scale=g_in[:, k:k + 1]).then_inc(w_hi_done, 1)

            def prep(t, i, par):
                act.wait_ge(x_in[par], 16 * i + 16)
                act.activation(squares[:, :], x[:, par, :], ACT.Square,
                               accum_out=x_ss[:, par:par + 1]).then_inc(x_sq, 1)
                wait_some(act, proj, NCH * (t - 1))
                act.wait_ge(xt_stored[par], 32 * i)
                for b in range(2):
                    act.wait_ge(xt_ps, 2 * t + b + 1)
                    act.activation(xt_hi[:, par, b * 512:(b + 1) * 512], ps_t[:, b, :],
                                   ACT.Copy).then_inc(xt_h, 1)

            def step(t, i, par, ahead):
                ahead()
                act.wait_ge(stored[par], 64 * i)
                for c in (QC, KC):
                    act.wait_ge(proj, NCH * t + c + 1)
                    if c == KC:
                        act.wait_ge(qk_ss, 2 * t + 1)
                    act.activation(squares[:, 0:DA], ps[:, c, :], ACT.Square).then_inc(qk_sq, 1)
                act.wait_ge(proj, NCH * t + VC + 1)
                act.activation(out[:, par, 2, :], ps[:, VC, :], ACT.Copy).then_inc(vg_out, 1)
                act.wait_ge(proj, NCH * t + G0 + 1)
                act.activation(out[:, par, 3, 0:half], ps[:, G0, 0:half], ACT.Silu).then_inc(vg_out, 1)
                act.wait_ge(proj, NCH * t + G1 + 1)
                act.activation(out[:, par, 3, half:DA], ps[:, G1, 0:g_rest], ACT.Silu).then_inc(vg_out, 1)
                act.wait_ge(qk_ss, 2 * t + 2)

            steps(act, step, prep)

        @block.vector
        def _(dve):
            dve.wait_ge(small_in, 48)
            for k in range(KT):
                dve.wait_ge(w_hi_done, k + 1)
                dve.scalar_tensor_tensor(w_lo[:, k, :], w_raw[:, k % 2, :], g_in[:, k:k + 1],
                                         w_hi[:, k, :].bitcast(F32), ALU.mult,
                                         ALU.subtract).then_inc(w_lo_done, 1)

            def prep(t, i, par):
                dve.wait_ge(x_rs, 2 * t + 2)
                dve.tensor_scalar(x[:, par, :], x[:, par, :], x_rstd[:, par:par + 1], None,
                                  ALU.mult).then_inc(x_norm, 1)
                for b in range(2):
                    dve.wait_ge(xt_h, 2 * t + b + 1)
                    part = slice(b * 512, (b + 1) * 512)
                    dve.tensor_tensor(xt_lo[:, par, part], ps_t[:, b, :], xt_hi[:, par, part].bitcast(F32),
                                      ALU.subtract).then_inc(xt_l, 1)

            def step(t, i, par, ahead):
                ahead()
                dve.wait_ge(stored[par], 64 * i)
                for c in (QC, KC):
                    dve.wait_ge(qk_sq, 2 * t + c + 1)
                    dve.wait_ge(qk_rs, 4 * t)
                    dve.tensor_reduce(h_ss[:, c, :], squares[:, 0:DA].rearrange("p (h d) -> p h d", h=H),
                                      AX_X, ALU.add).then_inc(qk_ss, 1)
                for c in (QC, KC):
                    dve.wait_ge(qk_rs, 4 * t + 2 * c + 2)
                    rstd = h_rstd[:, c, :].rearrange("p (h o) -> p h o", o=1).to_broadcast([P, H, HD])
                    dve.tensor_tensor(out[:, par, c, :].rearrange("p (h d) -> p h d", h=H),
                                      ps[:, c, :].rearrange("p (h d) -> p h d", h=H), rstd,
                                      ALU.mult).then_inc(qk_n, 1)
                dve.wait_ge(vg_out, 3 * t + 3)
                dve.tensor_copy(fl_raw[:, ds(t * H, H)], ps[:, G1, g_rest:half]).then_inc(fl_out, 1)

            steps(dve, step, prep)

        @block.tensor
        def _(pe):
            def prep(t, i, par):
                pe.wait_ge(x_norm, t + 1)
                for b in range(2):
                    pe.wait_ge(xt_l, 2 * t)
                    for n in range(4):
                        k = 4 * b + n
                        mm = pe.transpose(ps_t[:, b, n * P:(n + 1) * P], x[:, par, k * P:(k + 1) * P], ident[:, :])
                    mm.then_inc(xt_ps, 1)

            def step(t, i, par, ahead):
                for c, (c0, n) in enumerate(chunks):
                    if c == QC:
                        pe.wait_ge(xt_l, 2 * t + 2)
                        pe.wait_ge(w_lo_done, KT)
                    if c in (QC, KC):
                        pe.wait_ge(qk_n, 2 * t)
                    elif c == G1:
                        pe.wait_ge(fl_out, t)
                    else:
                        pe.wait_ge(vg_out, 3 * t)
                    for k in range(KT):
                        kk = slice(k * P, (k + 1) * P)
                        for j, (xa, wa) in enumerate(((xt_hi, w_hi), (xt_hi, w_lo), (xt_lo, w_hi))):
                            mm = pe.matmul(ps[:, c, 0:n], xa[:, par, kk], wa[:, k, c0:c0 + n],
                                           start=(k == 0 and j == 0), stop=(k == KT - 1 and j == 2))
                    mm.then_inc(proj, 1)
                    if c == QC:
                        ahead()

            steps(pe, step, prep)


def forget_sums(nc, ident, tri, fl_raw, f_t_all, b_f, cache_logf, new_logf, new_logf_s, f_all):
    TS = PAST // P
    with ExitStack() as ctx:
        m = Memory(nc, ctx, "fs")
        bias = m.sbuf("bias", [P, H])
        z = m.sbuf("z", [P, NT, H])
        mag = m.sbuf("mag", [P, NT, H])
        logf = m.sbuf("logf", [P, NT, H])
        streams = m.sbuf("streams", [P, TS + 1, NB * H])
        ones = m.sbuf("ones", [P, P])
        carry = m.sbuf("carry", [P, PT, H])
        total = m.sbuf("total", [P, PT, H])
        carry_s = m.sbuf("carry_s", [P, TS + 1, NB * H])
        total_s = m.sbuf("total_s", [P, TS, NB * H])
        f_p = m.sbuf("f_p", [P, PT * H])
        f_pt = m.sbuf("f_pt", [P, P])
        f_s = m.sbuf("f_s", [P, TS + 1, NB * H])
        split = m.sbuf("split", [P, TS + 1, 2, NB * H], F32R)
        f_t = m.sbuf("f_t", [P, (TS + 1) * P])
        ps_p = m.psum("ps_p", [P, 2, P])
        ps_l = m.psum("ps_l", [P, 2, 512])
        ps_n = m.psum("ps_n", [P, 512])
        ps_f = m.psum("ps_f", [P, P])
        ps_t = m.psum("ps_t", [P, 3, 512])

        loaded = m.sem("bias_loaded")
        cached = m.sem("cache_loaded")
        zeroed = m.sem("new_tile_zeroed")
        ones_made = m.sem("ones_made")
        z_done = m.sem("z_done")
        soft = m.sem("softplus_done")
        logf_done = m.sem("logf_done")
        logf_stored = m.sem("logf_stored")
        new_in = m.sem("new_logf_loaded")
        sums_p = m.sem("prompt_summed")
        sums_s = m.sem("streams_summed")
        chain = m.sem("vector_chain")
        f_ready = m.sem("f_prompt_ready")
        f_turned = m.sem("f_prompt_transposed")
        f_copied = m.sem("f_prompt_copied")
        f_stored = m.sem("f_prompt_stored")
        split_ready = m.sem("streams_split")
        s_turned = m.sem("streams_transposed")
        t_copied = m.sem("streams_copied")
        block = ctx.enter_context(nc.Block())

        @block.sync
        def _(sp):
            sp.dma_start(bias[:, :], b_f.partition_broadcast(P)).then_inc(loaded, 16)
            for b in range(NB):
                sp.dma_start(streams[:, 0:TS, b * H:(b + 1) * H],
                             cache_logf[b].rearrange("(t p) h -> p t h", p=P)).then_inc(cached, 16)
            sp.wait_ge(logf_done, 1)
            sp.dma_start(new_logf.rearrange("(t p) h -> p t h", p=P), logf[:, 0:PT, :]).then_inc(logf_stored, 16)
            sp.dma_start(new_logf_s, logf[:, PT, :]).then_inc(logf_stored, 16)
            sp.wait_ge(logf_stored, 32)
            sp.wait_ge(zeroed, 1)
            sp.dma_start(streams[0:NQ, TS, :].rearrange("p (b h) -> p b h", b=NB),
                         new_logf_s.rearrange("(b t) h -> t b h", b=NB)).then_inc(new_in, 16)
            sp.wait_ge(f_copied, 1)
            sp.dma_start(f_all, f_pt[:, :]).then_inc(f_stored, 16)
            sp.wait_ge(t_copied, 2)
            sp.dma_start(f_t_all, f_t[:, :]).then_inc(f_stored, 16)
            sp.wait_ge(f_stored, 32)

        @block.gpsimd
        def _(pool):
            pool.memset(streams[:, TS, :], 0.0).then_inc(zeroed, 1)
            pool.memset(ones[:, :], 1.0).then_inc(ones_made, 1)

        @block.scalar
        def _(act):
            act.wait_ge(z_done, 2)
            act.activation(mag[:, :, :], mag[:, :, :], ACT.Exp, scale=-1.0).then_inc(soft, 1)
            act.wait_ge(soft, 1)
            act.activation(mag[:, :, :], mag[:, :, :], ACT.Ln, bias=1.0).then_inc(soft, 1)

        @block.vector
        def _(dve):
            dve.wait_ge(loaded, 16)
            dve.tensor_tensor(z[:, :, :], fl_raw[:, :].rearrange("p (t h) -> p t h", h=H),
                              bias[:, :].rearrange("p (o h) -> p o h", o=1).to_broadcast([P, NT, H]),
                              ALU.add).then_inc(z_done, 1)
            dve.wait_ge(z_done, 1)
            dve.scalar_tensor_tensor(mag[:, :, :], z[:, :, :], -1.0, z[:, :, :], ALU.mult,
                                     ALU.max).then_inc(z_done, 1)
            dve.wait_ge(soft, 2)
            dve.scalar_tensor_tensor(logf[:, :, :], z[:, :, :], 0.0, mag[:, :, :], ALU.min,
                                     ALU.subtract).then_inc(logf_done, 1)
            dve.wait_ge(sums_p, 1)
            dve.memset(carry[:, 0, :], 0.0).then_inc(chain, 1)
            dve.memset(carry_s[:, 0, :], 0.0).then_inc(chain, 1)
            dve.tensor_copy(total[:, :, :], ps_p[:, 1, :].rearrange("p (t h) -> p t h", h=H)).then_inc(chain, 1)
            dve.wait_ge(sums_s, 1)
            dve.tensor_copy(total_s[:, :, :], ps_n[:, :].rearrange("p (t c) -> p t c", t=TS)).then_inc(chain, 1)
            done = 4
            for t in range(1, PT):
                dve.wait_ge(chain, done)
                dve.tensor_tensor(carry[:, t, :], carry[:, t - 1, :], total[:, t - 1, :], ALU.add).then_inc(chain, 1)
                done += 1
                if t <= TS:
                    dve.tensor_tensor(carry_s[:, t, :], carry_s[:, t - 1, :], total_s[:, t - 1, :],
                                      ALU.add).then_inc(chain, 1)
                    done += 1
            dve.wait_ge(chain, done)
            dve.tensor_tensor(f_p[:, :], ps_p[:, 0, :], carry[:, :, :].rearrange("p t h -> p (t h)"),
                              ALU.add).then_inc(f_ready, 1)
            dve.tensor_tensor(f_s[:, 0:TS, :], ps_l[:, 0, :].rearrange("p (t c) -> p t c", t=TS),
                              carry_s[:, 0:TS, :], ALU.add).then_inc(chain, 1)
            dve.tensor_tensor(f_s[:, TS, :], ps_l[:, 1, 0:NB * H], carry_s[:, TS, :], ALU.add).then_inc(chain, 1)
            dve.wait_ge(chain, done + 2)
            dve.tensor_copy(split[:, :, 0, :], f_s[:, :, :]).then_inc(chain, 1)
            dve.wait_ge(chain, done + 3)
            dve.tensor_tensor(split[:, :, 1, :], f_s[:, :, :], split[:, :, 0, :].bitcast(F32),
                              ALU.subtract).then_inc(split_ready, 1)
            dve.wait_ge(f_turned, 1)
            dve.tensor_copy(f_pt[:, :], ps_f[:, :]).then_inc(f_copied, 1)
            dve.wait_ge(s_turned, 1)
            dve.tensor_copy(f_t[:, 0:8 * P], ps_t[:, 0:2, :].rearrange("p b n -> p (b n)")).then_inc(t_copied, 1)
            dve.tensor_copy(f_t[:, 8 * P:9 * P], ps_t[:, 2, 0:P]).then_inc(t_copied, 1)

        @block.tensor
        def _(pe):
            pe.wait_ge(logf_done, 1)
            pe.wait_ge(ones_made, 1)
            rows = logf[:, 0:PT, :].rearrange("p t h -> p (t h)")
            pe.matmul(ps_p[:, 0, :], tri[:, :], rows, start=True, stop=True)
            pe.matmul(ps_p[:, 1, :], ones[:, :], rows, start=True, stop=True).then_inc(sums_p, 1)
            pe.wait_ge(cached, 16 * NB)
            pe.wait_ge(new_in, 16)
            rows = streams[:, 0:TS, :].rearrange("p t c -> p (t c)")
            pe.matmul(ps_l[:, 0, :], tri[:, :], rows, start=True, stop=True)
            pe.matmul(ps_l[:, 1, 0:NB * H], tri[:, :], streams[:, TS, :], start=True, stop=True)
            pe.matmul(ps_n[:, :], ones[:, :], rows, start=True, stop=True).then_inc(sums_s, 1)
            pe.wait_ge(f_ready, 1)
            pe.transpose(ps_f[:, :], f_p[:, :], ident[:, :]).then_inc(f_turned, 1)
            pe.wait_ge(split_ready, 1)
            for t in range(TS + 1):
                mm = pe.transpose(ps_t[:, t // 4, (t % 4) * P:(t % 4 + 1) * P],
                                  split[:, t, :, :].rearrange("p s c -> p (s c)").bitcast(F32), ident[:, :])
            mm.then_inc(s_turned, 1)


def pool_conv(nc, ident, w_in, norm_g, xt_hi_all, xt_lo_all, pool_w, pool_scale, conv_w, state_pool, state_conv,
              new_pool, new_conv, new_pool_s, new_conv_s, mix_all):
    T = 3 * P
    NCK = PT // 3
    LAST = 2 * P
    PU, PG, CB, CC, CX, CG = 0, 256, 512, 768, 1024, 1280
    CW = 1536
    groups = [(PU, 0, "act"), (PG, 0, "act"), (PU, 1, "act"), (PG, 1, "act"),
              (CC, 0, "act"), (CX, 0, "dve"), (CB, 0, "dve"), (CG, 0, "act"),
              (CC, 1, "act"), (CX, 1, "dve"), (CB, 1, "dve"), (CG, 1, "act")]
    NG = len(groups)
    NBANK = 6
    N_ACT = sum(g[2] == "act" for g in groups)
    N_DVE = NG - N_ACT

    def read(g, who):
        return sum(x[2] == who for x in groups[:g + 1])

    def at(kind, j):
        return [n for n, g in enumerate(groups) if g[:2] == (kind, j)][0]

    with ExitStack() as ctx:
        m = Memory(nc, ctx, "pc")
        w_hi = m.sbuf("w_hi", [P, KT, CW], F32R)
        w_lo = m.sbuf("w_lo", [P, KT, CW], F32R)
        w_raw = m.sbuf("w_raw", [P, 2, CW])
        g_in = m.sbuf("g_in", [P, KT])
        xt_hi = m.sbuf("xt_hi", [P, 2, 3, D], F32R)
        xt_lo = m.sbuf("xt_lo", [P, 2, 3, D], F32R)
        pw = m.sbuf("pw", [P, 2, P])
        scale = m.sbuf("scale", [P, 2])
        cw = m.sbuf("cw", [P, CONV_W, 2])
        inv_w = m.sbuf("inv_w", [P, 2])
        first = m.sbuf("first", [P, 2, 16])
        u = m.sbuf("u", [P, 2, HIST + T])
        s_a = m.sbuf("s_a", [P, HIST + T])
        s_b = m.sbuf("s_b", [P, HIST + T])
        pooled = m.sbuf("pooled", [P, 2, T])
        z = m.sbuf("z", [P, 2, CONV_W - 1 + T])
        c_in = m.sbuf("c_in", [P, 2, T])
        y = m.sbuf("y", [P, T])
        gate = m.sbuf("gate", [P, 2, 2, T])
        mix = m.sbuf("mix", [P, 2, 2, T])
        past_u = m.sbuf("past_u", [NB * HIST, DP])
        past_z = m.sbuf("past_z", [NB * 2, DC])
        us = m.sbuf("us", [P, 2, NB, HIST + NQ])
        zs = m.sbuf("zs", [P, 2, NB, 2 + NQ])
        ends_u = m.sbuf("ends_u", [P, 2, NB * HIST])
        ends_z = m.sbuf("ends_z", [P, 2, NB * 2])
        rows_u = m.sbuf("rows_u", [P, DP])
        rows_us = m.sbuf("rows_us", [P, DP])
        rows_z = m.sbuf("rows_z", [P, DC])
        rows_zs = m.sbuf("rows_zs", [P, DC])
        ps = m.psum("ps", [P, NBANK, 512])
        ps_a = m.psum("ps_a", [P, 2, 512])

        small = m.sem("small_loaded")
        pw_zero = m.sem("pool_w_zeroed")
        pw_in = m.sem("pool_w_loaded")
        w_loaded = [m.sem(f"w_loaded{i}") for i in range(2)]
        w_hi_done = m.sem("w_hi_done")
        w_lo_done = m.sem("w_lo_done")
        tables = m.sem("tables")
        x_in = [m.sem(f"xt_loaded{i}") for i in range(2)]
        proj = m.sem("group_projected")
        act_read = m.sem("act_read")
        dve_read = m.sem("dve_read")
        steps_v = m.sem("vector_steps")
        pool_ready = m.sem("pooled_ready")
        pool_mm = m.sem("pooled_multiplied")
        mixed = m.sem("half_mixed")
        chunk_end = m.sem("chunk_ended")
        mix_stored = m.sem("mix_stored")
        past_t = m.sem("history_transposed")
        ends = m.sem("ends_gathered")
        ends_t = m.sem("ends_transposed")
        ends_c = m.sem("ends_copied")
        states_out = m.sem("states_stored")
        block = ctx.enter_context(nc.Block())

        w_v = w_in.rearrange("(k p) c -> p k c", p=P)
        STEPS = 20

        def chunks(eng, chunk):
            chunk(0, 0, T)
            with eng.Fori(0, (NCK - 1) // 2) as i:
                chunk(i * 2 + 1, 1, T)
                chunk(i * 2 + 2, 0, T)
            chunk(NCK, 1, LAST)

        @block.sync
        def _(sp):
            sp.dma_start(g_in[:, :], norm_g.rearrange("(k p) -> p k", p=P),
                         allow_slow_non_contiguous=True).then_inc(small, 16)
            sp.dma_start(scale[:, :], pool_scale.rearrange("(j p) -> p j", p=P),
                         allow_slow_non_contiguous=True).then_inc(small, 16)
            for w in range(CONV_W):
                sp.dma_start(cw[:, w, :], conv_w[w].rearrange("(j p) -> p j", p=P),
                             allow_slow_non_contiguous=True).then_inc(small, 16)
            sp.dma_start(past_u[:, :], state_pool).then_inc(small, 16)
            sp.dma_start(past_z[:, :], state_conv).then_inc(small, 16)
            sp.wait_ge(pw_zero, 1)
            for g in range(4):
                at_p = slice(64 * (g % 2), 64 * (g % 2) + 64)
                sp.dma_start(pw[at_p, g // 2, at_p], pool_w[g]).then_inc(pw_in, 16)
            for k in range(KT):
                if k >= 2:
                    sp.wait_ge(w_lo_done, k - 1)
                sp.dma_start(w_raw[:, k % 2, 0:CB], w_v[:, k, 0:Q0]).then_inc(w_loaded[k % 2], 16)
                sp.dma_start(w_raw[:, k % 2, CB:CW], w_v[:, k, C0:C0 + CW - CB]).then_inc(w_loaded[k % 2], 16)

            def load_x(c, par, tiles):
                for part, src in ((xt_hi, xt_hi_all), (xt_lo, xt_lo_all)):
                    sp.dma_start(part[:, par, 0:tiles, :].bitcast(F32),
                                 src[ds(c * T, tiles * P), :].rearrange("(n p) d -> p n d", p=P)).then_inc(x_in[par], 16)


            def chunk(c, par, n, ahead):
                if ahead:
                    wait_some(sp, proj, NG * c)
                    load_x(c + 1, 1 - par, ahead)
                for half in range(2):
                    for j in range(2):
                        sp.wait_ge(mixed, 4 * c + 2 * half + j + 1)
                        sp.dma_start(mix_all[2 * half + j][:, ds(c * T, n)],
                                     mix[:, half, j, 0:n]).then_inc(mix_stored, 16)

            load_x(0, 0, 3)
            for c in range(NCK + 1):
                chunk(c, c % 2, T if c < NCK else LAST, 3 if c < NCK - 1 else 2 if c < NCK else 0)
            sp.wait_ge(mix_stored, 16 * 4 * (NCK + 1))
            sp.wait_ge(ends_c, 4)
            sp.dma_start(new_pool, rows_u[0:HIST, :]).then_inc(states_out, 16)
            sp.dma_start(new_conv, rows_z[0:2, :]).then_inc(states_out, 16)
            sp.dma_start(new_pool_s, rows_us[0:NB * HIST, :]).then_inc(states_out, 16)
            sp.dma_start(new_conv_s, rows_zs[0:NB * 2, :]).then_inc(states_out, 16)
            sp.wait_ge(states_out, 64)

        @block.gpsimd
        def _(pool):
            pool.memset(pw[:, :, :], 0.0).then_inc(pw_zero, 1)
            for t in range(16):
                pool.memset(first[:, :, t:t + 1], 1.0 / (t + 1)).then_inc(tables, 1)
            pool.memset(u[:, :, 0:HIST], 0.0).then_inc(tables, 1)
            pool.memset(z[:, :, 0:2], 0.0).then_inc(tables, 1)

        def columns(last):
            return [(False, 0, P), (True, P, NQ)] if last else [(False, 0, T)]

        def cut(buf, streams, start, lo, hi):
            if not streams:
                return buf[:, start + lo:start + hi]
            return buf[:, start:start + NB * NQ].rearrange("p (b t) -> p b t", b=NB)[:, :, lo:hi]

        @block.scalar
        def _(act):
            act.wait_ge(small, 16 * (4 + CONV_W))
            for k in range(KT):
                act.wait_ge(w_loaded[k % 2], 32 * (k // 2 + 1))
                act.activation(w_hi[:, k, :], w_raw[:, k % 2, :], ACT.Copy,
                               scale=g_in[:, k:k + 1]).then_inc(w_hi_done, 1)

            def chunk(c, par, n):
                act.wait_ge(chunk_end, c + 1)
                for g, (kind, j, who) in enumerate(groups):
                    if who != "act":
                        continue
                    act.wait_ge(proj, NG * c + g + 1)
                    bank = ps[:, g % NBANK, :]
                    parts = columns(n == LAST)
                    for streams, col, t in parts:
                        src = cut(bank, streams, col, 0, t)
                        if kind == PU:
                            dst = us[:, j, :, HIST:HIST + NQ] if streams else u[:, j, HIST:HIST + t]
                        elif kind == CC:
                            dst = cut(c_in[:, j, :], streams, col, 0, t)
                        else:
                            dst = cut(gate[:, 0 if kind == PG else 1, j, :], streams, col, 0, t)
                        done = act.activation(dst, src, ACT.Copy if kind in (PU, CC) else ACT.Silu)
                    done.then_inc(act_read, 1)

            chunks(act, chunk)

        @block.vector
        def _(dve):
            for j in range(2):
                for h in range(2):
                    dve.memset(inv_w[64 * h:64 * h + 64, j:j + 1], 1.0 / POOL_WINDOWS[2 * j + h]).then_inc(tables, 1)
            dve.wait_ge(tables, 4 + 16 + 2)
            dve.wait_ge(small, 16 * (4 + CONV_W))
            for j in range(2):
                dve.tensor_scalar(first[:, j, :], first[:, j, :], inv_w[:, j:j + 1], None, ALU.max).then_inc(steps_v, 1)
            for k in range(KT):
                dve.wait_ge(w_hi_done, k + 1)
                dve.scalar_tensor_tensor(w_lo[:, k, :], w_raw[:, k % 2, :], g_in[:, k:k + 1],
                                         w_hi[:, k, :].bitcast(F32), ALU.mult,
                                         ALU.subtract).then_inc(w_lo_done, 1)
            dve.wait_ge(steps_v, 2)
            for j in range(2):
                for h in range(2):
                    half = slice(64 * h, 64 * h + 64)
                    dve.tensor_scalar(first[half, j, :], first[half, j, :], float(POOL_WINDOWS[2 * j + h]), None,
                                      ALU.mult).then_inc(steps_v, 1)
            dve.wait_ge(past_t, 1)
            for j in range(2):
                dve.tensor_copy(us[:, j, :, 0:HIST],
                                ps[:, 0, j * 120:(j + 1) * 120].rearrange("p (b t) -> p b t", b=NB)).then_inc(steps_v, 1)
                dve.tensor_copy(zs[:, j, :, 0:2],
                                ps[:, 0, 240 + 16 * j:256 + 16 * j].rearrange("p (b t) -> p b t", b=NB)).then_inc(steps_v, 1)
            dve.wait_ge(steps_v, 10)
            dve.tensor_copy(y[:, 0:1], scale[:, 0:1]).then_inc(chunk_end, 1)

            def chunk(c, par, n):
                parts = columns(n == LAST)
                count = [0]
                base = 10 + c * STEPS

                def link(ins):
                    count[0] += 1
                    ins.then_inc(steps_v, 1)
                    dve.wait_ge(steps_v, base + count[0])

                for j in range(2):
                    dve.wait_ge(act_read, N_ACT * c + read(at(PU, j), "act"))
                    wait_some(dve, pool_mm, 2 * c)
                    for streams, col, t in parts:
                        e = HIST + t
                        if streams:
                            uu = us[:, j, :, :]
                            a = s_a[:, 0:NB * e].rearrange("p (b e) -> p b e", b=NB)
                            b = s_b[:, 0:NB * e].rearrange("p (b e) -> p b e", b=NB)

                            def w(buf, lo, hi, part=slice(0, P)):
                                return buf[part, :, lo:hi]
                        else:
                            uu, a, b = u[:, j, :], s_a, s_b

                            def w(buf, lo, hi, part=slice(0, P)):
                                return buf[part, lo:hi]
                        link(dve.tensor_tensor(w(a, 1, e), w(uu, 1, e), w(uu, 0, e - 1), ALU.add))
                        link(dve.tensor_tensor(w(b, 3, e), w(a, 3, e), w(a, 1, e - 2), ALU.add))
                        if j == 1:
                            link(dve.tensor_tensor(w(a, 7, e), w(b, 7, e), w(b, 3, e - 4), ALU.add))
                            link(dve.tensor_tensor(w(b, 15, e), w(a, 15, e), w(a, 7, e - 8), ALU.add))
                        for h, sums in ((0, a), (1, b)):
                            half = slice(64 * h, 64 * h + 64)
                            if not streams:
                                link(dve.tensor_tensor(w(sums, HIST, HIST + 16, half), w(sums, HIST, HIST + 16, half),
                                                       first[half, j, :], ALU.mult))
                            dst = pooled[half, j, col:col + (NB * NQ if streams else t)]
                            if streams:
                                dst = dst.rearrange("p (b t) -> p b t", b=NB)
                            link(dve.scalar_tensor_tensor(dst, w(sums, HIST, e, half), inv_w[half, j:j + 1],
                                                          w(uu, HIST, e, half), ALU.mult, ALU.subtract))
                    dve.memset(first[:, j, :], 1.0).then_inc(pool_ready, 1)
                wait_some(dve, mix_stored, 64 * c)
                for j in range(2):
                    dve.wait_ge(pool_mm, 2 * c + j + 1)
                    dve.wait_ge(act_read, N_ACT * c + read(at(PG, j), "act"))
                    dve.scalar_tensor_tensor(mix[:, 0, j, 0:n], ps_a[:, j, 0:n], scale[:, j:j + 1],
                                             gate[:, 0, j, 0:n], ALU.mult, ALU.mult).then_inc(mixed, 1)
                for j in range(2):
                    dve.wait_ge(act_read, N_ACT * c + read(at(CC, j), "act"))
                    dve.wait_ge(proj, NG * c + at(CX, j) + 1)
                    bank = ps[:, at(CX, j) % NBANK, :]
                    for streams, col, t in parts:
                        dst = zs[:, j, :, 2:2 + t] if streams else z[:, j, 2:2 + t]
                        done = dve.tensor_tensor(dst, cut(bank, streams, col, 0, t),
                                                 cut(c_in[:, j, :], streams, col, 0, t), ALU.mult)
                    done.then_inc(dve_read, 1)
                    dve.wait_ge(dve_read, N_DVE * c + read(at(CX, j), "dve"))
                    for streams, col, t in parts:
                        def tap(k):
                            return zs[:, j, :, k:k + t] if streams else z[:, j, k:k + t]

                        yy = cut(y, streams, col, 0, t)
                        link(dve.tensor_scalar(yy, tap(0), cw[:, 0, j:j + 1], None, ALU.mult))
                        for k in (1, 2):
                            link(dve.scalar_tensor_tensor(yy, tap(k), cw[:, k, j:j + 1], yy, ALU.mult, ALU.add))
                    dve.wait_ge(proj, NG * c + at(CB, j) + 1)
                    dve.tensor_tensor(y[:, 0:n], ps[:, at(CB, j) % NBANK, 0:n], y[:, 0:n], ALU.mult).then_inc(dve_read, 1)
                    dve.wait_ge(dve_read, N_DVE * c + read(at(CB, j), "dve"))
                    dve.wait_ge(act_read, N_ACT * c + read(at(CG, j), "act"))
                    dve.tensor_tensor(mix[:, 1, j, 0:n], y[:, 0:n], gate[:, 1, j, 0:n], ALU.mult).then_inc(mixed, 1)
                if n == T:
                    assert count[0] == STEPS, count[0]
                    dve.tensor_copy(u[:, :, 0:HIST], u[:, :, T:T + HIST])
                    dve.tensor_copy(z[:, :, 0:2], z[:, :, T:T + 2]).then_inc(chunk_end, 1)

            chunks(dve, chunk)
            for j in range(2):
                dve.tensor_copy(ends_u[:, j, :].rearrange("p (b t) -> p b t", b=NB), us[:, j, :, NQ:NQ + HIST]).then_inc(ends, 1)
                dve.tensor_copy(ends_z[:, j, :].rearrange("p (b t) -> p b t", b=NB), zs[:, j, :, NQ:NQ + 2]).then_inc(ends, 1)
            for bank, (rows, n) in enumerate(((rows_u, HIST), (rows_us, NB * HIST), (rows_z, 2), (rows_zs, NB * 2))):
                dve.wait_ge(ends_t, bank + 1)
                dve.tensor_copy(rows[0:n, :], ps[0:n, bank, 0:DP]).then_inc(ends_c, 1)

        @block.tensor
        def _(pe):
            pe.wait_ge(small, 16 * (4 + CONV_W))
            for j in range(2):
                pe.transpose(ps[:, 0, j * 120:(j + 1) * 120], past_u[:, j * P:(j + 1) * P], ident[0:NB * HIST, 0:NB * HIST])
                mm = pe.transpose(ps[:, 0, 240 + 16 * j:256 + 16 * j], past_z[:, j * P:(j + 1) * P], ident[0:NB * 2, 0:NB * 2])
            mm.then_inc(past_t, 1)
            pe.wait_ge(w_lo_done, KT)
            pe.wait_ge(pw_in, 64)
            pe.wait_ge(chunk_end, 1)

            def chunk(c, par, n):
                tiles = n // P
                pe.wait_ge(x_in[par], (c - par) * 16 + 32)
                for g, (kind, j, who) in enumerate(groups):
                    if g >= NBANK:
                        src, cc = g - NBANK, c
                    else:
                        src, cc = g + NG - NBANK, c - 1
                    whose = groups[src][2]
                    sem, per = (act_read, N_ACT) if whose == "act" else (dve_read, N_DVE)
                    wait_some(pe, sem, per * cc + read(src, whose))
                    c0 = kind + j * P
                    for k in range(KT):
                        for q, (wa, xa) in enumerate(((w_hi, xt_hi), (w_hi, xt_lo), (w_lo, xt_hi))):
                            mm = pe.matmul(ps[:, g % NBANK, 0:n], wa[:, k, c0:c0 + P],
                                           xa[:, par, 0:tiles, k * P:(k + 1) * P],
                                           start=(k == 0 and q == 0), stop=(k == KT - 1 and q == 2))
                    mm.then_inc(proj, 1)
                    if (kind, j) in ((CX, 0), (CG, 0)):
                        jj = 0 if kind == CX else 1
                        pe.wait_ge(pool_ready, 2 * c + jj + 1)
                        pe.wait_ge(chunk_end, c + 1)
                        pe.matmul(ps_a[:, jj, 0:n], pw[:, jj, :], pooled[:, jj, 0:n], start=True,
                                  stop=True).then_inc(pool_mm, 1)

            chunks(pe, chunk)
            pe.wait_ge(ends, 4)
            for bank, (rows, n) in enumerate(((lambda j: u[:, j, P:P + HIST], HIST), (lambda j: ends_u[:, j, :], NB * HIST),
                                              (lambda j: z[:, j, P:P + 2], 2), (lambda j: ends_z[:, j, :], NB * 2))):
                pe.wait_ge(mixed, 4 * (NCK + 1))
                for j in range(2):
                    mm = pe.transpose(ps[0:n, bank, j * P:(j + 1) * P], rows(j), ident[:, :])
                mm.then_inc(ends_t, 1)


def prompt_attention(nc, ident, q_all, k_all, v_all, gate_all, f_all, att_all):
    NJ = PT
    BLK = 8

    def s_chunks(j):
        return [(b, min(BLK, j + 1 - b)) for b in range(0, j + 1, BLK)]

    def t_chunks(j):
        return [(b, min(4, j + 1 - b)) for b in range(0, j + 1, 4)]

    def s_before(j):
        return sum(len(s_chunks(n)) for n in range(j))

    def t_before(j):
        return sum(len(t_chunks(n)) for n in range(j))

    NS, NTC, NG, NPREP = s_before(NJ), t_before(NJ), NJ // 2, 12
    NSLOT = 3
    PREP0 = 2
    spare = []
    for j in range(NJ):
        if PREP0 <= j < PREP0 + NPREP:
            spare.append(("prep", j - PREP0))
        if j % 2 == 0 and j >= 2:
            spare.append(("turn", j // 2 - 1))
    spare.append(("turn", NG - 1))

    with ExitStack() as ctx:
        m = Memory(nc, ctx, "pa")
        ident_r = m.sbuf("ident_r", [P, P], F32R)
        ident_b = m.sbuf("ident_b", [P, P], BF16)
        mask_b = m.sbuf("mask_b", [P, P], BF16)
        q_raw = m.sbuf("q_raw", [P, NJ, HD])
        k_raw = m.sbuf("k_raw", [P, NJ, HD])
        v_raw = m.sbuf("v_raw", [P, NJ, HD])
        g_raw = m.sbuf("g_raw", [P, 2, NJ, HD])
        f_b = m.sbuf("f_b", [P, 2, SEQ])
        split = m.sbuf("split", [P, NSLOT, 4, 2, HD], F32R)
        qs = m.sbuf("qs", [P, 2, SEQ], F32R)
        k_h = m.sbuf("k_h", [P, 2, SEQ], F32R)
        k_l = m.sbuf("k_l", [P, 2, SEQ], F32R)
        vs = m.sbuf("vs", [P, 2, NJ, 2, HD], F32R)
        s0 = m.sbuf("s0", [P, P])
        s1 = m.sbuf("s1", [P, 2 * P])
        s_ring = m.sbuf("s_ring", [P, 3, SEQ])
        mx = m.sbuf("mx", [P, 2, NJ, 2])
        nmax = m.sbuf("nmax", [P, 2, NJ])
        rsum = m.sbuf("rsum", [P, 2, NJ])
        rinv = m.sbuf("rinv", [P, 2, 2])
        pt_hi = m.sbuf("pt_hi", [P, 2, NJ, 2 * P], F32R)
        pt_lo = m.sbuf("pt_lo", [P, 2, NJ, 2 * P], F32R)
        o_t = m.sbuf("o_t", [P, 2, 2 * P])
        gr = m.sbuf("gr", [P, 2, 2, HD])
        parts = m.sbuf("parts", [P, 2, 2, 2, HD])
        ob = m.sbuf("ob", [P, 2, 2, HD])
        ps_s = m.psum("ps_s", [P, 2, BLK * P])
        ps_t = m.psum("ps_t", [P, 2, 512])
        ps_o = m.psum("ps_o", [P, 512])
        ps_x = m.psum("ps_x", [P, 512])

        consts = m.sem("consts_made")
        ident_done = m.sem("ident_rounded")
        qkv_in = m.sem("qkv_loaded")
        f_in = [m.sem(f"f_loaded{i}") for i in range(2)]
        g_in = [m.sem(f"gate_loaded{i}") for i in range(2)]
        vs_done = m.sem("v_split")
        v_hi = m.sem("v_hi_done")
        q_hi = m.sem("q_hi_done")
        split_done = m.sem("prep_split")
        prep_t = m.sem("prep_transposed")
        prep_done = m.sem("prep_copied")
        scored = m.sem("chunk_scored")
        s_taken = m.sem("chunk_with_f_and_max")
        max_done = m.sem("tile_max")
        exp_done = m.sem("tile_exp")
        turned = m.sem("p_chunk_transposed")
        hi_done = m.sem("p_hi_done")
        lo_done = m.sem("p_lo_done")
        zeroed = m.sem("corner_zeroed")
        pv_done = m.sem("pair_output")
        o_copied = m.sem("output_copied")
        o_turned = m.sem("output_turned")
        ri_done = m.sem("row_sums_inverted")
        gr_done = m.sem("gates_scaled")
        gated = m.sem("output_gated")
        ob_done = m.sem("output_added")
        stored = [m.sem(f"stored{i}") for i in range(2)]
        pool_on = m.sem("pool_passed_waits")
        sync_on = m.sem("sync_passed_waits")
        vector_on = m.sem("vector_passed_waits")
        block = ctx.enter_context(nc.Block())

        def heads(eng, body):
            with eng.Fori(0, H // 2 - 1) as i:
                body(i * 2, i, 0, False)
                body(i * 2 + 1, i, 1, False)
            body(H - 2, H // 2 - 1, 0, False)
            body(H - 1, H // 2 - 1, 1, True)

        def tile_after(h, par, j, n, last):
            if j + n < NJ:
                return h, par, j + n
            return None if last else (h + 1, 1 - par, j + n - NJ)

        def scores_of(j):
            if j < 2:
                return (s0, s1)[j]
            return s_ring[:, (j - 2) % 3, :]

        def before(g):
            return max(g - 1, 0)

        @block.sync
        def _(sp):
            def load_qkv(h):
                for raw, src in ((q_raw, q_all), (k_raw, k_all), (v_raw, v_all)):
                    sp.dma_start(raw[:, :, :], src[0:SEQ, ds(h * HD, HD)].rearrange("(t p) d -> p t d", p=P))\
                      .then_inc(qkv_in, 16)

            def load_f_gate(h, par):
                sp.dma_start(f_b[:, par, :].rearrange("p (t j) -> p t j", j=P),
                             f_all.rearrange("(t h) j -> h t j", h=H)[ds(h, 1), :, :]
                             .rearrange("o t j -> (o t) j").partition_broadcast(P)).then_inc(f_in[par], 16)
                sp.dma_start(g_raw[:, par, :, :],
                             gate_all[0:SEQ, ds(h * HD, HD)].rearrange("(t p) d -> p t d", p=P)).then_inc(g_in[par], 16)

            def body(h, i, par, last):
                if not last:
                    sp.wait_ge(s_taken, h * NS)
                    passed(sp, sync_on)
                    sp.wait_ge(gr_done, h * NG)
                    passed(sp, sync_on)
                    load_f_gate(h + 1, 1 - par)
                for g in range(NG):
                    if g == NG - 3 and not isinstance(h, int):
                        sp.wait_ge(split_done, (h + 2) * NPREP)
                        passed(sp, sync_on)
                        sp.wait_ge(vs_done, h + 2)
                        passed(sp, sync_on)
                        load_qkv(h + 2)
                    sp.wait_ge(ob_done, h * NG + g + 1)
                    sp.dma_start(att_all[2 * g * P:(2 * g + 2) * P, ds(h * HD, HD)].rearrange("(t p) d -> p t d", p=P),
                                 ob[:, g % 2, :, :]).then_inc(stored[g % 2], 16)

            load_qkv(0)
            load_f_gate(0, 0)
            sp.wait_ge(split_done, NPREP)
            sp.wait_ge(vs_done, 1)
            load_qkv(1)
            heads(sp, body)
            for p in range(2):
                sp.wait_ge(stored[p], 16 * H * NG // 2)

        @block.gpsimd
        def _(pool):
            pool.memset(ident_b[:, :], 0.0).then_inc(consts, 1)
            pool.memset(mask_b[:, :], 0.0).then_inc(consts, 1)
            pool.wait_ge(consts, 2)
            pool.affine_select(out=ident_b[:, :], in_=ident_b[:, :], compare_op=ALU.not_equal, fill=1.0,
                               base=0, pattern=[[-1, P]], channel_multiplier=1).then_inc(consts, 1)
            pool.affine_select(out=mask_b[:, :], in_=mask_b[:, :], compare_op=ALU.is_ge, fill=MASKED,
                               base=0, pattern=[[-1, P]], channel_multiplier=1).then_inc(consts, 1)

            def high(dst, src):
                return pool.tensor_scalar(dst, src, 1.0, 0.0, ALU.mult, ALU.add)

            def split_step(h, s):
                c, kind = s // 3, s % 3
                tiles = slice(4 * c, 4 * c + 4)
                slot = split[:, s % NSLOT, :, :, :]
                wait_some(pool, prep_t, h * NPREP + s + 1 - NSLOT)
                passed(pool, pool_on)
                if kind == 0:
                    high(slot[:, :, 0, :], q_raw[:, tiles, :]).then_inc(q_hi, 1)
                    pool.wait_ge(q_hi, h * 4 + c + 1)
                    pool.tensor_tensor(slot[:, :, 1, :], q_raw[:, tiles, :], slot[:, :, 0, :].bitcast(F32),
                                       ALU.subtract).then_inc(split_done, 1)
                elif kind == 1:
                    high(slot[:, :, 0, :], k_raw[:, tiles, :])
                    high(slot[:, :, 1, :], k_raw[:, tiles, :]).then_inc(split_done, 1)
                else:
                    k_high = split[:, (s - 1) % NSLOT, :, :, :]
                    pool.wait_ge(split_done, h * NPREP + s)
                    for part in range(2):
                        last = pool.tensor_tensor(slot[:, :, part, :], k_raw[:, tiles, :],
                                                  k_high[:, :, part, :].bitcast(F32), ALU.subtract)
                    last.then_inc(split_done, 1)

            def split_v(h, par):
                high(vs[:, par, :, 0, :], v_raw[:, :, :]).then_inc(v_hi, 1)
                pool.wait_ge(v_hi, h + 1)
                pool.tensor_tensor(vs[:, par, :, 1, :], v_raw[:, :, :], vs[:, par, :, 0, :].bitcast(F32),
                                   ALU.subtract).then_inc(vs_done, 1)

            def body(h, i, par, last):
                def scale_gates(g):
                    pool.wait_ge(g_in[par], 16 * i + 16)
                    pool.wait_ge(ri_done, h * NG + g + 1)
                    pool.wait_ge(gated, h * NG + before(g))
                    rows = rinv[:, g % 2, :].rearrange("p (t o) -> p t o", o=1).to_broadcast([P, 2, HD])
                    pool.tensor_tensor(gr[:, g % 2, :, :], g_raw[:, par, 2 * g:2 * g + 2, :], rows,
                                       ALU.mult).then_inc(gr_done, 1)

                def add_parts(g):
                    pool.wait_ge(gated, h * NG + g + 1)
                    pool.wait_ge(stored[g % 2], h * (16 * NG // 2) + 16 * (g // 2))
                    pool.tensor_tensor(ob[:, g % 2, :, :], parts[:, g % 2, 0, :, :], parts[:, g % 2, 1, :, :],
                                       ALU.add).then_inc(ob_done, 1)

                for j in range(NJ):
                    if j % 2 == 0:
                        g = j // 2
                        pool.wait_ge(pv_done, h * NG + before(g))
                        passed(pool, pool_on)
                        pool.memset(pt_hi[:, g % 2, 2 * g + 1, 0:P].bitcast(F32), 0.0)
                        pool.memset(pt_lo[:, g % 2, 2 * g + 1, 0:P].bitcast(F32), 0.0).then_inc(zeroed, 1)
                    if not last:
                        if j == 1:
                            pool.wait_ge(qkv_in, 48 * (h + 2))
                            pool.wait_ge(pv_done, h * NG)
                            passed(pool, pool_on)
                            split_v(h + 1, 1 - par)
                        if PREP0 - 1 <= j < PREP0 - 1 + NPREP:
                            split_step(h + 1, j - PREP0 + 1)
                    if j % 2 == 0 and j >= 2:
                        scale_gates(j // 2 - 1)
                    if j % 2 == 1 and j >= 3:
                        add_parts((j - 3) // 2)
                scale_gates(NG - 1)
                add_parts(NG - 1)

            pool.wait_ge(qkv_in, 48)
            for s in range(NPREP):
                split_step(0, s)
            split_v(0, 0)
            heads(pool, body)

        @block.scalar
        def _(act):
            def prep_copy(h, par, s):
                c, kind = s // 3, s % 3
                act.wait_ge(prep_t, h * NPREP + s + 1)
                act.activation((qs, k_h, k_l)[kind][:, par, c * 512:(c + 1) * 512], ps_x[:, :],
                               ACT.Copy).then_inc(prep_done, 1)

            def exps(h, par, j):
                act.wait_ge(max_done, h * NJ + j + 1)
                sc = scores_of(j)[:, 0:(j + 1) * P]
                act.activation(sc, sc, ACT.Exp, bias=nmax[:, par, j:j + 1],
                               accum_out=rsum[:, par, j:j + 1]).then_inc(exp_done, 1)

            def body(h, i, par, last):
                def copy_output(g):
                    act.wait_ge(pv_done, h * NG + g + 1)
                    act.wait_ge(o_turned, h * NG + before(g))
                    act.activation(o_t[:, g % 2, :], ps_o[:, 0:2 * P], ACT.Copy).then_inc(o_copied, 1)

                for j in range(NJ):
                    nxt = tile_after(h, par, j, 1, last)
                    if nxt:
                        exps(*nxt)
                    if PREP0 <= j < PREP0 + NPREP and not last:
                        prep_copy(h + 1, 1 - par, j - PREP0)
                    if j % 2 == 0 and j >= 2:
                        copy_output(j // 2 - 1)
                    g = j // 2
                    act.wait_ge(pv_done, h * NG + before(g))
                    for n, (b, nb) in enumerate(t_chunks(j)):
                        act.wait_ge(turned, h * NTC + t_before(j) + n + 1)
                        act.activation(pt_hi[:, g % 2, b:b + nb, (j % 2) * P:(j % 2 + 1) * P],
                                       ps_t[:, (t_before(j) + n) % 2, 0:nb * P].rearrange("p (b q) -> p b q", q=P),
                                       ACT.Copy).then_inc(hi_done, 1)
                copy_output(NG - 1)

            for s in range(NPREP):
                prep_copy(0, 0, s)
            exps(0, 0, 0)
            heads(act, body)

        @block.vector
        def _(dve):
            dve.tensor_copy(ident_r[:, :], ident[:, :]).then_inc(ident_done, 1)

            def take_scores(h, par, j):
                parts_j = s_chunks(j)
                for n, (b, nb) in enumerate(parts_j):
                    dve.wait_ge(scored, h * NS + s_before(j) + n + 1)
                    passed(dve, vector_on)
                    dve.tensor_tensor_reduce(scores_of(j)[:, b * P:(b + nb) * P],
                                             ps_s[:, (s_before(j) + n) % 2, 0:nb * P],
                                             f_b[:, par, b * P:(b + nb) * P], 1.0, 3 * MASKED,
                                             ALU.subtract, ALU.max, mx[:, par, j, n:n + 1]).then_inc(s_taken, 1)
                dve.wait_ge(s_taken, h * NS + s_before(j + 1))
                if len(parts_j) == 1:
                    dve.tensor_scalar(nmax[:, par, j:j + 1], mx[:, par, j, 0:1], -1.0, None, ALU.mult)\
                       .then_inc(max_done, 1)
                else:
                    dve.tensor_scalar(nmax[:, par, j:j + 1], mx[:, par, j, 0:1], mx[:, par, j, 1:2], -1.0,
                                      ALU.max, ALU.mult).then_inc(max_done, 1)

            def body(h, i, par, last):
                def gate_output(g):
                    dve.wait_ge(o_turned, h * NG + g + 1)
                    dve.wait_ge(gr_done, h * NG + g + 1)
                    dve.wait_ge(ob_done, h * NG + before(g))
                    rows = ps_x[:, 0:2 * P].rearrange("p (t s d) -> p t s d", t=2, s=2)
                    for s in range(2):
                        done = dve.tensor_tensor(parts[:, g % 2, s, :, :], rows[:, :, s, :], gr[:, g % 2, :, :],
                                                 ALU.mult)
                    done.then_inc(gated, 1)

                for j in range(NJ):
                    nxt = tile_after(h, par, j, 2, last)
                    if nxt:
                        if j == NJ - 2:
                            dve.wait_ge(f_in[1 - par], 16 * (i + par) + 16)
                        take_scores(*nxt)
                    for n, (b, nb) in enumerate(t_chunks(j)):
                        dve.wait_ge(hi_done, h * NTC + t_before(j) + n + 1)
                        cols = slice((j % 2) * P, (j % 2 + 1) * P)
                        g = j // 2
                        dve.tensor_tensor(pt_lo[:, g % 2, b:b + nb, cols],
                                          ps_t[:, (t_before(j) + n) % 2, 0:nb * P].rearrange("p (b q) -> p b q", q=P),
                                          pt_hi[:, g % 2, b:b + nb, cols].bitcast(F32),
                                          ALU.subtract).then_inc(lo_done, 1)
                    if j % 2 == 1:
                        dve.wait_ge(exp_done, h * NJ + j + 1)
                        dve.wait_ge(gr_done, h * NG + before(j // 2))
                        dve.reciprocal(rinv[:, (j // 2) % 2, :], rsum[:, par, j - 1:j + 1]).then_inc(ri_done, 1)
                    elif j >= 2:
                        gate_output(j // 2 - 1)
                gate_output(NG - 1)

            dve.wait_ge(f_in[0], 16)
            take_scores(0, 0, 0)
            take_scores(0, 0, 1)
            heads(dve, body)

        @block.tensor
        def _(pe):
            pe.wait_ge(consts, 4)
            pe.wait_ge(ident_done, 1)

            def prep(h, s):
                pe.wait_ge(split_done, h * NPREP + s + 1)
                for t in range(4):
                    mm = pe.transpose(ps_x[:, t * P:(t + 1) * P].bitcast(F32R),
                                      split[:, s % NSLOT, t, :, :].rearrange("p s d -> p (s d)"), ident_r[:, :])
                mm.then_inc(prep_t, 1)

            def score(h, par, j):
                queries = qs[:, par, j * P:(j + 1) * P]
                for n, (b, nb) in enumerate(s_chunks(j)):
                    at = s_before(j) + n
                    wait_some(pe, s_taken, h * NS + at - 1)
                    for o in range(0, nb, 4):
                        w = min(4, nb - o)
                        cols = max(w, 2) * P
                        keys = slice((b + o) * P, (b + o) * P + cols)
                        out = ps_s[:, at % 2, o * P:o * P + cols]
                        pe.matmul(out, queries, k_h[:, par, keys], start=True, stop=False)
                        if b + o + w == j + 1:
                            pe.matmul(ps_s[:, at % 2, (j - b) * P:(j - b + 1) * P], ident_b[:, :], mask_b[:, :],
                                      start=False, stop=False)
                        mm = pe.matmul(out, queries, k_l[:, par, keys], start=False, stop=True)
                    mm.then_inc(scored, 1)

            def body(h, i, par, last):
                def free_spare(use):
                    n = spare.index(use)
                    if last:
                        n = [x for x in spare if x[0] == "turn"].index(use)
                        former = ("turn", n - 1) if n else None
                    else:
                        former = spare[n - 1] if n else None
                    if former is None:
                        pe.wait_ge(gated, h * NG)
                    elif former[0] == "prep":
                        pe.wait_ge(prep_done, (h + 1) * NPREP + former[1] + 1)
                    else:
                        pe.wait_ge(gated, h * NG + former[1] + 1)

                def values(g):
                    pe.wait_ge(zeroed, h * NG + g + 1)
                    pe.wait_ge(o_copied, h * NG + g)
                    if g == 0:
                        pe.wait_ge(vs_done, h + 1)
                    chunks = t_chunks(2 * g + 1)
                    for n, (b, nb) in enumerate(chunks):
                        pe.wait_ge(lo_done, h * NTC + t_before(2 * g + 1) + n + 1)
                        for k in range(b, b + nb):
                            v = vs[:, par, k, :, :].rearrange("p s d -> p (s d)")
                            pe.matmul(ps_o[:, 0:2 * P], v, pt_hi[:, g % 2, k, :], start=(k == 0), stop=False)
                            mm = pe.matmul(ps_o[:, 0:2 * P], v, pt_lo[:, g % 2, k, :], start=False,
                                           stop=(k == 2 * g + 1))
                    mm.then_inc(pv_done, 1)

                def turn_output(g):
                    pe.wait_ge(o_copied, h * NG + g + 1)
                    free_spare(("turn", g))
                    for t in range(2):
                        mm = pe.transpose(ps_x[:, t * P:(t + 1) * P], o_t[:, g % 2, t * P:(t + 1) * P], ident[:, :])
                    mm.then_inc(o_turned, 1)

                for j in range(NJ):
                    nxt = tile_after(h, par, j, 2, last)
                    if nxt:
                        if j == NJ - 2:
                            pe.wait_ge(prep_done, (h + 2) * NPREP)
                        score(*nxt)
                    if PREP0 <= j < PREP0 + NPREP and not last:
                        free_spare(("prep", j - PREP0))
                        prep(h + 1, j - PREP0)
                    if j % 2 == 0 and j >= 2:
                        values(j // 2 - 1)
                    pe.wait_ge(exp_done, h * NJ + j + 1)
                    for n, (b, nb) in enumerate(t_chunks(j)):
                        at = t_before(j) + n
                        pe.wait_ge(lo_done, h * NTC + max(at - 1, 0))
                        for k in range(nb):
                            mm = pe.transpose(ps_t[:, at % 2, k * P:(k + 1) * P],
                                              scores_of(j)[:, (b + k) * P:(b + k + 1) * P], ident[:, :])
                        mm.then_inc(turned, 1)
                    if j % 2 == 0 and j >= 2:
                        turn_output(j // 2 - 1)
                values(NG - 1)
                turn_output(NG - 1)

            for s in range(NPREP):
                wait_some(pe, prep_done, s)
                prep(0, s)
            pe.wait_ge(prep_done, NPREP)
            score(0, 0, 0)
            score(0, 0, 1)
            heads(pe, body)


def sample_attention(nc, ident, q_all, cache_k, cache_v, new_k, new_v, gate_all, f_t_all, o_all, att_all):
    TC = PAST // P
    TILES = [range(0, 3), range(3, 6), range(6, 9)]
    WID = [3 * P, 3 * P, 2 * P + NQ]
    OFF = [0, 3 * P, 6 * P]
    NC_ = len(TILES)
    NP = H // 2
    KB = NC_ * NP
    PB = [range(0, 4), range(4, 8), range(8, 9)]
    ROW = 640
    with ExitStack() as ctx:
        m = Memory(nc, ctx, "sa")
        ident_b = m.sbuf("ident_b", [P, P], BF16)
        mask_b = m.sbuf("mask_b", [P, NQ], BF16)
        later = m.sbuf("later", [P, H, NQ])
        mask_f = m.sbuf("mask_f", [P, NQ])
        own = m.sbuf("own", [P, H])
        sel_f = m.sbuf("sel_f", [P, P])
        sel = m.sbuf("sel", [P, P], F32R)
        q_in = m.sbuf("q_in", [P, DA])
        q_t = m.sbuf("q_t", [P, NP, P])
        qz_hi = m.sbuf("qz_hi", [P, 2, ROW], F32R)
        qz_lo = m.sbuf("qz_lo", [P, 2, ROW], F32R)
        f_s = m.sbuf("f_s", [P, 2, PAST + NQ], F32R)
        k_c = m.sbuf("k_c", [P, 2, TC + 1, DA])
        v_c = m.sbuf("v_c", [P, TC + 1, DA])
        v_hi = m.sbuf("v_hi", [P, 2, TC + 1, DA], F32R)
        v_lo = m.sbuf("v_lo", [P, 2, TC + 1, DA], F32R)
        kt_hi = m.sbuf("kt_hi", [P, NC_, NP, 3 * P], F32R)
        kt_lo = m.sbuf("kt_lo", [P, NC_, NP, 3 * P], F32R)
        mx = m.sbuf("mx", [P, 2, 4])
        nmax = m.sbuf("nmax", [P, 2])
        p = m.sbuf("p", [P, 2, PAST + NQ])
        rsum = m.sbuf("rsum", [P, 2, 4])
        own_inv = m.sbuf("own_inv", [P, H])
        p_hi = m.sbuf("p_hi", [P, TC + 1, P], F32R)
        p_lo = m.sbuf("p_lo", [P, TC + 1, P], F32R)
        o_own = m.sbuf("o_own", [P, H, HD])
        o = m.sbuf("o", [P, 2, HD])
        ps_k = m.psum("ps_k", [P, 2, 512])
        ps_s = m.psum("ps_s", [P, NC_, 512])
        ps_p = m.psum("ps_p", [P, 2, 512])
        ps_o = m.psum("ps_o", [P, 512])

        made = m.sem("consts_made")
        rounded = m.sem("consts_rounded")
        q_loaded = m.sem("q_loaded")
        q_turned = m.sem("q_transposed")
        q_copied = m.sem("q_copied")
        qz_h = m.sem("qz_hi_done")
        qz_done = m.sem("qz_done")
        k_in = [m.sem(f"k_loaded{i}") for i in range(2)]
        v_in = m.sem("v_loaded")
        f_in = [m.sem(f"f_loaded{i}") for i in range(2)]
        k_turned = m.sem("k_bank_transposed")
        kt_h = m.sem("kt_hi_done")
        kt_l = m.sem("kt_lo_done")
        vh_done = m.sem("v_hi_done")
        vn_h = m.sem("v_new_hi_done")
        vn_done = m.sem("v_new_lo_done")
        vl_done = m.sem("v_lo_done")
        scored = m.sem("chunk_scored")
        chunk_max = m.sem("chunk_max")
        all_max = m.sem("row_max")
        neg_max = m.sem("row_neg_max")
        exp_done = m.sem("chunk_exp")
        p_turned = m.sem("p_bank_transposed")
        p_h = m.sem("p_hi_done")
        p_l = m.sem("p_lo_done")
        pv_done = m.sem("values_done")
        out_step = m.sem("output_steps")
        o_done = m.sem("o_done")
        o_stored = [m.sem(f"o_stored{i}") for i in range(2)]
        back = m.sem("o_and_gate_loaded")
        gated = m.sem("o_gated")
        att_stored = m.sem("att_stored")
        pool_on = m.sem("pool_passed_waits")
        sync_on = m.sem("sync_passed_waits")
        block = ctx.enter_context(nc.Block())

        def streams(eng, body):
            body(0, 0, False, True)
            with eng.Fori(0, NB // 2 - 1) as i:
                body(i * 2 + 1, 1, True, True)
                body(i * 2 + 2, 0, True, True)
            body(NB - 1, 1, True, False)

        def count(b, par, unit):
            return (b - par) * (unit // 2) + unit

        @block.sync
        def _(sp):
            def load_k(b, par):
                sp.dma_start(k_c[:, par, 0:TC, :],
                             cache_k[ds(b * PAST, PAST), :].rearrange("(t p) d -> p t d", p=P)).then_inc(k_in[par], 16)
                sp.dma_start(k_c[0:NQ, par, TC, :], new_k[ds(b * NQ, NQ), :]).then_inc(k_in[par], 16)
                for part in range(2):
                    sp.dma_start(f_s[part * H:(part + 1) * H, par, :].bitcast(F32),
                                 f_t_all[ds(b * H + part * NB * H, H), 0:PAST + NQ]).then_inc(f_in[par], 16)

            def load_v(b):
                sp.dma_start(v_c[:, 0:TC, :],
                             cache_v[ds(b * PAST, PAST), :].rearrange("(t p) d -> p t d", p=P)).then_inc(v_in, 16)
                sp.dma_start(v_c[0:NQ, TC, :], new_v[ds(b * NQ, NQ), :]).then_inc(v_in, 16)

            def store(b, par):
                sp.wait_ge(o_done, b + 1)
                sp.dma_start(o_all[ds(b * P, P), :], o[:, par, :]).then_inc(o_stored[par], 16)

            sp.wait_ge(made, 8)
            sp.dma_start(q_in[:, :], q_all[SEQ:SEQ + P, :]).then_inc(q_loaded, 16)
            load_k(0, 0)
            load_v(0)
            load_k(1, 1)

            def body(b, par, before, after):
                if after:
                    if before:
                        sp.wait_ge(k_turned, b * KB)
                        passed(sp, sync_on)
                        sp.wait_ge(scored, b * NC_)
                        passed(sp, sync_on)
                        load_k(b + 1, 1 - par)
                    sp.wait_ge(vn_done, b + 1)
                    passed(sp, sync_on)
                    sp.wait_ge(vl_done, 4 * (b + 1))
                    passed(sp, sync_on)
                    load_v(b + 1)
                if before:
                    store(b - 1, 1 - par)

            streams(sp, body)
            store(NB - 1, 1)
            for par in range(2):
                sp.wait_ge(o_stored[par], 16 * NB // 2)
            for b in range(NB):
                sp.dma_start(o_own[b * NQ:(b + 1) * NQ, :, :], o_all[b * P:(b + 1) * P, :].rearrange("(h q) d -> q h d", q=NQ)).then_inc(back, 16)
            sp.dma_start(q_in[:, :], gate_all[SEQ:SEQ + P, :]).then_inc(back, 16)
            sp.wait_ge(gated, 1)
            sp.dma_start(att_all[SEQ:SEQ + P, :], o_own[:, :, :].rearrange("p h d -> p (h d)")).then_inc(att_stored, 16)
            sp.wait_ge(att_stored, 16)

        @block.gpsimd
        def _(pool):
            pool.memset(ident_b[:, :], 0.0).then_inc(made, 1)
            pool.memset(own[:, :], 1.0).then_inc(made, 1)
            pool.memset(later[:, :, :], 0.0).then_inc(made, 1)
            pool.memset(sel_f[:, :], 0.0).then_inc(made, 1)
            pool.memset(qz_hi[:, :, :].bitcast(F32), 0.0).then_inc(made, 1)
            pool.memset(qz_lo[:, :, :].bitcast(F32), 0.0).then_inc(made, 1)
            pool.memset(f_s[:, 0, :].bitcast(F32), 0.0).then_inc(made, 1)
            pool.memset(f_s[:, 1, :].bitcast(F32), 0.0).then_inc(made, 1)
            pool.wait_ge(made, 8)
            pool.affine_select(out=ident_b[:, :], in_=ident_b[:, :], compare_op=ALU.not_equal, fill=1.0,
                               base=0, pattern=[[-1, P]], channel_multiplier=1).then_inc(made, 1)
            pool.affine_select(out=own[:, :], in_=own[:, :], compare_op=ALU.is_ge, fill=0.0,
                               base=0, pattern=[[-NQ, H]], channel_multiplier=1).then_inc(made, 1)
            pool.affine_select(out=later[:, :, :], in_=later[:, :, :], compare_op=ALU.is_ge, fill=MASKED,
                               base=0, pattern=[[-NQ, H], [-1, NQ]], channel_multiplier=1).then_inc(made, 1)
            rows = sel_f[:, :].rearrange("p (h q) -> p h q", h=H)
            pool.affine_select(out=rows, in_=rows, compare_op=ALU.not_equal, fill=-1.0,
                               base=0, pattern=[[-1, H], [0, NQ]], channel_multiplier=1).then_inc(made, 1)
            pool.wait_ge(made, 12)
            pool.affine_select(out=own[:, :], in_=own[:, :], compare_op=ALU.is_ge, fill=0.0,
                               base=NQ - 1, pattern=[[NQ, H]], channel_multiplier=-1).then_inc(made, 1)
            pool.affine_select(out=rows, in_=rows, compare_op=ALU.not_equal, fill=-1.0,
                               base=-H, pattern=[[-1, H], [0, NQ]], channel_multiplier=1).then_inc(made, 1)

            def lay_q(b, par):
                wait_some(pool, scored, NC_ * (b - 1))
                for half in range(2):
                    rows = slice(64 * half, 64 * half + 64)
                    cols = slice(NQ * half, NQ * half + NQ)
                    src = q_t[rows, :, ds(b * NQ, NQ)]
                    hi = qz_hi[rows, par, :].rearrange("p (a c) -> p a c", c=160)[:, :, cols]
                    lo = qz_lo[rows, par, :].rearrange("p (a c) -> p a c", c=160)[:, :, cols]
                    pool.tensor_copy(hi, src).then_inc(qz_h, 1)
                    pool.wait_ge(qz_h, 2 * b + half + 1)
                    passed(pool, pool_on)
                    pool.tensor_tensor(lo, src, hi.bitcast(F32), ALU.subtract).then_inc(qz_done, 1)
                    pool.wait_ge(qz_done, 2 * b + half + 1)

            def split_v_hi(b, par):
                pool.wait_ge(v_in, 32 * (b + 1))
                wait_some(pool, pv_done, b - 1)
                passed(pool, pool_on)
                pool.tensor_scalar(v_hi[:, par, 0:TC, :], v_c[:, 0:TC, :], 1.0, 0.0, ALU.mult,
                                   ALU.add).then_inc(vh_done, 1)
                pool.wait_ge(vh_done, b + 1)
                passed(pool, pool_on)
                pool.tensor_scalar(v_hi[0:NQ, par, TC, :], v_c[0:NQ, TC, :], 1.0, 0.0, ALU.mult,
                                   ALU.add).then_inc(vn_h, 1)
                pool.wait_ge(vn_h, b + 1)
                pool.tensor_tensor(v_lo[0:NQ, par, TC, :], v_c[0:NQ, TC, :],
                                   v_hi[0:NQ, par, TC, :].bitcast(F32), ALU.subtract).then_inc(vn_done, 1)
                pool.wait_ge(vn_done, b + 1)

            pool.wait_ge(q_copied, 1)
            lay_q(0, 0)

            def body(b, par, before, after):
                if after:
                    lay_q(b + 1, 1 - par)
                split_v_hi(b, par)

            streams(pool, body)

        def k_banks(b, c):
            return [(b * KB + c * NP + n, n) for n in range(NP)]

        @block.scalar
        def _(act):
            def high_k(b, c):
                for at, n in k_banks(b, c):
                    act.wait_ge(k_turned, at + 1)
                    act.activation(kt_hi[:, c, n, 0:WID[c]], ps_k[:, n % 2, 0:WID[c]], ACT.Copy).then_inc(kt_h, 1)

            def high_p(b):
                for n, tiles in enumerate(PB):
                    act.wait_ge(p_turned, b * 3 + n + 1)
                    rows = P if n < 2 else NQ
                    src = ps_p[0:rows, n % 2, 0:len(tiles) * P].rearrange("p (t r) -> p t r", r=P)
                    act.activation(p_hi[0:rows, tiles[0]:tiles[-1] + 1, :], src, ACT.Copy).then_inc(p_h, 1)

            def exps(b, par):
                act.wait_ge(neg_max, b + 1)
                for c in range(NC_):
                    act.activation(p[:, par, OFF[c]:OFF[c] + WID[c]], ps_s[:, c, 0:WID[c]], ACT.Exp,
                                   bias=nmax[:, par:par + 1], accum_out=rsum[:, par, c:c + 1]).then_inc(exp_done, 1)

            high_k(0, 0)
            high_k(0, 1)

            def body(b, par, before, after):
                high_k(b, 2)
                if after:
                    high_k(b + 1, 0)
                    high_k(b + 1, 1)
                if before:
                    high_p(b - 1)
                exps(b, par)

            streams(act, body)
            high_p(NB - 1)

        @block.vector
        def _(dve):
            dve.wait_ge(made, 14)
            dve.tensor_tensor(later[:, :, :], later[:, :, :],
                              own[:, :].rearrange("p (h o) -> p h o", o=1).to_broadcast([P, H, NQ]),
                              ALU.mult).then_inc(rounded, 1)
            dve.wait_ge(rounded, 1)
            dve.tensor_reduce(mask_f[:, :], later[:, :, :].rearrange("p h q -> p q h"), AX_X, ALU.add).then_inc(rounded, 1)
            dve.wait_ge(rounded, 2)
            dve.tensor_copy(mask_b[:, :], mask_f[:, :]).then_inc(rounded, 1)
            dve.tensor_copy(sel[:, :], sel_f[:, :]).then_inc(rounded, 1)
            dve.wait_ge(q_turned, 1)
            dve.tensor_copy(q_t[:, :, :].rearrange("p a r -> p (a r)"), ps_o[:, :]).then_inc(q_copied, 1)

            def low_k(b, c):
                for at, n in k_banks(b, c):
                    dve.wait_ge(kt_h, at + 1)
                    dve.tensor_tensor(kt_lo[:, c, n, 0:WID[c]], ps_k[:, n % 2, 0:WID[c]],
                                      kt_hi[:, c, n, 0:WID[c]].bitcast(F32), ALU.subtract).then_inc(kt_l, 1)

            def low_v(b, par, quarter):
                if quarter == 0:
                    dve.wait_ge(vh_done, b + 1)
                tiles = slice(quarter * TC // 4, (quarter + 1) * TC // 4)
                dve.tensor_tensor(v_lo[:, par, tiles, :], v_c[:, tiles, :], v_hi[:, par, tiles, :].bitcast(F32),
                                  ALU.subtract).then_inc(vl_done, 1)

            def low_p(b):
                for n, tiles in enumerate(PB):
                    dve.wait_ge(p_h, b * 3 + n + 1)
                    rows = P if n < 2 else NQ
                    tt = slice(tiles[0], tiles[-1] + 1)
                    src = ps_p[0:rows, n % 2, 0:len(tiles) * P].rearrange("p (t r) -> p t r", r=P)
                    dve.tensor_tensor(p_lo[0:rows, tt, :], src, p_hi[0:rows, tt, :].bitcast(F32),
                                      ALU.subtract).then_inc(p_l, 1)

            def maxima(b, par, c):
                dve.wait_ge(scored, b * NC_ + c + 1)
                dve.tensor_reduce(mx[:, par, c:c + 1], ps_s[:, c, 0:WID[c]], AX_X, ALU.max).then_inc(chunk_max, 1)

            def output(b, par):
                dve.wait_ge(exp_done, b * NC_ + NC_)
                dve.tensor_reduce(rsum[:, par, 3:4], rsum[:, par, 0:3], AX_X, ALU.add).then_inc(out_step, 1)
                dve.wait_ge(out_step, b * 4 + 1)
                dve.reciprocal(rsum[:, par, 3:4], rsum[:, par, 3:4]).then_inc(out_step, 1)
                dve.wait_ge(out_step, b * 4 + 2)
                dve.tensor_scalar(own_inv[:, :], own[:, :], rsum[:, par, 3:4], None, ALU.mult).then_inc(out_step, 1)
                dve.wait_ge(out_step, b * 4 + 3)
                dve.wait_ge(pv_done, b + 1)
                dve.tensor_tensor(o_own[:, :, :], ps_o[:, :].rearrange("p (h d) -> p h d", h=H),
                                  own_inv[:, :].rearrange("p (h o) -> p h o", o=1).to_broadcast([P, H, HD]),
                                  ALU.mult).then_inc(out_step, 1)
                dve.wait_ge(out_step, b * 4 + 4)
                dve.wait_ge(o_stored[par], count(b, par, 16) - 16)
                dve.tensor_reduce(o[:, par, :], o_own[:, :, :].rearrange("p h d -> p d h"), AX_X,
                                  ALU.add).then_inc(o_done, 1)

            low_k(0, 0)
            low_k(0, 1)

            def body(b, par, before, after):
                low_k(b, 2)
                low_v(b, par, 0)
                maxima(b, par, 0)
                low_v(b, par, 1)
                if after:
                    low_k(b + 1, 0)
                maxima(b, par, 1)
                low_v(b, par, 2)
                if after:
                    low_k(b + 1, 1)
                low_v(b, par, 3)
                if before:
                    low_p(b - 1)
                maxima(b, par, 2)
                dve.wait_ge(chunk_max, b * NC_ + NC_)
                dve.tensor_reduce(mx[:, par, 3:4], mx[:, par, 0:3], AX_X, ALU.max).then_inc(all_max, 1)
                dve.wait_ge(all_max, b + 1)
                dve.tensor_scalar(nmax[:, par:par + 1], mx[:, par, 3:4], -1.0, None, ALU.mult).then_inc(neg_max, 1)
                if before:
                    output(b - 1, 1 - par)

            streams(dve, body)
            low_p(NB - 1)
            output(NB - 1, 1)
            dve.wait_ge(back, 16 * (NB + 1))
            dve.tensor_tensor(o_own[:, :, :], o_own[:, :, :], q_in[:, :].rearrange("p (h d) -> p h d", h=H),
                              ALU.mult).then_inc(gated, 1)

        @block.tensor
        def _(pe):
            pe.wait_ge(q_loaded, 16)
            for n in range(NP):
                mm = pe.transpose(ps_o[:, n * P:(n + 1) * P], q_in[:, n * P:(n + 1) * P], ident[:, :])
            mm.then_inc(q_turned, 1)

            def turn_k(b, par, c, n):
                if n == 0 and c == 0:
                    pe.wait_ge(k_in[par], count(b, par, 32))
                wait_some(pe, kt_l, b * KB + c * NP + n - 1)
                for at, t in enumerate(TILES[c]):
                    rows = P if t < TC else NQ
                    mm = pe.transpose(ps_k[:, n % 2, at * P:at * P + rows],
                                      k_c[0:rows, par, t, n * P:(n + 1) * P], ident[0:rows, 0:rows])
                mm.then_inc(k_turned, 1)

            def score(b, par, c, ahead):
                out = ps_s[:, c, 0:WID[c]]
                if c == 0:
                    pe.wait_ge(f_in[par], count(b, par, 32))
                    pe.wait_ge(qz_done, 2 * b + 2)
                wait_some(pe, exp_done, NC_ * b - (NC_ - 1 - c))
                pe.matmul(out, sel[:, :], f_s[:, par, OFF[c]:OFF[c] + WID[c]], start=True, stop=False)
                if c == NC_ - 1:
                    pe.matmul(ps_s[:, c, 2 * P:2 * P + NQ], ident_b[:, :], mask_b[:, :], start=False, stop=False)
                for n in range(NP):
                    pe.wait_ge(kt_l, b * KB + c * NP + n + 1)
                    z = slice(n * P, (n + 1) * P)
                    for q, (qa, ka) in enumerate(((qz_hi, kt_hi), (qz_lo, kt_hi), (qz_hi, kt_lo))):
                        mm = pe.matmul(out, qa[:, par, z], ka[:, c, n, 0:WID[c]], start=False,
                                       stop=(n == NP - 1 and q == 2))
                    if n == NP - 1:
                        mm.then_inc(scored, 1)
                    ahead(n)

            def turn_p(b, par):
                pe.wait_ge(exp_done, b * NC_ + NC_)
                for n, tiles in enumerate(PB):
                    wait_some(pe, p_l, b * 3 + max(n - 1, 0))
                    for at, t in enumerate(tiles):
                        w = P if t < TC else NQ
                        mm = pe.transpose(ps_p[0:w, n % 2, at * P:(at + 1) * P], p[:, par, t * P:t * P + w], ident[:, :])
                    mm.then_inc(p_turned, 1)

            def values(b, par):
                wait_some(pe, o_done, b)
                pe.wait_ge(vl_done, 4 * b + 4)
                pe.wait_ge(vn_done, b + 1)
                for n, tiles in enumerate(PB):
                    pe.wait_ge(p_l, b * 3 + n + 1)
                    for t in tiles:
                        rows = P if t < TC else NQ
                        for q, (pa, va) in enumerate(((p_hi, v_hi), (p_lo, v_hi), (p_hi, v_lo))):
                            mm = pe.matmul(ps_o[:, :], pa[0:rows, t, :], va[0:rows, par, t, :],
                                           start=(t == 0 and q == 0), stop=(t == TC and q == 2))
                mm.then_inc(pv_done, 1)

            for c in range(2):
                for n in range(NP):
                    turn_k(0, 0, c, n)
            pe.wait_ge(rounded, 4)
            pe.wait_ge(made, 14)
            pe.wait_ge(q_copied, 1)

            def body(b, par, before, after):
                score(b, par, 0, lambda n: turn_k(b, par, 2, n))
                score(b, par, 1, (lambda n: turn_k(b + 1, 1 - par, 0, n)) if after else (lambda n: None))
                score(b, par, 2, (lambda n: turn_k(b + 1, 1 - par, 1, n)) if after else (lambda n: None))
                if before:
                    turn_p(b - 1, 1 - par)
                    values(b - 1, 1 - par)

            streams(pe, body)
            turn_p(NB - 1, 1)
            values(NB - 1, 1)


def output_projection(nc, ident, w_out, x_prompt, x_sample, att_all, mix_all, y_prompt, y_sample):
    NM = 4
    rows_of = [0, 1, 6, 7, 2, 3, 4, 5]
    NCH = D // 512
    with ExitStack() as ctx:
        m = Memory(nc, ctx, "op")
        w_hi = m.sbuf("w_hi", [P, KT, D], F32R)
        w_lo = m.sbuf("w_lo", [P, KT, D], F32R)
        w_raw = m.sbuf("w_raw", [P, 2, D])
        x = m.sbuf("x", [P, 2, D])
        att = m.sbuf("att", [P, 2, DA])
        mix = m.sbuf("mix", [P, 2, NM, P])
        mt_hi = m.sbuf("mt_hi", [P, 2, 2 * NM, P], F32R)
        mt_lo = m.sbuf("mt_lo", [P, 2, 2 * NM, P], F32R)
        y = m.sbuf("y", [P, 2, D])
        ps = m.psum("ps", [P, 2, NCH, 512])
        ps_t = m.psum("ps_t", [P, 2, 512])

        w_in_sem = [m.sem(f"w_loaded{i}") for i in range(2)]
        w_hi_done = m.sem("w_hi_done")
        w_lo_done = m.sem("w_lo_done")
        x_in = [m.sem(f"x_loaded{i}") for i in range(2)]
        mixed_in = [m.sem(f"mixed_loaded{i}") for i in range(2)]
        turned = m.sem("attention_transposed")
        hi_done = m.sem("hi_done")
        lo_done = m.sem("lo_done")
        proj = m.sem("chunk_projected")
        y_done = m.sem("y_done")
        stored = [m.sem(f"stored{i}") for i in range(2)]
        block = ctx.enter_context(nc.Block())

        def steps(eng, step, prep):
            prep(0, 0)
            step(0, 0, lambda: prep(1, 1))
            with eng.Fori(0, PT // 2 - 1) as i:
                step(i * 2 + 1, 1, lambda: prep(i * 2 + 2, 0))
                step(i * 2 + 2, 0, lambda: prep(i * 2 + 3, 1))
            step(PT - 1, 1, lambda: prep(PT, 0))
            step(PT, 0, lambda: None)

        @block.sync
        def _(sp):
            def load(t, par, x_rows):
                wait_some(sp, lo_done, 2 * (t - 1))
                sp.dma_start(att[:, par, :], att_all[ds(t * P, P), :]).then_inc(mixed_in[par], 16)
                sp.dma_start(mix[:, par, :, :],
                             mix_all.rearrange("m p t -> p m t")[:, :, ds(t * P, P)]).then_inc(mixed_in[par], 16)
                wait_some(sp, y_done, NCH * (t - 1))
                sp.dma_start(x[:, par, :], x_rows).then_inc(x_in[par], 16)

            def store(t, par, rows):
                sp.wait_ge(y_done, NCH * t + NCH)
                sp.dma_start(rows, y[:, par, :]).then_inc(stored[par], 16)

            load(0, 0, x_prompt[0:P, :])
            load(1, 1, x_prompt[P:2 * P, :])
            for k in range(KT):
                if k >= 2:
                    sp.wait_ge(w_lo_done, k - 1)
                sp.dma_start(w_raw[:, k % 2, :], w_out[k * P:(k + 1) * P, :]).then_inc(w_in_sem[k % 2], 16)
            with sp.Fori(0, PT // 2 - 1) as i:
                for par in range(2):
                    t = i * 2 + par
                    store(t, par, y_prompt[ds(t * P, P), :])
                    load(t + 2, par, x_prompt[ds((t + 2) * P, P), :])
            store(PT - 2, 0, y_prompt[(PT - 2) * P:(PT - 1) * P, :])
            load(PT, 0, x_sample)
            store(PT - 1, 1, y_prompt[(PT - 1) * P:PT * P, :])
            store(PT, 0, y_sample)
            for par in range(2):
                sp.wait_ge(stored[par], 16 * (PT // 2 + 1 - par))

        def tiles_in(t, par):
            return (t - par) * 8 + 16

        @block.scalar
        def _(act):
            for k in range(KT):
                act.wait_ge(w_in_sem[k % 2], 16 * (k // 2 + 1))
                act.activation(w_hi[:, k, :], w_raw[:, k % 2, :], ACT.Copy).then_inc(w_hi_done, 1)

            def prep(t, par):
                wait_some(act, proj, NCH * (t - 1))
                act.wait_ge(mixed_in[par], 2 * tiles_in(t, par))
                act.activation(mt_hi[:, par, 0:NM, :], mix[:, par, :, :], ACT.Copy).then_inc(hi_done, 1)
                act.wait_ge(turned, t + 1)
                act.activation(mt_hi[:, par, NM:2 * NM, :].rearrange("p m t -> p (m t)"), ps_t[:, par, :],
                               ACT.Copy).then_inc(hi_done, 1)

            steps(act, lambda t, par, ahead: ahead(), prep)

        @block.vector
        def _(dve):
            for k in range(KT):
                dve.wait_ge(w_hi_done, k + 1)
                dve.tensor_tensor(w_lo[:, k, :], w_raw[:, k % 2, :], w_hi[:, k, :].bitcast(F32),
                                  ALU.subtract).then_inc(w_lo_done, 1)

            def prep(t, par):
                dve.wait_ge(hi_done, 2 * t + 1)
                dve.tensor_tensor(mt_lo[:, par, 0:NM, :], mix[:, par, :, :], mt_hi[:, par, 0:NM, :].bitcast(F32),
                                  ALU.subtract).then_inc(lo_done, 1)
                dve.wait_ge(hi_done, 2 * t + 2)
                dve.tensor_tensor(mt_lo[:, par, NM:2 * NM, :].rearrange("p m t -> p (m t)"), ps_t[:, par, :],
                                  mt_hi[:, par, NM:2 * NM, :].rearrange("p m t -> p (m t)").bitcast(F32),
                                  ALU.subtract).then_inc(lo_done, 1)

            def step(t, par, ahead):
                ahead()
                dve.wait_ge(x_in[par], tiles_in(t, par))
                dve.wait_ge(stored[par], tiles_in(t, par) - 16)
                for c in range(NCH):
                    dve.wait_ge(proj, NCH * t + c + 1)
                    cols = slice(c * 512, (c + 1) * 512)
                    dve.tensor_tensor(y[:, par, cols], ps[:, par, c, :], x[:, par, cols], ALU.add).then_inc(y_done, 1)

            steps(dve, step, prep)

        @block.tensor
        def _(pe):
            def prep(t, par):
                pe.wait_ge(mixed_in[par], 2 * tiles_in(t, par))
                wait_some(pe, lo_done, 2 * (t - 1))
                for n in range(NM):
                    mm = pe.transpose(ps_t[:, par, n * P:(n + 1) * P], att[:, par, n * P:(n + 1) * P], ident[:, :])
                mm.then_inc(turned, 1)

            def step(t, par, ahead):
                for c in range(NCH):
                    if c == 0:
                        pe.wait_ge(w_lo_done, KT)
                        pe.wait_ge(lo_done, 2 * t + 2)
                        wait_some(pe, y_done, NCH * (t - 1))
                    cols = slice(c * 512, (c + 1) * 512)
                    for n in range(2 * NM):
                        for q, (ma, wa) in enumerate(((mt_hi, w_hi), (mt_hi, w_lo), (mt_lo, w_hi))):
                            mm = pe.matmul(ps[:, par, c, :], ma[:, par, n, :], wa[:, rows_of[n], cols],
                                           start=(n == 0 and q == 0), stop=(n == 2 * NM - 1 and q == 2))
                    mm.then_inc(proj, 1)
                    if c == 0:
                        ahead()

            steps(pe, step, prep)


def encoder_layer(nc, x_prompt, x_sample, cache_k, cache_v, cache_logf, state_pool, state_conv, norm_g, w_in, b_f,
                  q_norm_g, k_norm_g, pool_w, pool_scale, conv_w, w_out,
                  y_prompt, y_sample, new_k, new_v, new_logf, new_pool, new_conv,
                  new_k_s, new_v_s, new_logf_s, new_pool_s, new_conv_s):
    def scratch(name, shape, dt=F32):
        return nc.dram_tensor(f"scratch_{name}", shape, dt, kind="Internal").ap()

    rows = NT * P
    q_all = scratch("q", (rows, DA))
    gate_all = scratch("gate", (rows, DA))
    xt_hi_all = scratch("xt_hi", (rows, D))
    xt_lo_all = scratch("xt_lo", (rows, D))
    f_all = scratch("f", (P, P))
    f_t_all = scratch("f_t", (2 * NB * H, PAST + P))
    mix_all = scratch("mix", (4, P, rows))
    att_all = scratch("att", (rows, DA))
    o_all = scratch("o", (NB * P, HD))

    with ExitStack() as whole:
        ident = whole.enter_context(nc.sbuf_tensor("ident", [P, P], F32))
        with ExitStack() as early:
            tri = early.enter_context(nc.sbuf_tensor("tri", [P, P], F32))
            fl_raw = early.enter_context(nc.sbuf_tensor("fl_raw", [P, NT * H], F32))
            make_constants(nc, ident, tri)
            attention_projection(nc, ident, fl_raw, x_prompt, x_sample, norm_g, w_in, q_norm_g, k_norm_g,
                                 new_k, new_v, new_k_s, new_v_s, q_all, gate_all, xt_hi_all, xt_lo_all)
            forget_sums(nc, ident, tri, fl_raw, f_t_all, b_f, cache_logf, new_logf, new_logf_s, f_all)
        pool_conv(nc, ident, w_in, norm_g, xt_hi_all, xt_lo_all, pool_w, pool_scale, conv_w, state_pool, state_conv,
                  new_pool, new_conv, new_pool_s, new_conv_s, mix_all)
        prompt_attention(nc, ident, q_all, new_k, new_v, gate_all, f_all, att_all)
        sample_attention(nc, ident, q_all, cache_k, cache_v, new_k_s, new_v_s, gate_all, f_t_all, o_all, att_all)
        output_projection(nc, ident, w_out, x_prompt, x_sample, att_all, mix_all, y_prompt, y_sample)


_INS = [("x_prompt", (SEQ, D)), ("x_sample", (NB * NQ, D)), ("cache_k", (NB * PAST, DA)),
        ("cache_v", (NB * PAST, DA)), ("cache_logf", (NB, PAST, H)), ("state_pool", (NB * HIST, DP)),
        ("state_conv", (NB * (CONV_W - 1), DC)), ("norm_g", (D,)), ("w_in", (D, C0 + 4 * DC)), ("b_f", (H,)),
        ("q_norm_g", (HD,)), ("k_norm_g", (HD,)), ("pool_w", (4, 64, 64)), ("pool_scale", (DP,)),
        ("conv_w", (CONV_W, DC)), ("w_out", (D, D))]
_OUTS = [((SEQ, D), (1, SEQ, D)), ((NB * NQ, D), (NB, NQ, D)),
         ((SEQ, DA), (1, 1, SEQ, H, HD)), ((SEQ, DA), (1, 1, SEQ, H, HD)), ((SEQ, H), (1, 1, SEQ, H)),
         ((HIST, DP), (1, 1, HIST, DP)), ((CONV_W - 1, DC), (1, 1, CONV_W - 1, DC)),
         ((NB * NQ, DA), (1, NB, NQ, H, HD)), ((NB * NQ, DA), (1, NB, NQ, H, HD)), ((NB * NQ, H), (1, NB, NQ, H)),
         ((NB * HIST, DP), (1, NB, HIST, DP)), ((NB * (CONV_W - 1), DC), (1, NB, CONV_W - 1, DC))]


def kernel(**inputs):
    import numpy as _np
    import concourse.bacc as _bacc
    from concourse.bass_utils import run_bass_kernel_spmd as _run

    nc = _bacc.Bacc("TRN2", target_bir_lowering=False, num_devices=1)
    arrays, args = {}, []
    for name, shape in _INS:
        arrays[f"in_{name}_dram"] = _np.ascontiguousarray(inputs[name]).reshape(shape)
        args.append(nc.dram_tensor(f"in_{name}_dram", shape, F32, kind="ExternalInput").ap())
    for i, (shape, _) in enumerate(_OUTS):
        args.append(nc.dram_tensor(f"out_{i}_dram", shape, F32, kind="ExternalOutput").ap())
    encoder_layer(nc, *args)
    r = _run(nc, [arrays], core_ids=[0])
    return tuple(_np.asarray(r.results[0][f"out_{i}_dram"]).reshape(shape) for i, (_, shape) in enumerate(_OUTS))
```

```python
from contextlib import ExitStack

import concourse.bass as bass
from concourse import mybir

F32 = mybir.dt.float32
F32R = mybir.dt.float32r
BF16 = mybir.dt.bfloat16
ALU = mybir.AluOpType
ACT = mybir.ActivationFunctionType
AX_X = mybir.AxisListType.X

P = 128
D = 1024
KT = D // P
SEQ = 2048
PT = SEQ // P
NB, NQ, PAST = 8, 16, 1024
H, HD = 8, 64
DA = H * HD
NT = PT + 1
DP = DC = 256
POOL_WINDOWS = (2, 4, 8, 16)
HIST = 15
CONV_W = 3
EPS = 1e-6
Q0 = 2 * DP
CA = 4 * DA + H
C0 = Q0 + CA
MASKED = 1e38


def ds(start, n):
    return bass.ds(start, n)


def wait_some(eng, sem, count):
    if not isinstance(count, int) or count > 0:
        eng.wait_ge(sem, count)


def passed(eng, waited):
    eng.sem_inc(waited, 1)


class Memory:

    def __init__(self, nc, ctx, stage):
        self.nc, self.ctx, self.stage = nc, ctx, stage

    def sbuf(self, name, shape, dt=F32):
        return self.ctx.enter_context(self.nc.sbuf_tensor(f"{self.stage}_{name}", shape, dt))

    def psum(self, name, shape, dt=F32):
        return self.ctx.enter_context(self.nc.psum_tensor(f"{self.stage}_{name}", shape, dt))

    def sem(self, name):
        return self.ctx.enter_context(self.nc.semaphore(f"{self.stage}_{name}"))


def make_constants(nc, ident, tri):
    with ExitStack() as ctx:
        made = Memory(nc, ctx, "const").sem("made")
        block = ctx.enter_context(nc.Block())

        @block.gpsimd
        def _(pool):
            pool.memset(ident[:, :], 0.0).then_inc(made, 1)
            pool.memset(tri[:, :], 1.0).then_inc(made, 1)
            pool.wait_ge(made, 2)
            pool.affine_select(out=ident[:, :], in_=ident[:, :], compare_op=ALU.not_equal, fill=1.0,
                               base=0, pattern=[[-1, P]], channel_multiplier=1).then_inc(made, 1)
            pool.affine_select(out=tri[:, :], in_=tri[:, :], compare_op=ALU.is_ge, fill=0.0,
                               base=0, pattern=[[1, P]], channel_multiplier=-1).then_inc(made, 1)
            pool.wait_ge(made, 4)


def attention_projection(nc, ident, waited, fl_raw, x_prompt, x_sample, norm_g, w_in, q_norm_g, k_norm_g,
                         new_k, new_v, new_k_s, new_v_s, q_all, gate_all, xt_hi_all, xt_lo_all):
    half = (DA + H) // 2
    chunks = [(0, DA), (DA, DA), (2 * DA, DA), (3 * DA, half), (3 * DA + half, half)]
    NCH = len(chunks)
    QC, KC, VC, G0, G1 = range(NCH)
    NRAW = 3
    g_rest = DA - half
    with ExitStack() as ctx:
        m = Memory(nc, ctx, "ap")
        w_hi = m.sbuf("w_hi", [P, KT, CA], F32R)
        w_lo = m.sbuf("w_lo", [P, KT, CA], F32R)
        w_raw = m.sbuf("w_raw", [P, NRAW, CA])
        g_in = m.sbuf("g_in", [P, KT])
        qk_g = m.sbuf("qk_g", [P, 2, HD])
        neg_half = m.sbuf("neg_half", [P, H])
        x = m.sbuf("x", [P, 2, D])
        xt_hi = m.sbuf("xt_hi", [P, 2, D], F32R)
        xt_lo = m.sbuf("xt_lo", [P, 2, D], F32R)
        x_ss = m.sbuf("x_ss", [P, 2])
        x_rstd = m.sbuf("x_rstd", [P, 2])
        squares = m.sbuf("squares", [P, D])
        h_ss = m.sbuf("h_ss", [P, 2, H])
        h_ms = m.sbuf("h_ms", [P, 2, H])
        h_rstd = m.sbuf("h_rstd", [P, 2, H])
        out = m.sbuf("out", [P, 2, 4, DA])
        ps = m.psum("ps", [P, NCH, 512])
        ps_t = m.psum("ps_t", [P, 2, 512])

        w_in_sem = [m.sem(f"w_loaded{i}") for i in range(NRAW)]
        norm_g_in = m.sem("norm_gain_loaded")
        small_in = m.sem("gains_loaded")
        w_hi_done = m.sem("w_hi_done")
        w_lo_done = m.sem("w_lo_done")
        gains = m.sem("gains_scaled")
        x_in = [m.sem(f"x_loaded{i}") for i in range(2)]
        x_sq = m.sem("x_squared")
        x_rs = m.sem("x_rstd_done")
        x_norm = m.sem("x_normed")
        xt_ps = m.sem("x_transposed")
        xt_h = m.sem("xt_hi_done")
        xt_l = m.sem("xt_lo_done")
        proj = m.sem("chunk_projected")
        qk_sq = m.sem("qk_squared")
        qk_ss = m.sem("qk_summed")
        qk_rs = m.sem("qk_rstd_done")
        qk_n = m.sem("qk_scaled")
        qk_out = m.sem("qk_out_done")
        vg_out = m.sem("v_gate_out_done")
        fl_out = m.sem("logits_out")
        stored = [m.sem(f"stored{i}") for i in range(2)]
        xt_stored = [m.sem(f"xt_stored{i}") for i in range(2)]
        block = ctx.enter_context(nc.Block())

        w_v = w_in.rearrange("(k p) c -> p k c", p=P)

        def steps(eng, step, prep):
            step(0, 0, 0, lambda: prep(1, 0, 1))
            step(1, 0, 1, lambda: prep(2, 1, 0))
            with eng.Fori(0, PT // 2 - 1) as i:
                step(i * 2 + 2, i + 1, 0, lambda: prep(i * 2 + 3, i + 1, 1))
                step(i * 2 + 3, i + 1, 1, lambda: prep(i * 2 + 4, i + 2, 0))
            step(PT, PT // 2, 0, lambda: None)

        @block.sync
        def _(sp):
            sp.dma_start(x[:, 0, :], x_prompt[0:P, :]).then_inc(x_in[0], 16)
            sp.dma_start(g_in[:, :], norm_g.rearrange("(k p) -> p k", p=P),
                         allow_slow_non_contiguous=True).then_inc(norm_g_in, 16)
            for k in range(KT):
                if k == NRAW:
                    sp.dma_start(x[:, 1, :], x_prompt[P:2 * P, :]).then_inc(x_in[1], 16)
                if k >= NRAW:
                    sp.wait_ge(w_hi_done, k - NRAW + 1)
                    sp.wait_ge(w_lo_done, k - NRAW + 1)
                sp.dma_start(w_raw[:, k % NRAW, :], w_v[:, k, Q0:Q0 + CA]).then_inc(w_in_sem[k % NRAW], 16)

            def store(t, i, par, rows):
                k_rows, v_rows = rows
                sp.wait_ge(qk_out, 2 * t + 1)
                sp.dma_start(q_all[ds(t * P, P), :], out[:, par, 0, :]).then_inc(stored[par], 16)
                sp.wait_ge(qk_out, 2 * t + 2)
                sp.dma_start(k_rows, out[:, par, 1, :]).then_inc(stored[par], 16)
                sp.wait_ge(vg_out, 3 * t + 1)
                sp.dma_start(v_rows, out[:, par, 2, :]).then_inc(stored[par], 16)
                sp.wait_ge(vg_out, 3 * t + 3)
                sp.dma_start(gate_all[ds(t * P, P), :], out[:, par, 3, :]).then_inc(stored[par], 16)

            def store_xt(t, par):
                sp.wait_ge(xt_l, 2 * t + 2)
                sp.dma_start(xt_hi_all[ds(t * P, P), :],
                             xt_hi[:, par, :].bitcast(F32)).then_inc(xt_stored[par], 16)
                sp.dma_start(xt_lo_all[ds(t * P, P), :],
                             xt_lo[:, par, :].bitcast(F32)).then_inc(xt_stored[par], 16)

            with sp.Fori(0, PT // 2 - 1) as i:
                for par in range(2):
                    t = i * 2 + par
                    store_xt(t, par)
                    sp.wait_ge(xt_ps, 2 * t + 2)
                    sp.dma_start(x[:, par, :], x_prompt[ds((t + 2) * P, P), :]).then_inc(x_in[par], 16)
                    store(t, i, par, (new_k[ds(t * P, P), :], new_v[ds(t * P, P), :]))
            for t in range(PT - 2, NT):
                store_xt(t, t % 2)
                if t == PT - 2:
                    sp.wait_ge(xt_ps, 2 * t + 2)
                    sp.dma_start(x[:, 0, :], x_sample).then_inc(x_in[0], 16)
                rows = ((new_k[t * P:(t + 1) * P, :], new_v[t * P:(t + 1) * P, :]) if t < PT
                        else (new_k_s, new_v_s))
                store(t, t // 2, t % 2, rows)
            for par in range(2):
                tiles = PT // 2 + (1 - par)
                sp.wait_ge(stored[par], 64 * tiles)
                sp.wait_ge(xt_stored[par], 32 * tiles)

        @block.gpsimd
        def _(pool):
            pool.dma_start(qk_g[:, 0, :], q_norm_g.partition_broadcast(P)).then_inc(small_in, 16)
            pool.dma_start(qk_g[:, 1, :], k_norm_g.partition_broadcast(P)).then_inc(small_in, 16)
            pool.memset(neg_half[:, :], -0.5).then_inc(gains, 1)
            pool.wait_ge(gains, 1)

            def prep(t, i, par):
                pool.wait_ge(x_sq, t + 1)
                passed(pool, waited)
                pool.tensor_scalar(x_rstd[:, par:par + 1], x_ss[:, par:par + 1], 1.0 / D, EPS,
                                   ALU.mult, ALU.add).then_inc(x_rs, 1)
                pool.wait_ge(x_rs, 2 * t + 1)
                pool.tensor_tensor(x_rstd[:, par:par + 1], x_rstd[:, par:par + 1], neg_half[:, 0:1],
                                   ALU.pow).then_inc(x_rs, 1)

            prep(0, 0, 0)
            pool.wait_ge(small_in, 32)
            pool.tensor_scalar(qk_g[:, 0, :], qk_g[:, 0, :], -HD ** -0.5, 0.0, ALU.mult, ALU.add).then_inc(gains, 1)
            pool.wait_ge(gains, 2)

            def step(t, i, par, ahead):
                ahead()
                for c in (QC, KC):
                    pool.wait_ge(qk_ss, 2 * t + c + 1)
                    passed(pool, waited)
                    pool.tensor_scalar(h_ms[:, c, :], h_ss[:, c, :], 1.0 / HD, EPS,
                                       ALU.mult, ALU.add).then_inc(qk_rs, 1)
                    pool.wait_ge(qk_rs, 4 * t + 2 * c + 1)
                    pool.tensor_tensor(h_rstd[:, c, :], h_ms[:, c, :], neg_half[:, :], ALU.pow).then_inc(qk_rs, 1)
                for c in (QC, KC):
                    pool.wait_ge(qk_n, 2 * t + c + 1)
                    rows = out[:, par, c, :].rearrange("p (h d) -> p h d", h=H)
                    gain = qk_g[:, c, :].rearrange("p (o d) -> p o d", o=1).to_broadcast([P, H, HD])
                    pool.tensor_tensor(rows, rows, gain, ALU.mult).then_inc(qk_out, 1)

            steps(pool, step, prep)

        @block.scalar
        def _(act):
            def square(t, i, par):
                act.wait_ge(x_in[par], 16 * i + 16)
                act.activation(squares[:, :], x[:, par, :], ACT.Square,
                               accum_out=x_ss[:, par:par + 1]).then_inc(x_sq, 1)

            def split_xt(t, i, par):
                wait_some(act, proj, NCH * (t - 1))
                wait_some(act, xt_stored[par], 32 * i)
                for b in range(2):
                    act.wait_ge(xt_ps, 2 * t + b + 1)
                    act.activation(xt_hi[:, par, b * 512:(b + 1) * 512], ps_t[:, b, :],
                                   ACT.Copy).then_inc(xt_h, 1)

            def prep(t, i, par):
                square(t, i, par)
                split_xt(t, i, par)

            square(0, 0, 0)
            act.wait_ge(norm_g_in, 16)
            for k in range(KT):
                act.wait_ge(w_in_sem[k % NRAW], 16 * (k // NRAW + 1))
                act.activation(w_hi[:, k, :], w_raw[:, k % NRAW, :], ACT.Copy,
                               scale=g_in[:, k:k + 1]).then_inc(w_hi_done, 1)
                if k == 0:
                    split_xt(0, 0, 0)

            def step(t, i, par, ahead):
                ahead()
                wait_some(act, stored[par], 64 * i)
                for c in (QC, KC):
                    act.wait_ge(proj, NCH * t + c + 1)
                    if c == KC:
                        act.wait_ge(qk_ss, 2 * t + 1)
                    act.activation(squares[:, 0:DA], ps[:, c, :], ACT.Square).then_inc(qk_sq, 1)
                act.wait_ge(proj, NCH * t + VC + 1)
                act.activation(out[:, par, 2, :], ps[:, VC, :], ACT.Copy).then_inc(vg_out, 1)
                act.wait_ge(proj, NCH * t + G0 + 1)
                act.activation(out[:, par, 3, 0:half], ps[:, G0, 0:half], ACT.Silu).then_inc(vg_out, 1)
                act.wait_ge(proj, NCH * t + G1 + 1)
                act.activation(out[:, par, 3, half:DA], ps[:, G1, 0:g_rest], ACT.Silu).then_inc(vg_out, 1)
                act.wait_ge(qk_ss, 2 * t + 2)

            steps(act, step, prep)

        @block.vector
        def _(dve):
            def norm_x(t, par):
                dve.wait_ge(x_rs, 2 * t + 2)
                dve.tensor_scalar(x[:, par, :], x[:, par, :], x_rstd[:, par:par + 1], None,
                                  ALU.mult).then_inc(x_norm, 1)

            def split_xt(t, par):
                for b in range(2):
                    dve.wait_ge(xt_h, 2 * t + b + 1)
                    part = slice(b * 512, (b + 1) * 512)
                    dve.tensor_tensor(xt_lo[:, par, part], ps_t[:, b, :], xt_hi[:, par, part].bitcast(F32),
                                      ALU.subtract).then_inc(xt_l, 1)

            def prep(t, i, par):
                norm_x(t, par)
                split_xt(t, par)

            norm_x(0, 0)
            dve.wait_ge(norm_g_in, 16)
            for k in range(KT):
                dve.wait_ge(w_hi_done, k + 1)
                dve.scalar_tensor_tensor(w_lo[:, k, :], w_raw[:, k % NRAW, :], g_in[:, k:k + 1],
                                         w_hi[:, k, :].bitcast(F32), ALU.mult,
                                         ALU.subtract).then_inc(w_lo_done, 1)
                if k == 0:
                    split_xt(0, 0)

            def step(t, i, par, ahead):
                ahead()
                wait_some(dve, stored[par], 64 * i)
                for c in (QC, KC):
                    dve.wait_ge(qk_sq, 2 * t + c + 1)
                    wait_some(dve, qk_rs, 4 * t)
                    dve.tensor_reduce(h_ss[:, c, :], squares[:, 0:DA].rearrange("p (h d) -> p h d", h=H),
                                      AX_X, ALU.add).then_inc(qk_ss, 1)
                for c in (QC, KC):
                    dve.wait_ge(qk_rs, 4 * t + 2 * c + 2)
                    rstd = h_rstd[:, c, :].rearrange("p (h o) -> p h o", o=1).to_broadcast([P, H, HD])
                    dve.tensor_tensor(out[:, par, c, :].rearrange("p (h d) -> p h d", h=H),
                                      ps[:, c, :].rearrange("p (h d) -> p h d", h=H), rstd,
                                      ALU.mult).then_inc(qk_n, 1)
                dve.wait_ge(vg_out, 3 * t + 3)
                dve.tensor_copy(fl_raw[:, ds(t * H, H)], ps[:, G1, g_rest:half]).then_inc(fl_out, 1)

            steps(dve, step, prep)

        @block.tensor
        def _(pe):
            def prep(t, i, par):
                pe.wait_ge(x_norm, t + 1)
                for b in range(2):
                    wait_some(pe, xt_l, 2 * t)
                    for n in range(4):
                        k = 4 * b + n
                        mm = pe.transpose(ps_t[:, b, n * P:(n + 1) * P], x[:, par, k * P:(k + 1) * P], ident[:, :])
                    mm.then_inc(xt_ps, 1)

            def multiply(par, c, k):
                c0, n = chunks[c]
                kk = slice(k * P, (k + 1) * P)
                for j, (xa, wa) in enumerate(((xt_hi, w_hi), (xt_hi, w_lo), (xt_lo, w_hi))):
                    mm = pe.matmul(ps[:, c, 0:n], xa[:, par, kk], wa[:, k, c0:c0 + n],
                                   start=(k == 0 and j == 0), stop=(k == KT - 1 and j == 2))
                return mm

            prep(0, 0, 0)
            pe.wait_ge(xt_l, 2)
            for k in range(KT):
                pe.wait_ge(w_lo_done, k + 1)
                for c in range(NCH):
                    mm = multiply(0, c, k)
                    if k == KT - 1:
                        mm.then_inc(proj, 1)
                if k == KT - 2:
                    prep(1, 0, 1)

            def step(t, i, par, ahead):
                if isinstance(t, int) and t == 0:
                    return
                for c in range(NCH):
                    if c == QC:
                        pe.wait_ge(xt_l, 2 * t + 2)
                    if c in (QC, KC):
                        pe.wait_ge(qk_n, 2 * t)
                    elif c == G1:
                        pe.wait_ge(fl_out, t)
                    else:
                        pe.wait_ge(vg_out, 3 * t)
                    for k in range(KT):
                        mm = multiply(par, c, k)
                    mm.then_inc(proj, 1)
                    if c == QC:
                        ahead()

            steps(pe, step, prep)


def forget_sums(nc, ident, tri, fl_raw, f_t_all, b_f, cache_logf, new_logf, new_logf_s, f_all):
    TS = PAST // P
    with ExitStack() as ctx:
        m = Memory(nc, ctx, "fs")
        bias = m.sbuf("bias", [P, H])
        z = m.sbuf("z", [P, NT, H])
        mag = m.sbuf("mag", [P, NT, H])
        logf = m.sbuf("logf", [P, NT, H])
        streams = m.sbuf("streams", [P, TS + 1, NB * H])
        ones = m.sbuf("ones", [P, P])
        carry = m.sbuf("carry", [P, PT, H])
        total = m.sbuf("total", [P, PT, H])
        carry_s = m.sbuf("carry_s", [P, TS + 1, NB * H])
        total_s = m.sbuf("total_s", [P, TS, NB * H])
        f_p = m.sbuf("f_p", [P, PT * H])
        f_pt = m.sbuf("f_pt", [P, P])
        f_s = m.sbuf("f_s", [P, TS + 1, NB * H])
        split = m.sbuf("split", [P, TS + 1, 2, NB * H], F32R)
        f_t = m.sbuf("f_t", [P, (TS + 1) * P])
        ps_p = m.psum("ps_p", [P, 2, P])
        ps_l = m.psum("ps_l", [P, 2, 512])
        ps_n = m.psum("ps_n", [P, 512])
        ps_f = m.psum("ps_f", [P, P])
        ps_t = m.psum("ps_t", [P, 3, 512])

        loaded = m.sem("bias_loaded")
        cached = m.sem("cache_loaded")
        made = m.sem("zeros_and_ones_made")
        z_done = m.sem("z_done")
        soft = m.sem("softplus_done")
        logf_done = m.sem("logf_done")
        stored = m.sem("logf_and_sums_stored")
        new_in = m.sem("new_logf_loaded")
        sums_p = m.sem("prompt_summed")
        sums_s = m.sem("streams_summed")
        chain = m.sem("vector_chain")
        f_ready = m.sem("f_prompt_ready")
        f_turned = m.sem("f_prompt_transposed")
        f_copied = m.sem("f_prompt_copied")
        split_ready = m.sem("streams_split")
        s_turned = m.sem("streams_transposed")
        t_copied = m.sem("streams_copied")
        block = ctx.enter_context(nc.Block())

        @block.sync
        def _(sp):
            sp.dma_start(bias[:, :], b_f.partition_broadcast(P)).then_inc(loaded, 16)
            for b in range(NB):
                sp.dma_start(streams[:, 0:TS, b * H:(b + 1) * H],
                             cache_logf[b].rearrange("(t p) h -> p t h", p=P)).then_inc(cached, 16)
            sp.wait_ge(logf_done, 1)
            sp.dma_start(new_logf_s, logf[:, PT, :]).then_inc(stored, 16)
            sp.wait_ge(stored, 16)
            sp.wait_ge(made, 1)
            sp.dma_start(streams[0:NQ, TS, :].rearrange("p (b h) -> p b h", b=NB),
                         new_logf_s.rearrange("(b t) h -> t b h", b=NB)).then_inc(new_in, 16)
            sp.dma_start(new_logf.rearrange("(t p) h -> p t h", p=P), logf[:, 0:PT, :]).then_inc(stored, 16)
            sp.wait_ge(f_copied, 1)
            sp.dma_start(f_all, f_pt[:, :]).then_inc(stored, 16)
            sp.wait_ge(t_copied, 2)
            sp.dma_start(f_t_all, f_t[:, :]).then_inc(stored, 16)
            sp.wait_ge(stored, 64)

        @block.gpsimd
        def _(pool):
            pool.memset(streams[:, TS, :], 0.0).then_inc(made, 1)
            pool.memset(ones[:, :], 1.0).then_inc(made, 1)

        @block.scalar
        def _(act):
            act.wait_ge(z_done, 2)
            act.activation(mag[:, :, :], mag[:, :, :], ACT.Exp, scale=-1.0).then_inc(soft, 1)
            act.wait_ge(soft, 1)
            act.activation(mag[:, :, :], mag[:, :, :], ACT.Ln, bias=1.0).then_inc(soft, 1)

        @block.vector
        def _(dve):
            dve.wait_ge(loaded, 16)
            dve.tensor_tensor(z[:, :, :], fl_raw[:, :].rearrange("p (t h) -> p t h", h=H),
                              bias[:, :].rearrange("p (o h) -> p o h", o=1).to_broadcast([P, NT, H]),
                              ALU.add).then_inc(z_done, 1)
            dve.wait_ge(z_done, 1)
            dve.scalar_tensor_tensor(mag[:, :, :], z[:, :, :], -1.0, z[:, :, :], ALU.mult,
                                     ALU.max).then_inc(z_done, 1)
            dve.wait_ge(soft, 2)
            dve.scalar_tensor_tensor(logf[:, :, :], z[:, :, :], 0.0, mag[:, :, :], ALU.min,
                                     ALU.subtract).then_inc(logf_done, 1)
            dve.wait_ge(sums_p, 1)
            dve.memset(carry[:, 0, :], 0.0).then_inc(chain, 1)
            dve.memset(carry_s[:, 0, :], 0.0).then_inc(chain, 1)
            dve.tensor_copy(total[:, :, :], ps_p[:, 1, :].rearrange("p (t h) -> p t h", h=H)).then_inc(chain, 1)
            dve.wait_ge(sums_s, 1)
            dve.tensor_copy(total_s[:, :, :], ps_n[:, :].rearrange("p (t c) -> p t c", t=TS)).then_inc(chain, 1)
            done = 4
            for t in range(1, PT):
                dve.wait_ge(chain, done)
                dve.tensor_tensor(carry[:, t, :], carry[:, t - 1, :], total[:, t - 1, :], ALU.add).then_inc(chain, 1)
                done += 1
                if t <= TS:
                    dve.tensor_tensor(carry_s[:, t, :], carry_s[:, t - 1, :], total_s[:, t - 1, :],
                                      ALU.add).then_inc(chain, 1)
                    done += 1
            dve.wait_ge(chain, done)
            dve.tensor_tensor(f_p[:, :], ps_p[:, 0, :], carry[:, :, :].rearrange("p t h -> p (t h)"),
                              ALU.add).then_inc(f_ready, 1)
            dve.wait_ge(sums_s, 2)
            dve.tensor_tensor(f_s[:, 0:TS, :], ps_l[:, 0, :].rearrange("p (t c) -> p t c", t=TS),
                              carry_s[:, 0:TS, :], ALU.add).then_inc(chain, 1)
            dve.tensor_tensor(f_s[:, TS, :], ps_l[:, 1, 0:NB * H], carry_s[:, TS, :], ALU.add).then_inc(chain, 1)
            dve.wait_ge(chain, done + 2)
            dve.tensor_copy(split[:, :, 0, :], f_s[:, :, :]).then_inc(chain, 1)
            dve.wait_ge(chain, done + 3)
            dve.tensor_tensor(split[:, :, 1, :], f_s[:, :, :], split[:, :, 0, :].bitcast(F32),
                              ALU.subtract).then_inc(split_ready, 1)
            dve.wait_ge(f_turned, 1)
            dve.tensor_copy(f_pt[:, :], ps_f[:, :]).then_inc(f_copied, 1)
            dve.wait_ge(s_turned, 1)
            dve.tensor_copy(f_t[:, 0:8 * P], ps_t[:, 0:2, :].rearrange("p b n -> p (b n)")).then_inc(t_copied, 1)
            dve.tensor_copy(f_t[:, 8 * P:9 * P], ps_t[:, 2, 0:P]).then_inc(t_copied, 1)

        @block.tensor
        def _(pe):
            pe.wait_ge(logf_done, 1)
            pe.wait_ge(made, 2)
            rows = logf[:, 0:PT, :].rearrange("p t h -> p (t h)")
            pe.matmul(ps_p[:, 0, :], tri[:, :], rows, start=True, stop=True)
            pe.matmul(ps_p[:, 1, :], ones[:, :], rows, start=True, stop=True).then_inc(sums_p, 1)
            pe.wait_ge(cached, 16 * NB)
            rows = streams[:, 0:TS, :].rearrange("p t c -> p (t c)")
            pe.matmul(ps_n[:, :], ones[:, :], rows, start=True, stop=True).then_inc(sums_s, 1)
            pe.matmul(ps_l[:, 0, :], tri[:, :], rows, start=True, stop=True)
            pe.wait_ge(new_in, 16)
            pe.matmul(ps_l[:, 1, 0:NB * H], tri[:, :], streams[:, TS, :], start=True, stop=True).then_inc(sums_s, 1)
            pe.wait_ge(f_ready, 1)
            pe.transpose(ps_f[:, :], f_p[:, :], ident[:, :]).then_inc(f_turned, 1)
            pe.wait_ge(split_ready, 1)
            for t in range(TS + 1):
                mm = pe.transpose(ps_t[:, t // 4, (t % 4) * P:(t % 4 + 1) * P],
                                  split[:, t, :, :].rearrange("p s c -> p (s c)").bitcast(F32), ident[:, :])
            mm.then_inc(s_turned, 1)


def pool_conv(nc, ident, w_in, norm_g, xt_hi_all, xt_lo_all, pool_w, pool_scale, conv_w, state_pool, state_conv,
              new_pool, new_conv, new_pool_s, new_conv_s, mix_all):
    T = 3 * P
    NCK = PT // 3
    LAST = 2 * P
    PU, PG, CB, CC, CX, CG = 0, 256, 512, 768, 1024, 1280
    CW = 1536
    groups = [(PU, 0, "act"), (PG, 0, "act"), (PU, 1, "act"), (PG, 1, "act"),
              (CC, 0, "act"), (CX, 0, "dve"), (CB, 0, "dve"), (CG, 0, "act"),
              (CC, 1, "act"), (CX, 1, "dve"), (CB, 1, "dve"), (CG, 1, "act")]
    NG = len(groups)
    NBANK = 6
    NRAW = 3
    N_ACT = sum(g[2] == "act" for g in groups)
    N_DVE = NG - N_ACT

    def read(g, who):
        return sum(x[2] == who for x in groups[:g + 1])

    def at(kind, j):
        return [n for n, g in enumerate(groups) if g[:2] == (kind, j)][0]

    with ExitStack() as ctx:
        m = Memory(nc, ctx, "pc")
        w_hi = m.sbuf("w_hi", [P, KT, CW], F32R)
        w_lo = m.sbuf("w_lo", [P, KT, CW], F32R)
        w_raw = m.sbuf("w_raw", [P, NRAW, CW])
        g_in = m.sbuf("g_in", [P, KT])
        xt_hi = m.sbuf("xt_hi", [P, 2, 3, D], F32R)
        xt_lo = m.sbuf("xt_lo", [P, 2, 3, D], F32R)
        pw = m.sbuf("pw", [P, 2, P])
        scale = m.sbuf("scale", [P, 2])
        cw = m.sbuf("cw", [P, CONV_W, 2])
        inv_w = m.sbuf("inv_w", [P, 2])
        first = m.sbuf("first", [P, 2, 16])
        u = m.sbuf("u", [P, 2, HIST + T])
        s_a = m.sbuf("s_a", [P, HIST + T])
        s_b = m.sbuf("s_b", [P, HIST + T])
        pooled = m.sbuf("pooled", [P, 2, T])
        z = m.sbuf("z", [P, 2, CONV_W - 1 + T])
        c_in = m.sbuf("c_in", [P, 2, T])
        y = m.sbuf("y", [P, T])
        gate = m.sbuf("gate", [P, 2, 2, T])
        mix = m.sbuf("mix", [P, 2, 2, T])
        past_u = m.sbuf("past_u", [NB * HIST, DP])
        past_z = m.sbuf("past_z", [NB * 2, DC])
        us = m.sbuf("us", [P, 2, NB, HIST + NQ])
        zs = m.sbuf("zs", [P, 2, NB, 2 + NQ])
        ends_u = m.sbuf("ends_u", [P, 2, NB * HIST])
        ends_z = m.sbuf("ends_z", [P, 2, NB * 2])
        rows_u = m.sbuf("rows_u", [P, DP])
        rows_us = m.sbuf("rows_us", [P, DP])
        rows_z = m.sbuf("rows_z", [P, DC])
        rows_zs = m.sbuf("rows_zs", [P, DC])
        ps = m.psum("ps", [P, NBANK, 512])
        ps_a = m.psum("ps_a", [P, 2, 512])

        small = m.sem("small_loaded")
        pw_zero = m.sem("pool_w_zeroed")
        pw_in = m.sem("pool_w_loaded")
        w_loaded = [m.sem(f"w_loaded{i}") for i in range(NRAW)]
        w_hi_done = m.sem("w_hi_done")
        w_lo_done = m.sem("w_lo_done")
        tables = m.sem("tables")
        x_in = [m.sem(f"xt_loaded{i}") for i in range(2)]
        proj = m.sem("group_projected")
        act_read = m.sem("act_read")
        dve_read = m.sem("dve_read")
        steps_v = m.sem("vector_steps")
        pool_ready = m.sem("pooled_ready")
        pool_mm = m.sem("pooled_multiplied")
        mixed = m.sem("half_mixed")
        chunk_end = m.sem("chunk_ended")
        mix_stored = m.sem("mix_stored")
        past_t = m.sem("history_transposed")
        ends = m.sem("ends_gathered")
        ends_t = m.sem("ends_transposed")
        ends_c = m.sem("ends_copied")
        states_out = m.sem("states_stored")
        block = ctx.enter_context(nc.Block())

        w_v = w_in.rearrange("(k p) c -> p k c", p=P)
        STEPS = 20

        def chunks(eng, chunk):
            chunk(0, 0, T)
            with eng.Fori(0, (NCK - 1) // 2) as i:
                chunk(i * 2 + 1, 1, T)
                chunk(i * 2 + 2, 0, T)
            chunk(NCK, 1, LAST)

        @block.sync
        def _(sp):
            sp.dma_start(g_in[:, :], norm_g.rearrange("(k p) -> p k", p=P),
                         allow_slow_non_contiguous=True).then_inc(w_loaded[0], 16)
            for k in range(KT):
                if k >= NRAW:
                    sp.wait_ge(w_lo_done, k - NRAW + 1)
                sp.dma_start(w_raw[:, k % NRAW, 0:CB], w_v[:, k, 0:Q0]).then_inc(w_loaded[k % NRAW], 16)
                sp.dma_start(w_raw[:, k % NRAW, CB:CW], w_v[:, k, C0:C0 + CW - CB]).then_inc(w_loaded[k % NRAW], 16)
                if k < 2:
                    cols = slice(k * D // 2, (k + 1) * D // 2)
                    for part, src in ((xt_hi, xt_hi_all), (xt_lo, xt_lo_all)):
                        sp.dma_start(part[:, 0, :, cols].bitcast(F32),
                                     src[0:T, cols].rearrange("(n p) d -> p n d", p=P)).then_inc(x_in[k], 16)
                if k == 2:
                    sp.dma_start(scale[:, :], pool_scale.rearrange("(j p) -> p j", p=P),
                                 allow_slow_non_contiguous=True).then_inc(small, 16)
                    for w in range(CONV_W):
                        sp.dma_start(cw[:, w, :], conv_w[w].rearrange("(j p) -> p j", p=P),
                                     allow_slow_non_contiguous=True).then_inc(small, 16)
                    sp.dma_start(past_u[:, :], state_pool).then_inc(small, 16)
                    sp.dma_start(past_z[:, :], state_conv).then_inc(small, 16)
            sp.wait_ge(pw_zero, 1)
            for g in range(4):
                at_p = slice(64 * (g % 2), 64 * (g % 2) + 64)
                sp.dma_start(pw[at_p, g // 2, at_p], pool_w[g]).then_inc(pw_in, 16)

            def load_x(c, par, tiles):
                for part, src in ((xt_hi, xt_hi_all), (xt_lo, xt_lo_all)):
                    sp.dma_start(part[:, par, 0:tiles, :].bitcast(F32),
                                 src[ds(c * T, tiles * P), :].rearrange("(n p) d -> p n d", p=P)).then_inc(x_in[par], 16)

            def chunk(c, par, n, ahead):
                if ahead:
                    sp.wait_ge(proj, max(NG * c, 1))
                    load_x(c + 1, 1 - par, ahead)
                for half in range(2):
                    for j in range(2):
                        sp.wait_ge(mixed, 4 * c + 2 * half + j + 1)
                        sp.dma_start(mix_all[2 * half + j][:, ds(c * T, n)],
                                     mix[:, half, j, 0:n]).then_inc(mix_stored, 16)

            for c in range(NCK + 1):
                chunk(c, c % 2, T if c < NCK else LAST, 3 if c < NCK - 1 else 2 if c < NCK else 0)
            sp.wait_ge(mix_stored, 16 * 4 * (NCK + 1))
            sp.wait_ge(ends_c, 4)
            sp.dma_start(new_pool, rows_u[0:HIST, :]).then_inc(states_out, 16)
            sp.dma_start(new_conv, rows_z[0:2, :]).then_inc(states_out, 16)
            sp.dma_start(new_pool_s, rows_us[0:NB * HIST, :]).then_inc(states_out, 16)
            sp.dma_start(new_conv_s, rows_zs[0:NB * 2, :]).then_inc(states_out, 16)
            sp.wait_ge(states_out, 64)

        @block.gpsimd
        def _(pool):
            pool.memset(pw[:, :, :], 0.0).then_inc(pw_zero, 1)
            for t in range(16):
                pool.memset(first[:, :, t:t + 1], 1.0 / (t + 1)).then_inc(tables, 1)
            pool.memset(u[:, :, 0:HIST], 0.0).then_inc(tables, 1)
            pool.memset(z[:, :, 0:2], 0.0).then_inc(tables, 1)

        def columns(last):
            return [(False, 0, P), (True, P, NQ)] if last else [(False, 0, T)]

        def cut(buf, streams, start, lo, hi):
            if not streams:
                return buf[:, start + lo:start + hi]
            return buf[:, start:start + NB * NQ].rearrange("p (b t) -> p b t", b=NB)[:, :, lo:hi]

        @block.scalar
        def _(act):
            for k in range(KT):
                act.wait_ge(w_loaded[k % NRAW], 32 * (k // NRAW + 1) + (16 if k % NRAW == 0 else 0))
                act.activation(w_hi[:, k, :], w_raw[:, k % NRAW, :], ACT.Copy,
                               scale=g_in[:, k:k + 1]).then_inc(w_hi_done, 1)

            def chunk(c, par, n):
                act.wait_ge(chunk_end, c + 1)
                for g, (kind, j, who) in enumerate(groups):
                    if who != "act":
                        continue
                    act.wait_ge(proj, NG * c + g + 1)
                    bank = ps[:, g % NBANK, :]
                    parts = columns(n == LAST)
                    for streams, col, t in parts:
                        src = cut(bank, streams, col, 0, t)
                        if kind == PU:
                            dst = us[:, j, :, HIST:HIST + NQ] if streams else u[:, j, HIST:HIST + t]
                        elif kind == CC:
                            dst = cut(c_in[:, j, :], streams, col, 0, t)
                        else:
                            dst = cut(gate[:, 0 if kind == PG else 1, j, :], streams, col, 0, t)
                        done = act.activation(dst, src, ACT.Copy if kind in (PU, CC) else ACT.Silu)
                    done.then_inc(act_read, 1)

            chunks(act, chunk)

        @block.vector
        def _(dve):
            for k in range(KT):
                dve.wait_ge(w_hi_done, k + 1)
                dve.scalar_tensor_tensor(w_lo[:, k, :], w_raw[:, k % NRAW, :], g_in[:, k:k + 1],
                                         w_hi[:, k, :].bitcast(F32), ALU.mult,
                                         ALU.subtract).then_inc(w_lo_done, 1)
            for j in range(2):
                for h in range(2):
                    dve.memset(inv_w[64 * h:64 * h + 64, j:j + 1], 1.0 / POOL_WINDOWS[2 * j + h]).then_inc(tables, 1)
            dve.wait_ge(tables, 4 + 16 + 2)
            dve.wait_ge(small, 16 * (3 + CONV_W))
            for j in range(2):
                dve.tensor_scalar(first[:, j, :], first[:, j, :], inv_w[:, j:j + 1], None, ALU.max).then_inc(steps_v, 1)
            dve.wait_ge(steps_v, 2)
            for j in range(2):
                for h in range(2):
                    half = slice(64 * h, 64 * h + 64)
                    dve.tensor_scalar(first[half, j, :], first[half, j, :], float(POOL_WINDOWS[2 * j + h]), None,
                                      ALU.mult).then_inc(steps_v, 1)
            dve.wait_ge(past_t, 1)
            for j in range(2):
                dve.tensor_copy(us[:, j, :, 0:HIST],
                                ps_a[:, 0, j * 120:(j + 1) * 120].rearrange("p (b t) -> p b t", b=NB))\
                   .then_inc(steps_v, 1)
                dve.tensor_copy(zs[:, j, :, 0:2],
                                ps_a[:, 0, 240 + 16 * j:256 + 16 * j].rearrange("p (b t) -> p b t", b=NB))\
                   .then_inc(steps_v, 1)
            dve.wait_ge(steps_v, 10)
            dve.tensor_copy(y[:, 0:1], scale[:, 0:1]).then_inc(chunk_end, 1)

            def chunk(c, par, n):
                parts = columns(n == LAST)
                count = [0]
                base = 10 + c * STEPS

                def link(ins):
                    count[0] += 1
                    ins.then_inc(steps_v, 1)
                    dve.wait_ge(steps_v, base + count[0])

                for j in range(2):
                    dve.wait_ge(act_read, N_ACT * c + read(at(PU, j), "act"))
                    wait_some(dve, pool_mm, 2 * c)
                    for streams, col, t in parts:
                        e = HIST + t
                        if streams:
                            uu = us[:, j, :, :]
                            a = s_a[:, 0:NB * e].rearrange("p (b e) -> p b e", b=NB)
                            b = s_b[:, 0:NB * e].rearrange("p (b e) -> p b e", b=NB)

                            def w(buf, lo, hi, part=slice(0, P)):
                                return buf[part, :, lo:hi]
                        else:
                            uu, a, b = u[:, j, :], s_a, s_b

                            def w(buf, lo, hi, part=slice(0, P)):
                                return buf[part, lo:hi]
                        link(dve.tensor_tensor(w(a, 1, e), w(uu, 1, e), w(uu, 0, e - 1), ALU.add))
                        link(dve.tensor_tensor(w(b, 3, e), w(a, 3, e), w(a, 1, e - 2), ALU.add))
                        if j == 1:
                            link(dve.tensor_tensor(w(a, 7, e), w(b, 7, e), w(b, 3, e - 4), ALU.add))
                            link(dve.tensor_tensor(w(b, 15, e), w(a, 15, e), w(a, 7, e - 8), ALU.add))
                        for h, sums in ((0, a), (1, b)):
                            half = slice(64 * h, 64 * h + 64)
                            if not streams:
                                link(dve.tensor_tensor(w(sums, HIST, HIST + 16, half), w(sums, HIST, HIST + 16, half),
                                                       first[half, j, :], ALU.mult))
                            dst = pooled[half, j, col:col + (NB * NQ if streams else t)]
                            if streams:
                                dst = dst.rearrange("p (b t) -> p b t", b=NB)
                            link(dve.scalar_tensor_tensor(dst, w(sums, HIST, e, half), inv_w[half, j:j + 1],
                                                          w(uu, HIST, e, half), ALU.mult, ALU.subtract))
                    dve.memset(first[:, j, :], 1.0).then_inc(pool_ready, 1)
                wait_some(dve, mix_stored, 64 * c)
                for j in range(2):
                    dve.wait_ge(pool_mm, 2 * c + j + 1)
                    dve.wait_ge(act_read, N_ACT * c + read(at(PG, j), "act"))
                    dve.scalar_tensor_tensor(mix[:, 0, j, 0:n], ps_a[:, j, 0:n], scale[:, j:j + 1],
                                             gate[:, 0, j, 0:n], ALU.mult, ALU.mult).then_inc(mixed, 1)
                for j in range(2):
                    dve.wait_ge(act_read, N_ACT * c + read(at(CC, j), "act"))
                    dve.wait_ge(proj, NG * c + at(CX, j) + 1)
                    bank = ps[:, at(CX, j) % NBANK, :]
                    for streams, col, t in parts:
                        dst = zs[:, j, :, 2:2 + t] if streams else z[:, j, 2:2 + t]
                        done = dve.tensor_tensor(dst, cut(bank, streams, col, 0, t),
                                                 cut(c_in[:, j, :], streams, col, 0, t), ALU.mult)
                    done.then_inc(dve_read, 1)
                    dve.wait_ge(dve_read, N_DVE * c + read(at(CX, j), "dve"))
                    for streams, col, t in parts:
                        def tap(k):
                            return zs[:, j, :, k:k + t] if streams else z[:, j, k:k + t]

                        yy = cut(y, streams, col, 0, t)
                        link(dve.tensor_scalar(yy, tap(0), cw[:, 0, j:j + 1], None, ALU.mult))
                        for k in (1, 2):
                            link(dve.scalar_tensor_tensor(yy, tap(k), cw[:, k, j:j + 1], yy, ALU.mult, ALU.add))
                    dve.wait_ge(proj, NG * c + at(CB, j) + 1)
                    dve.tensor_tensor(y[:, 0:n], ps[:, at(CB, j) % NBANK, 0:n], y[:, 0:n], ALU.mult).then_inc(dve_read, 1)
                    dve.wait_ge(dve_read, N_DVE * c + read(at(CB, j), "dve"))
                    dve.wait_ge(act_read, N_ACT * c + read(at(CG, j), "act"))
                    dve.tensor_tensor(mix[:, 1, j, 0:n], y[:, 0:n], gate[:, 1, j, 0:n], ALU.mult).then_inc(mixed, 1)
                if n == T:
                    assert count[0] == STEPS, count[0]
                    dve.tensor_copy(u[:, :, 0:HIST], u[:, :, T:T + HIST])
                    dve.tensor_copy(z[:, :, 0:2], z[:, :, T:T + 2]).then_inc(chunk_end, 1)

            chunks(dve, chunk)
            for j in range(2):
                dve.tensor_copy(ends_u[:, j, :].rearrange("p (b t) -> p b t", b=NB),
                                us[:, j, :, NQ:NQ + HIST]).then_inc(ends, 1)
                dve.tensor_copy(ends_z[:, j, :].rearrange("p (b t) -> p b t", b=NB),
                                zs[:, j, :, NQ:NQ + 2]).then_inc(ends, 1)
            for bank, (rows, n) in enumerate(((rows_u, HIST), (rows_us, NB * HIST), (rows_z, 2), (rows_zs, NB * 2))):
                dve.wait_ge(ends_t, bank + 1)
                dve.tensor_copy(rows[0:n, :], ps[0:n, bank, 0:DP]).then_inc(ends_c, 1)

        @block.tensor
        def _(pe):
            def multiply(par, n, g, k):
                kind, j, who = groups[g]
                c0 = kind + j * P
                for q, (wa, xa) in enumerate(((w_hi, xt_hi), (w_hi, xt_lo), (w_lo, xt_hi))):
                    mm = pe.matmul(ps[:, g % NBANK, 0:n], wa[:, k, c0:c0 + P],
                                   xa[:, par, 0:n // P, k * P:(k + 1) * P],
                                   start=(k == 0 and q == 0), stop=(k == KT - 1 and q == 2))
                return mm

            for k in range(KT):
                if k % 4 == 0:
                    pe.wait_ge(x_in[k // 4], 32)
                pe.wait_ge(w_lo_done, k + 1)
                for g in range(NBANK):
                    mm = multiply(0, T, g, k)
                    if k == KT - 1:
                        mm.then_inc(proj, 1)
            pe.wait_ge(small, 16 * (3 + CONV_W))
            for j in range(2):
                pe.transpose(ps_a[:, 0, j * 120:(j + 1) * 120], past_u[:, j * P:(j + 1) * P],
                             ident[0:NB * HIST, 0:NB * HIST])
                mm = pe.transpose(ps_a[:, 0, 240 + 16 * j:256 + 16 * j], past_z[:, j * P:(j + 1) * P],
                                  ident[0:NB * 2, 0:NB * 2])
            mm.then_inc(past_t, 1)
            pe.wait_ge(pw_in, 64)

            def chunk(c, par, n):
                pe.wait_ge(x_in[par], (c - par) * 16 + 32 + 32 * par)
                for g, (kind, j, who) in enumerate(groups):
                    early = isinstance(c, int) and c == 0 and g < NBANK
                    if g >= NBANK:
                        src, cc = g - NBANK, c
                    else:
                        src, cc = g + NG - NBANK, c - 1
                    whose = groups[src][2]
                    sem, per = (act_read, N_ACT) if whose == "act" else (dve_read, N_DVE)
                    wait_some(pe, sem, per * cc + read(src, whose))
                    if not early:
                        for k in range(KT):
                            mm = multiply(par, n, g, k)
                        mm.then_inc(proj, 1)
                    if (kind, j) in ((CX, 0), (CG, 0)):
                        jj = 0 if kind == CX else 1
                        pe.wait_ge(pool_ready, 2 * c + jj + 1)
                        pe.wait_ge(chunk_end, c + 1)
                        pe.matmul(ps_a[:, jj, 0:n], pw[:, jj, :], pooled[:, jj, 0:n], start=True,
                                  stop=True).then_inc(pool_mm, 1)

            chunks(pe, chunk)
            pe.wait_ge(ends, 4)
            for bank, (rows, n) in enumerate(((lambda j: u[:, j, P:P + HIST], HIST), (lambda j: ends_u[:, j, :], NB * HIST),
                                              (lambda j: z[:, j, P:P + 2], 2), (lambda j: ends_z[:, j, :], NB * 2))):
                pe.wait_ge(mixed, 4 * (NCK + 1))
                for j in range(2):
                    mm = pe.transpose(ps[0:n, bank, j * P:(j + 1) * P], rows(j), ident[:, :])
                mm.then_inc(ends_t, 1)


def prompt_attention(nc, ident, waited, q_all, k_all, v_all, gate_all, f_all, att_all):
    NJ = PT
    BLK = 8

    def e_chunks(j):
        return [(b, min(BLK, j + 1 - b)) for b in range(0, j + 1, BLK)]

    def quads(j):
        return [(b, min(4, j + 1 - b)) for b in range(0, j + 1, 4)]

    def e_before(j):
        return sum(len(e_chunks(n)) for n in range(j))

    def q_before(j):
        return sum(len(quads(n)) for n in range(j))

    NE, NQD, NG, NPREP = e_before(NJ), q_before(NJ), NJ // 2, 12
    NSLOT = 3
    PREP0 = 4
    AHEAD = 3
    LAG = 4

    def turn_uses(last):
        uses = []
        for j in range(NJ):
            for n in range(len(quads(j))):
                uses.append(("t", q_before(j) + n))
            if PREP0 <= j < PREP0 + NPREP and not last:
                uses.append(("p", j - PREP0))
        return uses

    def bank(n, length):
        return 1 if n == length - 1 else n % 3

    def former(n, length, length_before):
        mine = bank(n, length)
        for k in range(n - 1, -1, -1):
            if bank(k, length) == mine:
                return True, k
        return False, max(k for k in range(length_before) if bank(k, length_before) == mine)

    USES, LAST_USES = turn_uses(False), turn_uses(True)
    assert NQD % 3 == len(USES) % 3 == len(LAST_USES) % 3 == 1

    with ExitStack() as ctx:
        m = Memory(nc, ctx, "pa")
        ident_r = m.sbuf("ident_r", [P, P], F32R)
        ident_b = m.sbuf("ident_b", [P, P], BF16)
        mask_b = m.sbuf("mask_b", [P, P], BF16)
        q_raw = m.sbuf("q_raw", [P, NJ, HD])
        k_raw = m.sbuf("k_raw", [P, NJ, HD])
        v_raw = m.sbuf("v_raw", [P, NJ, HD])
        g_raw = m.sbuf("g_raw", [P, 2, NJ, HD])
        f_b = m.sbuf("f_b", [P, 2, SEQ])
        split = m.sbuf("split", [P, NSLOT, 4, 2, HD], F32R)
        qs = m.sbuf("qs", [P, 2, SEQ], F32R)
        k_h = m.sbuf("k_h", [P, 2, SEQ], F32R)
        k_l = m.sbuf("k_l", [P, 2, SEQ], F32R)
        vs = m.sbuf("vs", [P, 2, NJ, 2, HD], F32R)
        s_ring = [m.sbuf(f"s_ring{n}", [P, (NJ - AHEAD + n) * P]) for n in range(AHEAD + 1)]
        low = m.sbuf("low", [P, 2, NJ, 4])
        least = m.sbuf("least", [P, 2, NJ])
        rsum = m.sbuf("rsum", [P, 2, NJ, 2])
        rtot = m.sbuf("rtot", [P, 2, 2])
        rinv = m.sbuf("rinv", [P, 2, 2])
        pt_hi = m.sbuf("pt_hi", [P, 2, NJ, 2 * P], F32R)
        pt_lo = m.sbuf("pt_lo", [P, 2, NJ, 2 * P], F32R)
        o_t = m.sbuf("o_t", [P, 2, 2 * P])
        gr = m.sbuf("gr", [P, 2, 2, HD])
        parts = m.sbuf("parts", [P, 2, 2, 2, HD])
        ob = m.sbuf("ob", [P, 2, 2, HD])
        ps_s = m.psum("ps_s", [P, 3, 512])
        ps_t = m.psum("ps_t", [P, 3, 512])
        ps_o = m.psum("ps_o", [P, 2, 512])

        consts = m.sem("consts_made")
        ident_done = m.sem("ident_rounded")
        qkv_in = m.sem("qkv_loaded")
        f_in = [m.sem(f"f_loaded{i}") for i in range(2)]
        g_in = [m.sem(f"gate_loaded{i}") for i in range(2)]
        first_split = m.sem("first_head_split")
        first_step = m.sem("first_head_hi_done")
        first_vh = m.sem("first_v_hi_done")
        first_vs = m.sem("first_v_split")
        vs_done = m.sem("v_split")
        v_hi = m.sem("v_hi_done")
        q_hi = m.sem("q_hi_done")
        split_done = m.sem("prep_split")
        prep_t = m.sem("prep_transposed")
        prep_done = m.sem("prep_copied")
        scored = m.sem("chunk_scored")
        s_taken = m.sem("chunk_with_f_and_min")
        min_done = m.sem("tile_min")
        exp_done = m.sem("chunk_exp")
        added = m.sem("row_sums_added")
        turned = m.sem("p_chunk_transposed")
        hi_done = m.sem("p_hi_done")
        lo_done = m.sem("p_lo_done")
        zeroed = m.sem("corner_zeroed")
        pv_done = m.sem("pair_output")
        o_copied = m.sem("output_copied")
        o_turned = m.sem("output_turned")
        ri_done = m.sem("row_sums_inverted")
        gr_done = m.sem("gates_scaled")
        gated = m.sem("output_gated")
        ob_done = m.sem("output_added")
        stored = [m.sem(f"stored{i}") for i in range(2)]
        block = ctx.enter_context(nc.Block())

        def heads(eng, body):
            body(0, 0, 0, True, False)
            with eng.Fori(0, H // 2 - 1) as i:
                body(i * 2 + 1, i, 1, False, False)
                body(i * 2 + 2, i + 1, 0, False, False)
            body(H - 1, H // 2 - 1, 1, False, True)

        def tile_after(h, par, j, n, last):
            if j + n < NJ:
                return h, par, j + n
            return None if last else (h + 1, 1 - par, j + n - NJ)

        def scores_of(j):
            return s_ring[j % (AHEAD + 1)]

        def pair_ended(h, j, lag, first):
            if j >= lag:
                return h, 0, (j - lag) // 2
            return None if first else (h - 1, 1, (j - lag) // 2 + NG)

        @block.sync
        def _(sp):
            def load_qkv(h):
                for raw, src in ((q_raw, q_all), (k_raw, k_all), (v_raw, v_all)):
                    sp.dma_start(raw[:, :, :], src[0:SEQ, ds(h * HD, HD)].rearrange("(t p) d -> p t d", p=P))\
                      .then_inc(qkv_in, 16)

            def load_f_gate(h, par):
                sp.dma_start(f_b[:, par, :].rearrange("p (t j) -> p t j", j=P),
                             f_all.rearrange("(t h) j -> h t j", h=H)[ds(h, 1), :, :]
                             .rearrange("o t j -> (o t) j").partition_broadcast(P)).then_inc(f_in[par], 16)
                sp.dma_start(g_raw[:, par, :, :],
                             gate_all[0:SEQ, ds(h * HD, HD)].rearrange("(t p) d -> p t d", p=P)).then_inc(g_in[par], 16)

            def store(h, g):
                sp.wait_ge(ob_done, h * NG + g + 1)
                sp.dma_start(att_all[2 * g * P:(2 * g + 2) * P, ds(h * HD, HD)].rearrange("(t p) d -> p t d", p=P),
                             ob[:, g % 2, :, :]).then_inc(stored[g % 2], 16)

            def body(h, i, par, first, last):
                if not last:
                    if first:
                        sp.wait_ge(first_split, NPREP)
                        sp.wait_ge(first_vs, 1)
                    else:
                        sp.wait_ge(split_done, h * NPREP)
                        passed(sp, waited)
                        sp.wait_ge(vs_done, h)
                        passed(sp, waited)
                    load_qkv(h + 1)
                    if not first:
                        sp.wait_ge(s_taken, h * NQD)
                        passed(sp, waited)
                        sp.wait_ge(gr_done, h * NG)
                        passed(sp, waited)
                    load_f_gate(h + 1, 1 - par)
                for j in range(0, NJ, 2):
                    ended = pair_ended(h, j, LAG, first)
                    if ended:
                        store(ended[0], ended[2])

            load_qkv(0)
            load_f_gate(0, 0)
            heads(sp, body)
            for g in (NG - 2, NG - 1):
                store(H - 1, g)
            for p in range(2):
                sp.wait_ge(stored[p], 16 * H * NG // 2)

        @block.gpsimd
        def _(pool):
            pool.memset(ident_b[:, :], 0.0).then_inc(consts, 1)
            pool.memset(mask_b[:, :], 0.0).then_inc(consts, 1)
            pool.wait_ge(consts, 2)
            pool.affine_select(out=ident_b[:, :], in_=ident_b[:, :], compare_op=ALU.not_equal, fill=1.0,
                               base=0, pattern=[[-1, P]], channel_multiplier=1).then_inc(consts, 1)
            pool.affine_select(out=mask_b[:, :], in_=mask_b[:, :], compare_op=ALU.is_ge, fill=MASKED,
                               base=0, pattern=[[-1, P]], channel_multiplier=1).then_inc(consts, 1)

            def high(dst, src):
                return pool.tensor_scalar(dst, src, 1.0, 0.0, ALU.mult, ALU.add)

            def split_step(h, s):
                c, kind = s // 3, s % 3
                tiles = slice(4 * c, 4 * c + 4)
                slot = split[:, s % NSLOT, :, :, :]
                wait_some(pool, prep_t, h * NPREP + s + 1 - NSLOT)
                passed(pool, waited)
                if kind == 0:
                    high(slot[:, :, 0, :], q_raw[:, tiles, :]).then_inc(q_hi, 1)
                    pool.wait_ge(q_hi, (h - 1) * 4 + c + 1)
                    pool.tensor_tensor(slot[:, :, 1, :], q_raw[:, tiles, :], slot[:, :, 0, :].bitcast(F32),
                                       ALU.subtract).then_inc(split_done, 1)
                elif kind == 1:
                    high(slot[:, :, 0, :], k_raw[:, tiles, :])
                    high(slot[:, :, 1, :], k_raw[:, tiles, :]).then_inc(split_done, 1)
                else:
                    k_high = split[:, (s - 1) % NSLOT, :, :, :]
                    pool.wait_ge(split_done, (h - 1) * NPREP + s)
                    for part in range(2):
                        last = pool.tensor_tensor(slot[:, :, part, :], k_raw[:, tiles, :],
                                                  k_high[:, :, part, :].bitcast(F32), ALU.subtract)
                    last.then_inc(split_done, 1)

            def split_v(h, par, hi_sem, lo_sem, n):
                high(vs[:, par, :, 0, :], v_raw[:, :, :]).then_inc(hi_sem, 1)
                pool.wait_ge(hi_sem, n)
                pool.tensor_tensor(vs[:, par, :, 1, :], v_raw[:, :, :], vs[:, par, :, 0, :].bitcast(F32),
                                   ALU.subtract).then_inc(lo_sem, 1)

            def scale_gates(h, i, par, g):
                pool.wait_ge(g_in[par], 16 * i + 16)
                pool.wait_ge(ri_done, h * NG + g + 1)
                wait_some(pool, gated, h * NG + g - 1)
                rows = rinv[:, g % 2, :].rearrange("p (t o) -> p t o", o=1).to_broadcast([P, 2, HD])
                pool.tensor_tensor(gr[:, g % 2, :, :], g_raw[:, par, 2 * g:2 * g + 2, :], rows,
                                   ALU.mult).then_inc(gr_done, 1)

            def add_parts(h, g):
                pool.wait_ge(gated, h * NG + g + 1)
                wait_some(pool, stored[g % 2], h * (16 * NG // 2) + 16 * (g // 2))
                pool.tensor_tensor(ob[:, g % 2, :, :], parts[:, g % 2, 0, :, :], parts[:, g % 2, 1, :, :],
                                   ALU.add).then_inc(ob_done, 1)

            def body(h, i, par, first, last):
                for j in range(NJ):
                    if j % 2 == 0:
                        g = j // 2
                        wait_some(pool, pv_done, h * NG + g - 1)
                        passed(pool, waited)
                        pool.memset(pt_hi[:, g % 2, 2 * g + 1, 0:P].bitcast(F32), 0.0)
                        pool.memset(pt_lo[:, g % 2, 2 * g + 1, 0:P].bitcast(F32), 0.0).then_inc(zeroed, 1)
                        ended = pair_ended(h, j, 2, first)
                        if ended:
                            scale_gates(ended[0], i + par - 1 if ended[1] else i, (par + ended[1]) % 2, ended[2])
                    if not last and PREP0 - 1 <= j < PREP0 - 1 + NPREP:
                        if j == PREP0 - 1:
                            pool.wait_ge(qkv_in, 48 * (h + 2))
                        split_step(h + 1, j - PREP0 + 1)
                    if j == PREP0 + NPREP - 1 and not last:
                        wait_some(pool, pv_done, h * NG)
                        passed(pool, waited)
                        split_v(h + 1, 1 - par, v_hi, vs_done, h + 1)
                    if j % 2 == 1:
                        ended = pair_ended(h, j - 1, LAG, first)
                        if ended:
                            add_parts(ended[0], ended[2])

            pool.wait_ge(qkv_in, 48)
            split_v(0, 0, first_vh, first_vs, 1)
            heads(pool, body)
            scale_gates(H - 1, H // 2 - 1, 1, NG - 1)
            for g in (NG - 2, NG - 1):
                add_parts(H - 1, g)

        @block.scalar
        def _(act):
            def prep_copy(h, par, s, bank):
                c, kind = s // 3, s % 3
                act.wait_ge(prep_t, h * NPREP + s + 1)
                act.activation((qs, k_h, k_l)[kind][:, par, c * 512:(c + 1) * 512], ps_t[:, bank, :],
                               ACT.Copy).then_inc(prep_done, 1)

            def exp_chunk(h, par, j, c):
                if c == 0:
                    act.wait_ge(min_done, h * NJ + j + 1)
                b, nb = e_chunks(j)[c]
                sc = scores_of(j)[:, b * P:(b + nb) * P]
                lowest = low[:, par, j, 0:1] if len(quads(j)) == 1 else least[:, par, j:j + 1]
                act.activation(sc, sc, ACT.Exp, bias=lowest, scale=-1.0,
                               accum_out=rsum[:, par, j, c:c + 1]).then_inc(exp_done, 1)

            def copy_output(h, g):
                act.wait_ge(pv_done, h * NG + g + 1)
                wait_some(act, o_turned, h * NG + g - 1)
                act.activation(o_t[:, g % 2, :], ps_o[:, g % 2, 0:2 * P], ACT.Copy).then_inc(o_copied, 1)

            def body(h, i, par, first, last):
                for j in range(NJ):
                    nxt = tile_after(h, par, j, 1, last)
                    g = j // 2
                    wait_some(act, pv_done, h * NG + g - 1)
                    n_exp = len(e_chunks(nxt[2])) if nxt else 0
                    banks = quads(j)
                    uses = LAST_USES if last else USES
                    for n in range(max(len(banks), 2 * n_exp - 1)):
                        if n < len(banks):
                            b, nb = banks[n]
                            act.wait_ge(turned, h * NQD + q_before(j) + n + 1)
                            act.activation(pt_hi[:, g % 2, b:b + nb, (j % 2) * P:(j % 2 + 1) * P],
                                           ps_t[:, bank(uses.index(("t", q_before(j) + n)), len(uses)), 0:nb * P]
                                           .rearrange("p (b q) -> p b q", q=P), ACT.Copy).then_inc(hi_done, 1)
                        if n % 2 == 0 and n // 2 < n_exp:
                            exp_chunk(*nxt, n // 2)
                        if n == 0 and j % 2 == 0:
                            ended = pair_ended(h, j, LAG, first)
                            if ended:
                                copy_output(ended[0], ended[2])
                    if PREP0 <= j < PREP0 + NPREP and not last:
                        prep_copy(h + 1, 1 - par, j - PREP0, bank(uses.index(("p", j - PREP0)), len(uses)))

            for s in range(NPREP):
                prep_copy(0, 0, s, s % 3)
            exp_chunk(0, 0, 0, 0)
            heads(act, body)
            for g in (NG - 2, NG - 1):
                copy_output(H - 1, g)

        @block.vector
        def _(dve):
            dve.tensor_copy(ident_r[:, :], ident[:, :]).then_inc(ident_done, 1)

            def take_chunk(h, par, j, n):
                b, nb = quads(j)[n]
                at = q_before(j) + n
                dve.wait_ge(scored, h * NQD + at + 1)
                passed(dve, waited)
                done = dve.tensor_tensor_reduce(scores_of(j)[:, b * P:(b + nb) * P],
                                                ps_s[:, bank(at, NQD), 0:nb * P],
                                                f_b[:, par, b * P:(b + nb) * P], 1.0, 3 * MASKED,
                                                ALU.add, ALU.min, low[:, par, j, n:n + 1])
                done.then_inc(s_taken, 1)
                if b + nb < j + 1:
                    return
                dve.wait_ge(s_taken, h * NQD + q_before(j + 1))
                dve.tensor_reduce(least[:, par, j:j + 1], low[:, par, j, 0:n + 1], AX_X, ALU.min).then_inc(min_done, 1)

            def invert_sums(h, par, j):
                dve.wait_ge(exp_done, h * NE + e_before(j + 1))
                wait_some(dve, gr_done, h * NG + j // 2 - 1)
                total = rsum[:, par, j - 1:j + 1, 0]
                if j >= BLK:
                    total = rtot[:, (j // 2) % 2, :]
                    dve.tensor_tensor(total, rsum[:, par, j - 1:j + 1, 0], rsum[:, par, j - 1:j + 1, 1],
                                      ALU.add).then_inc(added, 1)
                    dve.wait_ge(added, h * (NG // 2) + (j - BLK) // 2 + 1)
                dve.reciprocal(rinv[:, (j // 2) % 2, :], total).then_inc(ri_done, 1)

            def gate_output(h, g):
                dve.wait_ge(o_turned, h * NG + g + 1)
                dve.wait_ge(gr_done, h * NG + g + 1)
                wait_some(dve, ob_done, h * NG + g - 1)
                rows = ps_o[:, g % 2, 0:2 * P].rearrange("p (t s d) -> p t s d", t=2, s=2)
                for s in range(2):
                    done = dve.tensor_tensor(parts[:, g % 2, s, :, :], rows[:, :, s, :], gr[:, g % 2, :, :],
                                             ALU.mult)
                done.then_inc(gated, 1)

            def body(h, i, par, first, last):
                for j in range(NJ):
                    nxt = tile_after(h, par, j, AHEAD, last)
                    if nxt and j == NJ - AHEAD:
                        dve.wait_ge(f_in[1 - par], 16 * (i + par) + 16)
                    banks = quads(j)
                    uses = LAST_USES if last else USES
                    n_take = len(quads(nxt[2])) if nxt else 0
                    slots = max(len(banks), n_take)
                    for n in range(slots):
                        if n < n_take:
                            take_chunk(*nxt, n)
                        if n < len(banks):
                            b, nb = banks[n]
                            dve.wait_ge(hi_done, h * NQD + q_before(j) + n + 1)
                            cols = slice((j % 2) * P, (j % 2 + 1) * P)
                            g = j // 2
                            dve.tensor_tensor(pt_lo[:, g % 2, b:b + nb, cols],
                                              ps_t[:, bank(uses.index(("t", q_before(j) + n)), len(uses)), 0:nb * P]
                                              .rearrange("p (b q) -> p b q", q=P),
                                              pt_hi[:, g % 2, b:b + nb, cols].bitcast(F32),
                                              ALU.subtract).then_inc(lo_done, 1)
                        if n == 0 and j % 2 == 0 and (j or not first):
                            invert_sums(*((h, par, j - 1) if j else (h - 1, 1 - par, NJ - 1)))
                        if n == min(1, slots - 1) and j % 2 == 1:
                            ended = pair_ended(h, j - 1, LAG, first)
                            if ended:
                                gate_output(ended[0], ended[2])

            dve.wait_ge(qkv_in, 48)
            for s in range(NPREP):
                c, kind = s // 3, s % 3
                tiles = slice(4 * c, 4 * c + 4)
                slot = split[:, s % NSLOT, :, :, :]
                raw = k_raw if kind else q_raw
                if s >= NSLOT:
                    dve.wait_ge(prep_t, s + 1 - NSLOT)
                if kind < 2:
                    dve.tensor_copy(slot[:, :, 0, :], raw[:, tiles, :]).then_inc(first_step, 1)
                if kind == 0:
                    dve.wait_ge(first_step, 2 * c + 1)
                    dve.tensor_tensor(slot[:, :, 1, :], raw[:, tiles, :], slot[:, :, 0, :].bitcast(F32),
                                      ALU.subtract).then_inc(first_split, 1)
                elif kind == 1:
                    dve.tensor_copy(slot[:, :, 1, :], raw[:, tiles, :]).then_inc(first_split, 1)
                else:
                    k_high = split[:, (s - 1) % NSLOT, :, :, :]
                    dve.wait_ge(first_split, s)
                    dve.wait_ge(first_step, 2 * c + 2)
                    for part in range(2):
                        done = dve.tensor_tensor(slot[:, :, part, :], raw[:, tiles, :],
                                                 k_high[:, :, part, :].bitcast(F32), ALU.subtract)
                    done.then_inc(first_split, 1)
            dve.wait_ge(f_in[0], 16)
            for j in range(AHEAD):
                take_chunk(0, 0, j, 0)
            heads(dve, body)
            invert_sums(H - 1, 1, NJ - 1)
            for g in (NG - 2, NG - 1):
                gate_output(H - 1, g)

        @block.tensor
        def _(pe):
            pe.wait_ge(consts, 4)
            pe.wait_ge(ident_done, 1)

            def free_bank(h, uses, use):
                n = uses.index(use)
                here, k = former(n, len(uses), len(USES))
                kind, at = (uses if here else USES)[k]
                hh = h if here else h - 1
                if isinstance(hh, int) and hh < 0:
                    pass
                elif kind == "t":
                    pe.wait_ge(lo_done, hh * NQD + at + 1)
                else:
                    pe.wait_ge(prep_done, (hh + 1) * NPREP + at + 1)
                return bank(n, len(uses))

            def prep(h, s, at):
                for t in range(4):
                    mm = pe.transpose(ps_t[:, at, t * P:(t + 1) * P].bitcast(F32R),
                                      split[:, s % NSLOT, t, :, :].rearrange("p s d -> p (s d)"), ident_r[:, :])
                mm.then_inc(prep_t, 1)

            def score(h, par, j, n):
                queries = qs[:, par, j * P:(j + 1) * P]
                at = q_before(j) + n
                here, k = former(at, NQD, NQD)
                wait_some(pe, s_taken, (h if here else h - 1) * NQD + k + 1)
                b, nb = quads(j)[n]
                cols = max(nb, 2) * P
                keys = slice(b * P, b * P + cols)
                out = ps_s[:, bank(at, NQD), 0:cols]
                pe.matmul(out, queries, k_h[:, par, keys], start=True, stop=False)
                if b + nb == j + 1:
                    pe.matmul(ps_s[:, bank(at, NQD), (nb - 1) * P:nb * P], ident_b[:, :], mask_b[:, :],
                              start=False, stop=False)
                pe.matmul(out, queries, k_l[:, par, keys], start=False, stop=True).then_inc(scored, 1)

            def turn(h, par, j, n, uses):
                b, nb = quads(j)[n]
                at = q_before(j) + n
                if n % 2 == 0:
                    pe.wait_ge(exp_done, h * NE + e_before(j) + n // 2 + 1)
                to = free_bank(h, uses, ("t", at))
                for k in range(nb):
                    mm = pe.transpose(ps_t[:, to, k * P:(k + 1) * P],
                                      scores_of(j)[:, (b + k) * P:(b + k + 1) * P], ident[:, :])
                mm.then_inc(turned, 1)

            def values(h, par, g, blocks):
                for k in blocks:
                    if k == 0:
                        wait_some(pe, gated, h * NG + g - 1)
                    if k == 0 and g == 0:
                        pe.wait_ge(*((first_vs, 1) if isinstance(h, int) and h == 0 else (vs_done, h)))
                    if k % 4 == 0:
                        pe.wait_ge(lo_done, h * NQD + q_before(2 * g + 1) + k // 4 + 1)
                    if k == 2 * g + 1:
                        pe.wait_ge(zeroed, h * NG + g + 1)
                    v = vs[:, par, k, :, :].rearrange("p s d -> p (s d)")
                    pe.matmul(ps_o[:, g % 2, 0:2 * P], v, pt_hi[:, g % 2, k, :], start=(k == 0), stop=False)
                    mm = pe.matmul(ps_o[:, g % 2, 0:2 * P], v, pt_lo[:, g % 2, k, :], start=False, stop=(k == 2 * g + 1))
                    if k == 2 * g + 1:
                        mm.then_inc(pv_done, 1)

            def turn_output(h, g):
                pe.wait_ge(o_copied, h * NG + g + 1)
                for t in range(2):
                    mm = pe.transpose(ps_o[:, g % 2, t * P:(t + 1) * P], o_t[:, g % 2, t * P:(t + 1) * P], ident[:, :])
                mm.then_inc(o_turned, 1)

            def body(h, i, par, first, last):
                uses = LAST_USES if last else USES
                for j in range(NJ):
                    nxt = tile_after(h, par, j, AHEAD, last)
                    if nxt and j == NJ - AHEAD:
                        pe.wait_ge(prep_done, (h + 1) * NPREP + 3)
                    if j == 0 and not first:
                        pe.wait_ge(prep_done, (h + 1) * NPREP)
                    n_turn = len(quads(j))
                    n_score = len(quads(nxt[2])) if nxt else 0
                    slots = max(n_turn, n_score)
                    ended = pair_ended(h, j - j % 2, 2, first)
                    ours = []
                    if ended:
                        half = ended[2] + 1
                        ours = list(range(half * (j % 2), half * (j % 2 + 1)))
                    for n in range(slots):
                        if n < n_turn:
                            turn(h, par, j, n, uses)
                        if n < n_score:
                            score(*nxt, n)
                        if n == 0 and j % 2 == 1:
                            done = pair_ended(h, j - 1, LAG, first)
                            if done:
                                turn_output(done[0], done[2])
                        if n == slots - 1 and PREP0 <= j < PREP0 + NPREP and not last:
                            pe.wait_ge(split_done, h * NPREP + j - PREP0 + 1)
                            prep(h + 1, j - PREP0, free_bank(h, uses, ("p", j - PREP0)))
                        if ended:
                            values(ended[0], (par + ended[1]) % 2, ended[2],
                                   ours[len(ours) * n // slots:len(ours) * (n + 1) // slots])
            for s in range(NPREP):
                pe.wait_ge(first_split, s + 1)
                if s >= 3:
                    pe.wait_ge(prep_done, s - 2)
                prep(0, s, s % 3)
            pe.wait_ge(prep_done, NPREP)
            for j in range(AHEAD):
                score(0, 0, j, 0)
            heads(pe, body)
            turn_output(H - 1, NG - 2)
            values(H - 1, 1, NG - 1, range(2 * NG))
            pe.wait_ge(gated, H * NG - 1)
            turn_output(H - 1, NG - 1)


def sample_attention(nc, ident, waited, q_all, cache_k, cache_v, new_k, new_v, gate_all, f_t_all, att_all):
    TC = PAST // P
    TILES = [range(0, 3), range(3, 6), range(6, 9)]
    WID = [3 * P, 3 * P, 2 * P + NQ]
    OFF = [0, 3 * P, 6 * P]
    NC_ = len(TILES)
    NP = H // 2
    KB = NC_ * NP
    PB = [range(0, 4), range(4, 8), range(8, 9)]
    ROW = 640
    with ExitStack() as ctx:
        m = Memory(nc, ctx, "sa")
        ident_b = m.sbuf("ident_b", [P, P], BF16)
        mask_b = m.sbuf("mask_b", [P, NQ], BF16)
        later = m.sbuf("later", [P, H, NQ])
        mask_f = m.sbuf("mask_f", [P, NQ])
        own = m.sbuf("own", [P, H])
        sel_f = m.sbuf("sel_f", [P, P])
        sel = m.sbuf("sel", [P, P], F32R)
        q_in = m.sbuf("q_in", [P, DA])
        q_t = m.sbuf("q_t", [P, NP, P])
        qz_hi = m.sbuf("qz_hi", [P, 2, ROW], F32R)
        qz_lo = m.sbuf("qz_lo", [P, 2, ROW], F32R)
        f_s = m.sbuf("f_s", [P, 2, PAST + NQ], F32R)
        k_c = m.sbuf("k_c", [P, 2, TC + 1, DA])
        v_c = m.sbuf("v_c", [P, TC + 1, DA])
        v_hi = m.sbuf("v_hi", [P, 2, TC + 1, DA], F32R)
        v_lo = m.sbuf("v_lo", [P, 2, TC + 1, DA], F32R)
        kt_hi = m.sbuf("kt_hi", [P, NC_, NP, 3 * P], F32R)
        kt_lo = m.sbuf("kt_lo", [P, NC_, NP, 3 * P], F32R)
        low = m.sbuf("low", [P, 2, 4])
        p = m.sbuf("p", [P, 2, PAST + NQ])
        rsum = m.sbuf("rsum", [P, 2, 4])
        own_inv = m.sbuf("own_inv", [P, H])
        p_hi = m.sbuf("p_hi", [P, TC + 1, P], F32R)
        p_lo = m.sbuf("p_lo", [P, TC + 1, P], F32R)
        o_own = m.sbuf("o_own", [P, H, HD])
        o_sum = m.sbuf("o_sum", [P, HD])
        o = m.sbuf("o", [P, 2, HD])
        ps_k = m.psum("ps_k", [P, 2, 512])
        ps_s = m.psum("ps_s", [P, NC_, 512])
        ps_p = m.psum("ps_p", [P, 2, 512])
        ps_o = m.psum("ps_o", [P, 512])

        made = m.sem("consts_made")
        rounded = m.sem("consts_rounded")
        q_loaded = m.sem("q_loaded")
        q_turned = m.sem("q_transposed")
        q_copied = m.sem("q_copied")
        qz_h = m.sem("qz_hi_done")
        qz_done = m.sem("qz_done")
        k_in = [m.sem(f"k_loaded{i}") for i in range(2)]
        v_in = m.sem("v_loaded")
        f_in = [m.sem(f"f_loaded{i}") for i in range(2)]
        k_turned = m.sem("k_bank_transposed")
        kt_h = m.sem("kt_hi_done")
        kt_l = m.sem("kt_lo_done")
        vh_done = m.sem("v_hi_done")
        vn_h = m.sem("v_new_hi_done")
        vn_done = m.sem("v_new_lo_done")
        vl_done = m.sem("v_lo_done")
        scored = m.sem("chunk_scored")
        chunk_min = m.sem("chunk_min")
        row_min = m.sem("row_min")
        exp_done = m.sem("chunk_exp")
        p_turned = m.sem("p_bank_transposed")
        p_h = m.sem("p_hi_done")
        p_l = m.sem("p_lo_done")
        pv_done = m.sem("values_done")
        out_step = m.sem("output_steps")
        o_done = m.sem("o_done")
        o_stored = [m.sem(f"o_stored{i}") for i in range(2)]
        gates_in = m.sem("gates_loaded")
        block = ctx.enter_context(nc.Block())

        def streams(eng, body):
            body(0, 0, False, True)
            body(1, 1, True, True)
            with eng.Fori(0, NB // 2 - 2) as i:
                body(i * 2 + 2, 0, True, True)
                body(i * 2 + 3, 1, True, True)
            body(NB - 2, 0, True, True)
            body(NB - 1, 1, True, False)

        def count(b, par, unit):
            return (b - par) * (unit // 2) + unit

        @block.sync
        def _(sp):
            def by_head(rows, b):
                return rows[ds(SEQ + b * NQ, NQ), :].rearrange("q (h d) -> h q d", d=HD)

            def load_k(b, par):
                sp.dma_start(k_c[:, par, 0:TC, :],
                             cache_k[ds(b * PAST, PAST), :].rearrange("(t p) d -> p t d", p=P)).then_inc(k_in[par], 16)
                sp.dma_start(k_c[0:NQ, par, TC, :], new_k[ds(b * NQ, NQ), :]).then_inc(k_in[par], 16)

            def load_f(b, par):
                for part in range(2):
                    sp.dma_start(f_s[part * H:(part + 1) * H, par, :].bitcast(F32),
                                 f_t_all[ds(b * H + part * NB * H, H), 0:PAST + NQ]).then_inc(f_in[par], 16)

            def load_v(b):
                sp.dma_start(v_c[:, 0:TC, :],
                             cache_v[ds(b * PAST, PAST), :].rearrange("(t p) d -> p t d", p=P)).then_inc(v_in, 16)
                sp.dma_start(v_c[0:NQ, TC, :], new_v[ds(b * NQ, NQ), :]).then_inc(v_in, 16)

            def store(b, par):
                sp.wait_ge(o_done, b + 1)
                sp.dma_start(by_head(att_all, b), o[:, par, :]).then_inc(o_stored[par], 16)

            sp.dma_start(q_in[:, :], q_all[SEQ:SEQ + P, :]).then_inc(q_loaded, 16)
            for b in range(2):
                load_k(b, b)
                if b == 0:
                    sp.wait_ge(made, 8)
                load_f(b, b)
                if b == 0:
                    load_v(0)

            def body(b, par):
                if not isinstance(b, int) or b + 2 < NB:
                    sp.wait_ge(k_turned, (b + 1) * KB)
                    passed(sp, waited)
                    load_k(b + 2, par)
                if not isinstance(b, int) or b + 1 < NB:
                    sp.wait_ge(vn_done, b + 1)
                    passed(sp, waited)
                    sp.wait_ge(vl_done, 4 * (b + 1))
                    passed(sp, waited)
                    load_v(b + 1)
                if not isinstance(b, int) or b + 2 < NB:
                    sp.wait_ge(scored, (b + 1) * NC_)
                    passed(sp, waited)
                    load_f(b + 2, par)
                if not isinstance(b, int) or b > 0:
                    store(b - 1, 1 - par)

            sp.wait_ge(q_turned, 1)
            for b in range(NB):
                sp.dma_start(q_in[:, b * HD:(b + 1) * HD],
                             by_head(gate_all, b)).then_inc(o_stored[b] if b < 2 else gates_in, 16)
            body(0, 0)
            with sp.Fori(0, (NB - 4) // 2) as i:
                body(i * 2 + 1, 1)
                body(i * 2 + 2, 0)
            for b in range(NB - 3, NB):
                body(b, b % 2)
            store(NB - 1, 1)
            for par in range(2):
                sp.wait_ge(o_stored[par], 16 * (NB // 2 + 1))

        @block.gpsimd
        def _(pool):
            pool.memset(ident_b[:, :], 0.0).then_inc(made, 1)
            pool.memset(own[:, :], 1.0).then_inc(made, 1)
            pool.memset(later[:, :, :], 0.0).then_inc(made, 1)
            pool.memset(sel_f[:, :], 0.0).then_inc(made, 1)
            pool.memset(qz_hi[:, :, :].bitcast(F32), 0.0).then_inc(made, 1)
            pool.memset(qz_lo[:, :, :].bitcast(F32), 0.0).then_inc(made, 1)
            pool.memset(f_s[:, 0, :].bitcast(F32), 0.0).then_inc(made, 1)
            pool.memset(f_s[:, 1, :].bitcast(F32), 0.0).then_inc(made, 1)
            pool.wait_ge(made, 8)
            pool.affine_select(out=ident_b[:, :], in_=ident_b[:, :], compare_op=ALU.not_equal, fill=1.0,
                               base=0, pattern=[[-1, P]], channel_multiplier=1).then_inc(made, 1)
            pool.affine_select(out=own[:, :], in_=own[:, :], compare_op=ALU.is_ge, fill=0.0,
                               base=0, pattern=[[-NQ, H]], channel_multiplier=1).then_inc(made, 1)
            pool.affine_select(out=later[:, :, :], in_=later[:, :, :], compare_op=ALU.is_ge, fill=MASKED,
                               base=0, pattern=[[-NQ, H], [-1, NQ]], channel_multiplier=1).then_inc(made, 1)
            rows = sel_f[:, :].rearrange("p (h q) -> p h q", h=H)
            pool.affine_select(out=rows, in_=rows, compare_op=ALU.not_equal, fill=1.0,
                               base=0, pattern=[[-1, H], [0, NQ]], channel_multiplier=1).then_inc(made, 1)
            pool.wait_ge(made, 12)
            pool.affine_select(out=own[:, :], in_=own[:, :], compare_op=ALU.is_ge, fill=0.0,
                               base=NQ - 1, pattern=[[NQ, H]], channel_multiplier=-1).then_inc(made, 1)
            pool.affine_select(out=rows, in_=rows, compare_op=ALU.not_equal, fill=1.0,
                               base=-H, pattern=[[-1, H], [0, NQ]], channel_multiplier=1).then_inc(made, 1)

            def lay_q(b, par):
                wait_some(pool, scored, NC_ * (b - 1))
                for half in range(2):
                    rows = slice(64 * half, 64 * half + 64)
                    cols = slice(NQ * half, NQ * half + NQ)
                    src = q_t[rows, :, ds(b * NQ, NQ)]
                    hi = qz_hi[rows, par, :].rearrange("p (a c) -> p a c", c=160)[:, :, cols]
                    lo = qz_lo[rows, par, :].rearrange("p (a c) -> p a c", c=160)[:, :, cols]
                    pool.tensor_copy(hi, src).then_inc(qz_h, 1)
                    pool.wait_ge(qz_h, 2 * b + half + 1)
                    passed(pool, waited)
                    pool.tensor_tensor(lo, src, hi.bitcast(F32), ALU.subtract).then_inc(qz_done, 1)
                    pool.wait_ge(qz_done, 2 * b + half + 1)

            def split_v_hi(b, par):
                pool.wait_ge(v_in, 32 * (b + 1))
                wait_some(pool, pv_done, b - 1)
                passed(pool, waited)
                pool.tensor_scalar(v_hi[:, par, 0:TC, :], v_c[:, 0:TC, :], 1.0, 0.0, ALU.mult,
                                   ALU.add).then_inc(vh_done, 1)
                pool.wait_ge(vh_done, b + 1)
                passed(pool, waited)
                pool.tensor_scalar(v_hi[0:NQ, par, TC, :], v_c[0:NQ, TC, :], 1.0, 0.0, ALU.mult,
                                   ALU.add).then_inc(vn_h, 1)
                pool.wait_ge(vn_h, b + 1)
                pool.tensor_tensor(v_lo[0:NQ, par, TC, :], v_c[0:NQ, TC, :],
                                   v_hi[0:NQ, par, TC, :].bitcast(F32), ALU.subtract).then_inc(vn_done, 1)
                pool.wait_ge(vn_done, b + 1)

            pool.wait_ge(q_copied, 1)
            lay_q(0, 0)

            def body(b, par, before, after):
                if after:
                    lay_q(b + 1, 1 - par)
                split_v_hi(b, par)

            streams(pool, body)

        def k_banks(b, c):
            return [(b * KB + c * NP + n, n) for n in range(NP)]

        @block.scalar
        def _(act):
            def high_k(b, c):
                for at, n in k_banks(b, c):
                    act.wait_ge(k_turned, at + 1)
                    act.activation(kt_hi[:, c, n, 0:WID[c]], ps_k[:, n % 2, 0:WID[c]], ACT.Copy).then_inc(kt_h, 1)

            def high_p(b):
                for n, tiles in enumerate(PB):
                    act.wait_ge(p_turned, b * 3 + n + 1)
                    rows = P if n < 2 else NQ
                    src = ps_p[0:rows, n % 2, 0:len(tiles) * P].rearrange("p (t r) -> p t r", r=P)
                    act.activation(p_hi[0:rows, tiles[0]:tiles[-1] + 1, :], src, ACT.Copy).then_inc(p_h, 1)

            def exps(b, par):
                act.wait_ge(row_min, b + 1)
                for c in range(NC_):
                    act.activation(p[:, par, OFF[c]:OFF[c] + WID[c]], ps_s[:, c, 0:WID[c]], ACT.Exp,
                                   scale=-1.0, bias=low[:, par, 3:4],
                                   accum_out=rsum[:, par, c:c + 1]).then_inc(exp_done, 1)

            high_k(0, 0)
            high_k(0, 1)

            def body(b, par, before, after):
                high_k(b, 2)
                if after:
                    high_k(b + 1, 0)
                    high_k(b + 1, 1)
                if before:
                    high_p(b - 1)
                exps(b, par)

            streams(act, body)
            high_p(NB - 1)

        @block.vector
        def _(dve):
            dve.wait_ge(made, 14)
            dve.tensor_tensor(later[:, :, :], later[:, :, :],
                              own[:, :].rearrange("p (h o) -> p h o", o=1).to_broadcast([P, H, NQ]),
                              ALU.mult).then_inc(rounded, 1)
            dve.wait_ge(rounded, 1)
            dve.tensor_reduce(mask_f[:, :], later[:, :, :].rearrange("p h q -> p q h"), AX_X,
                              ALU.add).then_inc(rounded, 1)
            dve.wait_ge(rounded, 2)
            dve.tensor_copy(mask_b[:, :], mask_f[:, :]).then_inc(rounded, 1)
            dve.tensor_copy(sel[:, :], sel_f[:, :]).then_inc(rounded, 1)
            dve.wait_ge(q_turned, 1)
            dve.tensor_copy(q_t[:, :, :].rearrange("p a r -> p (a r)"), ps_o[:, :]).then_inc(q_copied, 1)

            def low_k(b, c):
                for at, n in k_banks(b, c):
                    dve.wait_ge(kt_h, at + 1)
                    dve.tensor_tensor(kt_lo[:, c, n, 0:WID[c]], ps_k[:, n % 2, 0:WID[c]],
                                      kt_hi[:, c, n, 0:WID[c]].bitcast(F32), ALU.subtract).then_inc(kt_l, 1)

            def low_v(b, par, quarter):
                if quarter == 0:
                    dve.wait_ge(vh_done, b + 1)
                tiles = slice(quarter * TC // 4, (quarter + 1) * TC // 4)
                dve.tensor_tensor(v_lo[:, par, tiles, :], v_c[:, tiles, :], v_hi[:, par, tiles, :].bitcast(F32),
                                  ALU.subtract).then_inc(vl_done, 1)

            def low_p(b):
                for n, tiles in enumerate(PB):
                    dve.wait_ge(p_h, b * 3 + n + 1)
                    rows = P if n < 2 else NQ
                    tt = slice(tiles[0], tiles[-1] + 1)
                    src = ps_p[0:rows, n % 2, 0:len(tiles) * P].rearrange("p (t r) -> p t r", r=P)
                    dve.tensor_tensor(p_lo[0:rows, tt, :], src, p_hi[0:rows, tt, :].bitcast(F32),
                                      ALU.subtract).then_inc(p_l, 1)

            def minima(b, par, c):
                dve.wait_ge(scored, b * NC_ + c + 1)
                dve.tensor_reduce(low[:, par, c:c + 1], ps_s[:, c, 0:WID[c]], AX_X, ALU.min).then_inc(chunk_min, 1)

            def output(b, par):
                dve.wait_ge(exp_done, b * NC_ + NC_)
                dve.tensor_reduce(rsum[:, par, 3:4], rsum[:, par, 0:3], AX_X, ALU.add).then_inc(out_step, 1)
                dve.wait_ge(out_step, b * 5 + 1)
                dve.reciprocal(rsum[:, par, 3:4], rsum[:, par, 3:4]).then_inc(out_step, 1)
                dve.wait_ge(out_step, b * 5 + 2)
                dve.tensor_scalar(own_inv[:, :], own[:, :], rsum[:, par, 3:4], None, ALU.mult).then_inc(out_step, 1)
                dve.wait_ge(out_step, b * 5 + 3)
                dve.wait_ge(pv_done, b + 1)
                dve.tensor_tensor(o_own[:, :, :], ps_o[:, :].rearrange("p (h d) -> p h d", h=H),
                                  own_inv[:, :].rearrange("p (h o) -> p h o", o=1).to_broadcast([P, H, HD]),
                                  ALU.mult).then_inc(out_step, 1)
                dve.wait_ge(out_step, b * 5 + 4)
                dve.tensor_reduce(o_sum[:, :], o_own[:, :, :].rearrange("p h d -> p d h"), AX_X,
                                  ALU.add).then_inc(out_step, 1)
                dve.wait_ge(out_step, b * 5 + 5)
                dve.wait_ge(o_stored[par], count(b, par, 16))
                dve.tensor_tensor(o[:, par, :], o_sum[:, :], q_in[:, ds(b * HD, HD)],
                                  ALU.mult).then_inc(o_done, 1)

            low_k(0, 0)
            low_k(0, 1)

            def body(b, par, before, after):
                low_k(b, 2)
                minima(b, par, 0)
                if after:
                    low_k(b + 1, 0)
                minima(b, par, 1)
                if after:
                    low_k(b + 1, 1)
                minima(b, par, 2)
                dve.wait_ge(chunk_min, b * NC_ + NC_)
                dve.tensor_reduce(low[:, par, 3:4], low[:, par, 0:3], AX_X, ALU.min).then_inc(row_min, 1)
                if before:
                    low_p(b - 1)
                for quarter in range(4):
                    low_v(b, par, quarter)
                if before:
                    output(b - 1, 1 - par)
                else:
                    dve.wait_ge(gates_in, 16 * (NB - 2))

            streams(dve, body)
            low_p(NB - 1)
            output(NB - 1, 1)

        @block.tensor
        def _(pe):
            pe.wait_ge(q_loaded, 16)
            for n in range(NP):
                mm = pe.transpose(ps_o[:, n * P:(n + 1) * P], q_in[:, n * P:(n + 1) * P], ident[:, :])
            mm.then_inc(q_turned, 1)

            def turn_k(b, par, c, n):
                if n == 0 and c == 0:
                    pe.wait_ge(k_in[par], count(b, par, 32))
                wait_some(pe, kt_l, b * KB + c * NP + n - 1)
                for at, t in enumerate(TILES[c]):
                    rows = P if t < TC else NQ
                    mm = pe.transpose(ps_k[:, n % 2, at * P:at * P + rows],
                                      k_c[0:rows, par, t, n * P:(n + 1) * P], ident[0:rows, 0:rows])
                mm.then_inc(k_turned, 1)

            def score(b, par, c, ahead):
                out = ps_s[:, c, 0:WID[c]]
                if c == 0:
                    pe.wait_ge(f_in[par], count(b, par, 32))
                    pe.wait_ge(qz_done, 2 * b + 2)
                wait_some(pe, exp_done, NC_ * b - (NC_ - 1 - c))
                pe.matmul(out, sel[:, :], f_s[:, par, OFF[c]:OFF[c] + WID[c]], start=True, stop=False)
                if c == NC_ - 1:
                    pe.matmul(ps_s[:, c, 2 * P:2 * P + NQ], ident_b[:, :], mask_b[:, :], start=False, stop=False)
                for n in range(NP):
                    pe.wait_ge(kt_l, b * KB + c * NP + n + 1)
                    z = slice(n * P, (n + 1) * P)
                    for q, (qa, ka) in enumerate(((qz_hi, kt_hi), (qz_lo, kt_hi), (qz_hi, kt_lo))):
                        mm = pe.matmul(out, qa[:, par, z], ka[:, c, n, 0:WID[c]], start=False,
                                       stop=(n == NP - 1 and q == 2))
                    if n == NP - 1:
                        mm.then_inc(scored, 1)
                    ahead(n)

            def turn_p(b, par):
                pe.wait_ge(exp_done, b * NC_ + NC_)
                for n, tiles in enumerate(PB):
                    wait_some(pe, p_l, b * 3 + max(n - 1, 0))
                    for at, t in enumerate(tiles):
                        w = P if t < TC else NQ
                        mm = pe.transpose(ps_p[0:w, n % 2, at * P:(at + 1) * P], p[:, par, t * P:t * P + w], ident[:, :])
                    mm.then_inc(p_turned, 1)

            def values(b, par):
                wait_some(pe, o_done, b)
                pe.wait_ge(vl_done, 4 * b + 4)
                pe.wait_ge(vn_done, b + 1)
                for n, tiles in enumerate(PB):
                    pe.wait_ge(p_l, b * 3 + n + 1)
                    for t in tiles:
                        rows = P if t < TC else NQ
                        for q, (pa, va) in enumerate(((p_hi, v_hi), (p_lo, v_hi), (p_hi, v_lo))):
                            mm = pe.matmul(ps_o[:, :], pa[0:rows, t, :], va[0:rows, par, t, :],
                                           start=(t == 0 and q == 0), stop=(t == TC and q == 2))
                mm.then_inc(pv_done, 1)

            for c in range(2):
                for n in range(NP):
                    turn_k(0, 0, c, n)
            pe.wait_ge(rounded, 4)
            pe.wait_ge(made, 14)
            pe.wait_ge(q_copied, 1)

            def body(b, par, before, after):
                score(b, par, 0, lambda n: turn_k(b, par, 2, n))
                score(b, par, 1, (lambda n: turn_k(b + 1, 1 - par, 0, n)) if after else (lambda n: None))
                score(b, par, 2, (lambda n: turn_k(b + 1, 1 - par, 1, n)) if after else (lambda n: None))
                if before:
                    turn_p(b - 1, 1 - par)
                    values(b - 1, 1 - par)

            streams(pe, body)
            turn_p(NB - 1, 1)
            values(NB - 1, 1)


def output_projection(nc, ident, w_out, x_prompt, x_sample, att_all, mix_all, y_prompt, y_sample):
    NM = 4
    rows_of = [0, 1, 6, 7, 2, 3, 4, 5]
    NCH = D // 512
    with ExitStack() as ctx:
        m = Memory(nc, ctx, "op")
        w_hi = m.sbuf("w_hi", [P, KT, D], F32R)
        w_lo = m.sbuf("w_lo", [P, KT, D], F32R)
        w_raw = m.sbuf("w_raw", [P, 2, D])
        x = m.sbuf("x", [P, 2, D])
        att = m.sbuf("att", [P, 2, DA])
        mix = m.sbuf("mix", [P, 2, NM, P])
        mt_hi = m.sbuf("mt_hi", [P, 2, 2 * NM, P], F32R)
        mt_lo = m.sbuf("mt_lo", [P, 2, 2 * NM, P], F32R)
        y = m.sbuf("y", [P, 2, D])
        ps = m.psum("ps", [P, 2, NCH, 512])
        ps_t = m.psum("ps_t", [P, 2, 512])

        w_in_sem = [m.sem(f"w_loaded{i}") for i in range(2)]
        w_hi_done = m.sem("w_hi_done")
        w_lo_done = m.sem("w_lo_done")
        x_in = [m.sem(f"x_loaded{i}") for i in range(2)]
        mixed_in = [m.sem(f"mixed_loaded{i}") for i in range(2)]
        turned = m.sem("attention_transposed")
        hi_done = m.sem("hi_done")
        lo_done = m.sem("lo_done")
        proj = m.sem("chunk_projected")
        y_done = m.sem("y_done")
        stored = [m.sem(f"stored{i}") for i in range(2)]
        block = ctx.enter_context(nc.Block())

        def steps(eng, step, prep):
            step(0, 0, lambda: prep(1, 1))
            step(1, 1, lambda: prep(2, 0))
            with eng.Fori(0, PT // 2 - 1) as i:
                step(i * 2 + 2, 0, lambda: prep(i * 2 + 3, 1))
                step(i * 2 + 3, 1, lambda: prep(i * 2 + 4, 0))
            step(PT, 0, lambda: None)

        @block.sync
        def _(sp):
            def load(t, par, x_rows):
                wait_some(sp, lo_done, 2 * (t - 1))
                sp.dma_start(att[:, par, :], att_all[ds(t * P, P), :]).then_inc(mixed_in[par], 16)
                sp.dma_start(mix[:, par, :, :],
                             mix_all.rearrange("m p t -> p m t")[:, :, ds(t * P, P)]).then_inc(mixed_in[par], 16)
                wait_some(sp, y_done, NCH * (t - 1))
                sp.dma_start(x[:, par, :], x_rows).then_inc(x_in[par], 16)

            def store(t, par, rows):
                sp.wait_ge(y_done, NCH * t + NCH)
                sp.dma_start(rows, y[:, par, :]).then_inc(stored[par], 16)

            load(0, 0, x_prompt[0:P, :])
            for n, k in enumerate(rows_of):
                if n == 4:
                    load(1, 1, x_prompt[P:2 * P, :])
                if n >= 2:
                    sp.wait_ge(w_lo_done, n - 1)
                sp.dma_start(w_raw[:, n % 2, :], w_out[k * P:(k + 1) * P, :]).then_inc(w_in_sem[n % 2], 16)
            with sp.Fori(0, PT // 2 - 1) as i:
                for par in range(2):
                    t = i * 2 + par
                    store(t, par, y_prompt[ds(t * P, P), :])
                    load(t + 2, par, x_prompt[ds((t + 2) * P, P), :])
            store(PT - 2, 0, y_prompt[(PT - 2) * P:(PT - 1) * P, :])
            load(PT, 0, x_sample)
            store(PT - 1, 1, y_prompt[(PT - 1) * P:PT * P, :])
            store(PT, 0, y_sample)
            for par in range(2):
                sp.wait_ge(stored[par], 16 * (PT // 2 + 1 - par))

        def tiles_in(t, par):
            return (t - par) * 8 + 16

        @block.scalar
        def _(act):
            def prep(t, par):
                wait_some(act, proj, NCH * (t - 1))
                act.wait_ge(mixed_in[par], 2 * tiles_in(t, par))
                act.activation(mt_hi[:, par, 0:NM, :], mix[:, par, :, :], ACT.Copy).then_inc(hi_done, 1)
                act.wait_ge(turned, t + 1)
                act.activation(mt_hi[:, par, NM:2 * NM, :].rearrange("p m t -> p (m t)"), ps_t[:, par, :],
                               ACT.Copy).then_inc(hi_done, 1)

            for k in range(KT):
                act.wait_ge(w_in_sem[k % 2], 16 * (k // 2 + 1))
                act.activation(w_hi[:, k, :], w_raw[:, k % 2, :], ACT.Copy).then_inc(w_hi_done, 1)
                if k == 0:
                    prep(0, 0)

            steps(act, lambda t, par, ahead: ahead(), prep)

        @block.vector
        def _(dve):
            def prep(t, par):
                dve.wait_ge(hi_done, 2 * t + 1)
                dve.tensor_tensor(mt_lo[:, par, 0:NM, :], mix[:, par, :, :], mt_hi[:, par, 0:NM, :].bitcast(F32),
                                  ALU.subtract).then_inc(lo_done, 1)
                dve.wait_ge(hi_done, 2 * t + 2)
                dve.tensor_tensor(mt_lo[:, par, NM:2 * NM, :].rearrange("p m t -> p (m t)"), ps_t[:, par, :],
                                  mt_hi[:, par, NM:2 * NM, :].rearrange("p m t -> p (m t)").bitcast(F32),
                                  ALU.subtract).then_inc(lo_done, 1)

            def step(t, par, ahead):
                ahead()
                dve.wait_ge(x_in[par], tiles_in(t, par))
                wait_some(dve, stored[par], tiles_in(t, par) - 16)
                for c in range(NCH):
                    dve.wait_ge(proj, NCH * t + c + 1)
                    cols = slice(c * 512, (c + 1) * 512)
                    dve.tensor_tensor(y[:, par, cols], ps[:, par, c, :], x[:, par, cols], ALU.add).then_inc(y_done, 1)

            for k in range(KT):
                dve.wait_ge(w_hi_done, k + 1)
                dve.tensor_tensor(w_lo[:, k, :], w_raw[:, k % 2, :], w_hi[:, k, :].bitcast(F32),
                                  ALU.subtract).then_inc(w_lo_done, 1)
                if k == 0:
                    prep(0, 0)

            steps(dve, step, prep)

        @block.tensor
        def _(pe):
            def prep(t, par):
                pe.wait_ge(mixed_in[par], 2 * tiles_in(t, par))
                wait_some(pe, lo_done, 2 * (t - 1))
                for n in range(NM):
                    mm = pe.transpose(ps_t[:, par, n * P:(n + 1) * P], att[:, par, n * P:(n + 1) * P], ident[:, :])
                mm.then_inc(turned, 1)

            def multiply(par, c, n):
                for q, (ma, wa) in enumerate(((mt_hi, w_hi), (mt_hi, w_lo), (mt_lo, w_hi))):
                    mm = pe.matmul(ps[:, par, c, :], ma[:, par, n, :], wa[:, n, c * 512:(c + 1) * 512],
                                   start=(n == 0 and q == 0), stop=(n == 2 * NM - 1 and q == 2))
                return mm

            prep(0, 0)
            pe.wait_ge(lo_done, 1)
            for n in range(2 * NM):
                if n == NM:
                    pe.wait_ge(lo_done, 2)
                pe.wait_ge(w_lo_done, n + 1)
                for c in range(NCH):
                    mm = multiply(0, c, n)
                    if n == 2 * NM - 1:
                        mm.then_inc(proj, 1)
                if n == NM:
                    prep(1, 1)

            def step(t, par, ahead):
                if isinstance(t, int) and t == 0:
                    return
                for c in range(NCH):
                    if c == 0:
                        pe.wait_ge(lo_done, 2 * t + 2)
                        wait_some(pe, y_done, NCH * (t - 1))
                    for n in range(2 * NM):
                        mm = multiply(par, c, n)
                    mm.then_inc(proj, 1)
                    if c == 0:
                        ahead()

            steps(pe, step, prep)


def encoder_layer(nc, x_prompt, x_sample, cache_k, cache_v, cache_logf, state_pool, state_conv, norm_g, w_in, b_f,
                  q_norm_g, k_norm_g, pool_w, pool_scale, conv_w, w_out,
                  y_prompt, y_sample, new_k, new_v, new_logf, new_pool, new_conv,
                  new_k_s, new_v_s, new_logf_s, new_pool_s, new_conv_s):
    def scratch(name, shape, dt=F32):
        return nc.dram_tensor(f"scratch_{name}", shape, dt, kind="Internal").ap()

    rows = NT * P
    q_all = scratch("q", (rows, DA))
    gate_all = scratch("gate", (rows, DA))
    xt_hi_all = scratch("xt_hi", (rows, D))
    xt_lo_all = scratch("xt_lo", (rows, D))
    f_all = scratch("f", (P, P))
    f_t_all = scratch("f_t", (2 * NB * H, PAST + P))
    mix_all = scratch("mix", (4, P, rows))
    att_all = scratch("att", (rows, DA))

    with ExitStack() as whole:
        ident = whole.enter_context(nc.sbuf_tensor("ident", [P, P], F32))
        waited = whole.enter_context(nc.semaphore("waited"))
        with ExitStack() as early:
            tri = early.enter_context(nc.sbuf_tensor("tri", [P, P], F32))
            fl_raw = early.enter_context(nc.sbuf_tensor("fl_raw", [P, NT * H], F32))
            make_constants(nc, ident, tri)
            attention_projection(nc, ident, waited, fl_raw, x_prompt, x_sample, norm_g, w_in, q_norm_g, k_norm_g,
                                 new_k, new_v, new_k_s, new_v_s, q_all, gate_all, xt_hi_all, xt_lo_all)
            forget_sums(nc, ident, tri, fl_raw, f_t_all, b_f, cache_logf, new_logf, new_logf_s, f_all)
        pool_conv(nc, ident, w_in, norm_g, xt_hi_all, xt_lo_all, pool_w, pool_scale, conv_w, state_pool, state_conv,
                  new_pool, new_conv, new_pool_s, new_conv_s, mix_all)
        prompt_attention(nc, ident, waited, q_all, new_k, new_v, gate_all, f_all, att_all)
        sample_attention(nc, ident, waited, q_all, cache_k, cache_v, new_k_s, new_v_s, gate_all, f_t_all, att_all)
        output_projection(nc, ident, w_out, x_prompt, x_sample, att_all, mix_all, y_prompt, y_sample)


_INS = [("x_prompt", (SEQ, D)), ("x_sample", (NB * NQ, D)), ("cache_k", (NB * PAST, DA)),
        ("cache_v", (NB * PAST, DA)), ("cache_logf", (NB, PAST, H)), ("state_pool", (NB * HIST, DP)),
        ("state_conv", (NB * (CONV_W - 1), DC)), ("norm_g", (D,)), ("w_in", (D, C0 + 4 * DC)), ("b_f", (H,)),
        ("q_norm_g", (HD,)), ("k_norm_g", (HD,)), ("pool_w", (4, 64, 64)), ("pool_scale", (DP,)),
        ("conv_w", (CONV_W, DC)), ("w_out", (D, D))]
_OUTS = [((SEQ, D), (1, SEQ, D)), ((NB * NQ, D), (NB, NQ, D)),
         ((SEQ, DA), (1, 1, SEQ, H, HD)), ((SEQ, DA), (1, 1, SEQ, H, HD)), ((SEQ, H), (1, 1, SEQ, H)),
         ((HIST, DP), (1, 1, HIST, DP)), ((CONV_W - 1, DC), (1, 1, CONV_W - 1, DC)),
         ((NB * NQ, DA), (1, NB, NQ, H, HD)), ((NB * NQ, DA), (1, NB, NQ, H, HD)), ((NB * NQ, H), (1, NB, NQ, H)),
         ((NB * HIST, DP), (1, NB, HIST, DP)), ((NB * (CONV_W - 1), DC), (1, NB, CONV_W - 1, DC))]


def kernel(**inputs):
    import numpy as _np
    import concourse.bacc as _bacc
    from concourse.bass_utils import run_bass_kernel_spmd as _run

    nc = _bacc.Bacc("TRN2", target_bir_lowering=False, num_devices=1)
    arrays, args = {}, []
    for name, shape in _INS:
        arrays[f"in_{name}_dram"] = _np.ascontiguousarray(inputs[name]).reshape(shape)
        args.append(nc.dram_tensor(f"in_{name}_dram", shape, F32, kind="ExternalInput").ap())
    for i, (shape, _) in enumerate(_OUTS):
        args.append(nc.dram_tensor(f"out_{i}_dram", shape, F32, kind="ExternalOutput").ap())
    encoder_layer(nc, *args)
    r = _run(nc, [arrays], core_ids=[0])
    return tuple(_np.asarray(r.results[0][f"out_{i}_dram"]).reshape(shape) for i, (_, shape) in enumerate(_OUTS))
```
